# Optimizing a Trainium2 kernel written in Bass

```python
import math
import jax, jax.numpy as jnp
from jax import lax
import numpy as np

D_MODEL = 1024
BATCH = 1
SEQ = 2048
DEPTH = 1
DEC_BATCH = 1
DEC_SEQ = 512
PAST_LEN = 128

GRID_W = 64
ATT_HEADS = 8
ATT_HEAD_DIM = 64
D_ATT = ATT_HEADS * ATT_HEAD_DIM
WIN_ROWS = 8
WIN_COLS = 16
SSM_HEADS = 8
SSM_HEAD_DIM = 64
D_SSM = SSM_HEADS * SSM_HEAD_DIM
SSM_GROUPS = 2
D_STATE = 128
D_CONV = 5
CHUNK = 128
D_MIX = D_ATT + D_SSM
CONV_CH = D_SSM + 2 * SSM_GROUPS * D_STATE
D_IN_PROJ = 3 * D_ATT + D_SSM + CONV_CH + 2 * SSM_HEADS
D_FF = ((8 * D_MODEL + 3 * 256 - 1) // (3 * 256)) * 256
EPS = 1e-6

kernel_name = 'hymba_natten_ssd_encoder'

def rmsnorm(x, w):
    xf = x.astype(jnp.float32)
    y = xf * lax.rsqrt(jnp.mean(xf * xf, axis=-1, keepdims=True) + EPS)
    return (y * w.astype(jnp.float32)).astype(x.dtype)

def neighbourhood_attention(q, k, v, rpb):
    bsz, T, H, hd = q.shape
    rows = T // GRID_W
    wr = min(WIN_ROWS, rows)
    qg = q.reshape(bsz, rows, GRID_W, H, hd)
    kg = k.reshape(bsz, rows, GRID_W, H, hd)
    vg = v.reshape(bsz, rows, GRID_W, H, hd)
    cols = np.arange(GRID_W)
    c0 = np.clip(cols - WIN_COLS // 2, 0, GRID_W - WIN_COLS)
    col_idx = c0[:, None] + np.arange(WIN_COLS)[None, :]
    dc_idx = col_idx - cols[:, None] + (WIN_COLS - 1)
    rpb_c = rpb[:, :, dc_idx]

    def row_block(r):
        r0 = jnp.clip(r - WIN_ROWS // 2, 0, rows - wr)
        k_rows = lax.dynamic_slice_in_dim(kg, r0, wr, axis=1)
        v_rows = lax.dynamic_slice_in_dim(vg, r0, wr, axis=1)
        k_win = k_rows[:, :, col_idx]
        v_win = v_rows[:, :, col_idx]
        q_r = lax.dynamic_index_in_dim(qg, r, axis=1, keepdims=False)
        s = jnp.einsum('bqhd,brqchd->bhqrc', q_r, k_win).astype(jnp.float32)
        dr_idx = r0 - r + jnp.arange(wr) + (WIN_ROWS - 1)
        bias = jnp.take(rpb_c, dr_idx, axis=1).astype(jnp.float32)
        s = s + bias.transpose(0, 2, 1, 3)[None]
        p = jax.nn.softmax(s.reshape(bsz, H, GRID_W, wr * WIN_COLS), axis=-1)
        p = p.reshape(bsz, H, GRID_W, wr, WIN_COLS).astype(v.dtype)
        return jnp.einsum('bhqrc,brqchd->bqhd', p, v_win)

    out = lax.map(row_block, jnp.arange(rows))
    return out.transpose(1, 0, 2, 3, 4).reshape(bsz, T, H * hd)

def depthwise_conv(x, w, b):
    y = lax.conv_general_dilated(
        x, w[:, None, :], window_strides=(1,),
        padding=[(D_CONV // 2, D_CONV // 2)],
        dimension_numbers=('NWC', 'WIO', 'NWC'),
        feature_group_count=x.shape[-1])
    return y + b

def ssd_scan(x, dt, A, Bh, Ch):
    bsz, T, H, P = x.shape
    N = Bh.shape[-1]
    nc = T // CHUNK
    xdt = (x.astype(jnp.float32) * dt[..., None]).reshape(bsz, nc, CHUNK, H, P)
    Bc = Bh.astype(jnp.float32).reshape(bsz, nc, CHUNK, H, N)
    Cc = Ch.astype(jnp.float32).reshape(bsz, nc, CHUNK, H, N)
    a = (dt * A).reshape(bsz, nc, CHUNK, H).transpose(0, 3, 1, 2)
    a_cs = jnp.cumsum(a, axis=-1)
    tril = np.tril(np.ones((CHUNK, CHUNK), dtype=bool))
    seg = a_cs[..., :, None] - a_cs[..., None, :]
    Lmat = jnp.exp(jnp.where(tril, seg, -jnp.inf))
    cb = jnp.einsum('bclhn,bcshn->bhcls', Cc, Bc)
    y_diag = jnp.einsum('bhcls,bcshp->bclhp', cb * Lmat, xdt)
    decay_states = jnp.exp(a_cs[..., -1:] - a_cs)
    states = jnp.einsum('bclhn,bhcl,bclhp->bchpn', Bc, decay_states, xdt)
    chunk_decay = jnp.exp(a_cs[..., -1])

    def step(h, inp):
        s_c, d_c = inp
        return h * d_c[..., None, None] + s_c, h

    h0 = jnp.zeros((bsz, H, P, N), jnp.float32)
    _, prev = lax.scan(step, h0, (states.transpose(1, 0, 2, 3, 4), chunk_decay.transpose(2, 0, 1)))
    prev = prev.transpose(1, 0, 2, 3, 4)
    y_off = jnp.einsum('bclhn,bchpn,bhcl->bclhp', Cc, prev, jnp.exp(a_cs))
    return (y_diag + y_off).reshape(bsz, T, H, P)

def ssd_mixer(z, xBC, dt_f_raw, dt_b_raw, conv_w, conv_b, dt_bias_f, dt_bias_b,
              A_log_f, A_log_b, D_skip, ssm_norm_w):
    bsz, T, _ = z.shape
    xBC = jax.nn.silu(depthwise_conv(xBC, conv_w, conv_b))
    xs, Bm, Cm = jnp.split(xBC, [D_SSM, D_SSM + SSM_GROUPS * D_STATE], axis=-1)
    xs = xs.reshape(bsz, T, SSM_HEADS, SSM_HEAD_DIM)
    rep = SSM_HEADS // SSM_GROUPS
    Bh = jnp.repeat(Bm.reshape(bsz, T, SSM_GROUPS, D_STATE), rep, axis=2)
    Ch = jnp.repeat(Cm.reshape(bsz, T, SSM_GROUPS, D_STATE), rep, axis=2)
    dt_f = jax.nn.softplus(dt_f_raw.astype(jnp.float32) + dt_bias_f.astype(jnp.float32))
    dt_b = jax.nn.softplus(dt_b_raw.astype(jnp.float32) + dt_bias_b.astype(jnp.float32))
    A_f = -jnp.exp(A_log_f.astype(jnp.float32))
    A_b = -jnp.exp(A_log_b.astype(jnp.float32))
    y_f = ssd_scan(xs, dt_f, A_f, Bh, Ch)
    y_b = jnp.flip(ssd_scan(jnp.flip(xs, 1), jnp.flip(dt_b, 1), A_b,
                            jnp.flip(Bh, 1), jnp.flip(Ch, 1)), 1)
    y = y_f + y_b + D_skip.astype(jnp.float32)[:, None] * xs.astype(jnp.float32)
    g = y.reshape(bsz, T, D_SSM) * jax.nn.silu(z.astype(jnp.float32))
    g = g.reshape(bsz, T, SSM_GROUPS, D_SSM // SSM_GROUPS)
    g = g * lax.rsqrt(jnp.mean(g * g, axis=-1, keepdims=True) + EPS)
    g = g.reshape(bsz, T, D_SSM) * ssm_norm_w.astype(jnp.float32)
    return g.astype(z.dtype)

def hybrid_layer(x, norm1_w, w_in, q_norm_w, k_norm_w, rpb, conv_w, conv_b,
                 dt_bias_f, dt_bias_b, A_log_f, A_log_b, D_skip, ssm_norm_w,
                 w_out, norm2_w, w_gate, w_up, w_down):
    bsz, T, _ = x.shape
    h = rmsnorm(x, norm1_w)
    proj = h @ w_in
    splits = [D_ATT, 2 * D_ATT, 3 * D_ATT, 3 * D_ATT + D_SSM,
              3 * D_ATT + D_SSM + CONV_CH, 3 * D_ATT + D_SSM + CONV_CH + SSM_HEADS]
    q, k, v, z, xBC, dt_f, dt_b = jnp.split(proj, splits, axis=-1)
    q = rmsnorm(q.reshape(bsz, T, ATT_HEADS, ATT_HEAD_DIM), q_norm_w) * (ATT_HEAD_DIM ** -0.5)
    k = rmsnorm(k.reshape(bsz, T, ATT_HEADS, ATT_HEAD_DIM), k_norm_w)
    v = v.reshape(bsz, T, ATT_HEADS, ATT_HEAD_DIM)
    att = neighbourhood_attention(q, k, v, rpb)
    ssm = ssd_mixer(z, xBC, dt_f, dt_b, conv_w, conv_b, dt_bias_f, dt_bias_b,
                    A_log_f, A_log_b, D_skip, ssm_norm_w)
    x = x + jnp.concatenate([att, ssm], axis=-1) @ w_out
    h2 = rmsnorm(x, norm2_w)
    return x + (jax.nn.silu(h2 @ w_gate) * (h2 @ w_up)) @ w_down

def trunk(x, norm1_w, w_in, q_norm_w, k_norm_w, rpb, conv_w, conv_b,
          dt_bias_f, dt_bias_b, A_log_f, A_log_b, D_skip, ssm_norm_w,
          w_out, norm2_w, w_gate, w_up, w_down):
    for l in range(DEPTH):
        x = hybrid_layer(x, norm1_w[l], w_in[l], q_norm_w[l], k_norm_w[l], rpb[l],
                         conv_w[l], conv_b[l], dt_bias_f[l], dt_bias_b[l],
                         A_log_f[l], A_log_b[l], D_skip[l], ssm_norm_w[l],
                         w_out[l], norm2_w[l], w_gate[l], w_up[l], w_down[l])
    return x

def setup_inputs(seed: int = 0) -> dict:
    key = jax.random.key(seed)
    ks = jax.random.split(key, 24)
    f32 = jnp.float32
    L = DEPTH

    def nrm(k, shape, scale):
        return jax.random.normal(k, shape, f32) * scale

    def gain(k, shape):
        return 1.0 + 0.05 * jax.random.normal(k, shape, f32)

    def dt_bias(k):
        u = jax.random.uniform(k, (L, SSM_HEADS), f32)
        dt = jnp.exp(u * (math.log(0.1) - math.log(0.001)) + math.log(0.001))
        return dt + jnp.log(-jnp.expm1(-dt))

    return {
        'x_prompt': jax.random.normal(ks[0], (BATCH, SEQ, D_MODEL), f32),
        'x_sample': jax.random.normal(ks[1], (DEC_BATCH, DEC_SEQ, D_MODEL), f32),
        'norm1_w': gain(ks[2], (L, D_MODEL)),
        'w_in': nrm(ks[3], (L, D_MODEL, D_IN_PROJ), D_MODEL ** -0.5),
        'q_norm_w': gain(ks[4], (L, ATT_HEAD_DIM)),
        'k_norm_w': gain(ks[5], (L, ATT_HEAD_DIM)),
        'rpb': nrm(ks[6], (L, ATT_HEADS, 2 * WIN_ROWS - 1, 2 * WIN_COLS - 1), 0.1),
        'conv_w': nrm(ks[7], (L, D_CONV, CONV_CH), D_CONV ** -0.5),
        'conv_b': nrm(ks[8], (L, CONV_CH), 0.01),
        'dt_bias_f': dt_bias(ks[9]),
        'dt_bias_b': dt_bias(ks[10]),
        'A_log_f': jnp.log(jax.random.uniform(ks[11], (L, SSM_HEADS), f32, 1.0, 16.0)),
        'A_log_b': jnp.log(jax.random.uniform(ks[12], (L, SSM_HEADS), f32, 1.0, 16.0)),
        'D_skip': gain(ks[13], (L, SSM_HEADS)),
        'ssm_norm_w': gain(ks[14], (L, D_SSM)),
        'w_out': nrm(ks[15], (L, D_MIX, D_MODEL), D_MIX ** -0.5),
        'norm2_w': gain(ks[16], (L, D_MODEL)),
        'w_gate': nrm(ks[17], (L, D_MODEL, D_FF), D_MODEL ** -0.5),
        'w_up': nrm(ks[18], (L, D_MODEL, D_FF), D_MODEL ** -0.5),
        'w_down': nrm(ks[19], (L, D_FF, D_MODEL), D_FF ** -0.5),
    }

def reference(x_prompt, x_sample, norm1_w, w_in, q_norm_w, k_norm_w, rpb, conv_w, conv_b,
              dt_bias_f, dt_bias_b, A_log_f, A_log_b, D_skip, ssm_norm_w,
              w_out, norm2_w, w_gate, w_up, w_down):
    y_prompt = trunk(x_prompt, norm1_w, w_in, q_norm_w, k_norm_w, rpb, conv_w, conv_b,
                     dt_bias_f, dt_bias_b, A_log_f, A_log_b, D_skip, ssm_norm_w,
                     w_out, norm2_w, w_gate, w_up, w_down)
    y_sample = trunk(x_sample, norm1_w, w_in, q_norm_w, k_norm_w, rpb, conv_w, conv_b,
                     dt_bias_f, dt_bias_b, A_log_f, A_log_b, D_skip, ssm_norm_w,
                     w_out, norm2_w, w_gate, w_up, w_down)
    return (y_prompt, y_sample)


_drawn_inputs = setup_inputs


def setup_inputs(seed=0):
    import zlib

    import numpy as np

    out = dict(_drawn_inputs(seed))
    spreads = {}
    factors = {'q_norm_w': 8.0, 'k_norm_w': 8.0, 'rpb': 6.425, 'conv_b': 6.035, 'D_skip': 6.128}
    for name, (base, spread) in spreads.items():
        noise = np.random.default_rng([zlib.crc32(name.encode()), seed]).standard_normal(out[name].shape)
        drawn = base * np.exp(spread * noise) if base else spread * noise
        out[name] = __import__('jax').numpy.asarray(drawn.astype(out[name].dtype))
    for name, factor in factors.items():
        out[name] = (out[name] * factor).astype(out[name].dtype)
    return out
```

```python
from contextlib import ExitStack, contextmanager

import concourse.bass as bass
from concourse import mybir

ALU = mybir.AluOpType
ACT = mybir.ActivationFunctionType
AX_X = mybir.AxisListType.X
F32 = mybir.dt.float32
F32R = mybir.dt.float32r
BF16 = mybir.dt.bfloat16

P = 128
D_MODEL = 1024
D_FF = 2816
TB = 512
SEQ, DEC_SEQ = 2048, 512
T = SEQ + DEC_SEQ
NTB = T // TB
KD = D_MODEL // P
KF = D_FF // P
TT = TB // P
HEADS = 8
HEAD = 64
D_ATT = HEADS * HEAD
D_SSM = HEADS * HEAD
GROUPS = 2
D_STATE = 128
D_CONV = 5
CONV_CH = D_SSM + 2 * GROUPS * D_STATE
D_IN_PROJ = 3 * D_ATT + D_SSM + CONV_CH + 2 * HEADS
EPS = 1e-6
GRID_W = 64
WIN_ROWS, WIN_COLS = 8, 16
PR, PC = 4 + 2 * WIN_ROWS - 1 + 4, 16 + 2 * WIN_COLS - 1 + 16
PITCH = HEADS * PR * PC + PC
BIAS_SKEW = 15
LOWEST = -3.0e38


@contextmanager
def phase_semaphores(nc, prefix):
    held = []

    def sem(name):
        held.append(nc.alloc_semaphore(prefix + name))
        return held[-1]

    yield sem
    nc.clear_and_free_semaphores(held)
    nc.all_engine_barrier()


def split_products(pe, out, w_hi, w_lo, x_hi, x_lo, first, last):
    pe.matmul(out, w_hi, x_hi, start=first, stop=False)
    pe.matmul(out, w_hi, x_lo, start=False, stop=False)
    return pe.matmul(out, w_lo, x_hi, start=False, stop=last)


def in_proj_phase(nc, x, w_in, cols, qk_w, ident_dram, q_s, k_s, v_s, z_s, dtT, xbcT, xcT):
    SLOTS = 12
    USES = 6
    USE = {4: 2, 6: 3, 8: 4, 10: 5}
    COL = {4: 3 * D_ATT, 6: 2 * D_ATT, 8: 0, 10: D_ATT}
    XBC0 = 3 * D_ATT + D_SSM
    LAST = D_IN_PROJ - P
    KH = KD // 2
    KX = CONV_CH // P
    HALO = D_CONV // 2

    with ExitStack() as ctx:
        def sb(name, shape, dt=F32):
            return ctx.enter_context(nc.sbuf_tensor("i_" + name, shape, dt))

        sem = ctx.enter_context(phase_semaphores(nc, "i_"))

        def some(name, n):
            return [sem(f"{name}{i}") for i in range(n)]

        ident = sb("ident", [P, P])
        par_cols = sb("cols", [P, KD, 8])
        qk_rows = sb("qk_rows", [P, 2, HEAD])
        q_gain = sb("q_gain", [P, HEAD])
        eps = sb("eps", [P, 1])
        raw = sb("raw", [P, 2, 2 * KD * P])
        w_hi = sb("w_hi", [P, 2, 2 * KD * P], F32R)
        w_lo = sb("w_lo", [P, 2, 2 * KD * P], F32R)
        dt_raw = sb("dt_raw", [P, KD, P])
        dt_hi = sb("dt_hi", [P, KD, P], F32R)
        dt_lo = sb("dt_lo", [P, KD, P], F32R)
        x_t = sb("x_t", [P, TT, D_MODEL])
        junk = sb("junk", [P, D_MODEL])
        x_ss = sb("x_ss", [P, TT])
        x_ln = sb("x_ln", [P, TT])
        x_rstd = sb("x_rstd", [P, TT])
        h_f = sb("h_f", [P, KD, TB])
        h_hi = sb("h_hi", [P, KD, TB], F32R)
        h_lo = sb("h_lo", [P, KD, TB], F32R)
        ev = sb("ev", [P, TT, TB])
        dt_ev = sb("dt_ev", [P, TB])
        sq = sb("sq", [P, TT, TB])
        ss = sb("ss", [P, TT, HEADS])
        ss_ln = sb("ss_ln", [P, TT, HEADS])
        rstd = sb("rstd", [P, TT, HEADS])
        cx = sb("cx", [P, 2, TB + 2 * HALO])
        cy = sb("cy", [P, 2, TB])
        co = sb("co", [P, 2, TB])

        acc = ctx.enter_context(nc.psum_tensor("i_acc", [P, TT, TB], F32))
        ps_turn = ctx.enter_context(nc.psum_tensor("i_ps_turn", [P, KD, P], F32))
        ps_dt = ctx.enter_context(nc.psum_tensor("i_ps_dt", [P, TB], F32))

        zero = sb("zero", [P, CONV_CH // P, 2 * HALO])

        const_loaded = sem("const_loaded")
        zero_made = sem("zero_made")
        halo_stored = sem("halo_stored")
        xbc_seen = sem("xbc_seen")
        consts_made = sem("consts_made")
        dt_hi_done = sem("dt_hi_done")
        dt_lo_done = sem("dt_lo_done")
        slot_loaded = some("slot_loaded", 2)
        slot_hi_done = some("slot_hi_done", 2)
        slot_lo_done = some("slot_lo_done", 2)
        half_done = sem("half_done")
        acc_ready = some("acc_ready", TT)
        ev_ready = some("ev_ready", TT)
        ev_stored = some("ev_stored", TT)
        dt_ready = sem("dt_ready")
        dt_ev_ready = sem("dt_ev_ready")
        dt_stored = sem("dt_stored")
        sq_done = some("sq_done", TT)
        ss_done = some("ss_done", TT)
        ln_done = some("ln_done", TT)
        rstd_done = some("rstd_done", TT)
        q_scaled = some("q_scaled", TT)
        x_loaded = sem("x_loaded")
        x_sq_done = sem("x_sq_done")
        x_ln_done = sem("x_ln_done")
        x_rstd_done = sem("x_rstd_done")
        xn_done = sem("xn_done")
        h_turned = sem("h_turned")
        h_f_done = sem("h_f_done")
        h_hi_done = sem("h_hi_done")
        h_lo_done = sem("h_lo_done")
        cx_loaded = some("cx_loaded", 2)
        tap0_done = some("tap0_done", 2)
        taps_done = some("taps_done", 2)
        tap_step = sem("tap_step")
        co_ready = some("co_ready", 2)
        co_stored = some("co_stored", 2)

        def wait_slot_used(eng, tb, s):
            if s % 2 == 0 and s not in (2, 4):
                eng.wait_ge(half_done, tb * 4 + (s - 4) // 2 if s >= 6 else tb * 4)
            elif s in (2, 4):
                eng.wait_ge(acc_ready[1], tb * USES + s // 2)
            else:
                eng.wait_ge(acc_ready[3], tb * USES + s // 2)

        def blocks(eng, body):
            body(0, True, False)
            with eng.Fori(1, NTB - 1) as tb:
                body(tb, True, True)
            body(NTB - 1, False, True)

        def xbc_col(tb):
            return tb * TB + HALO + (2 * HALO if isinstance(tb, int) and tb == NTB - 1 else 0)

        block = ctx.enter_context(nc.Block())

        @block.sync
        def _(sp):
            w_src = w_in.rearrange("(k p) c -> p k c", p=P)
            x_src = x.rearrange("(t p) d -> p t d", p=P)
            sp.dma_start(ident[:], ident_dram).then_inc(const_loaded, 16)
            sp.dma_start(par_cols[:], cols).then_inc(const_loaded, 16)
            sp.dma_start(qk_rows[:], qk_w).then_inc(const_loaded, 16)

            def load_x(tb):
                sp.wait_ge(h_turned, TT * tb)
                sp.dma_start(x_t[:], x_src[:, bass.ds(tb * TT, TT), :]).then_inc(x_loaded, 16)

            def load_slot(tb, s):
                par, n = s % 2, tb * (SLOTS // 2) + s // 2
                sp.wait_ge(slot_lo_done[par], n)
                s = s % SLOTS
                if s < 4:
                    dst = raw[:, par].rearrange("p (k c) -> p k c", k=KD)
                    src = w_src[:, :, XBC0 + 2 * P * s:XBC0 + 2 * P * (s + 1)]
                else:
                    c0, k0 = COL[s - s % 2], KH * (s % 2)
                    dst = raw[:, par].rearrange("p (k c) -> p k c", k=KH)
                    src = w_src[:, k0:k0 + KH, c0:c0 + TB]
                sp.dma_start(dst, src).then_inc(slot_loaded[par], 16)

            def load_conv(tb, j):
                n = tb * (KX // 2) + j // 2
                sp.wait_ge(taps_done[j % 2], n)
                if j == 0:
                    sp.sem_inc(xbc_seen, 1)
                    if not isinstance(tb, int) or tb < NTB - 1:
                        for u in range(TT):
                            sp.wait_ge(ev_stored[u], 16 * ((tb + 1) * USES + 2))
                    sp.wait_ge(halo_stored, 16 * 3)
                    sp.sem_inc(xbc_seen, 1)
                sp.dma_start(cx[:, j % 2], xbcT[j * P:(j + 1) * P, bass.ds(xbc_col(tb) - HALO, TB + 2 * HALO)]) \
                  .then_inc(cx_loaded[j % 2], 16)

            load_x(0)
            sp.dma_start(dt_raw[:], w_src[:, :, LAST:LAST + P]).then_inc(const_loaded, 16)
            load_slot(0, 0)
            load_slot(0, 1)

            def store_rows(tb, s, dst):
                for u in range(TT):
                    sp.wait_ge(ev_ready[u], tb * USES + USE[s - 1] + 1)
                    sp.dma_start(dst[bass.ds(tb * TB + u * P, P), :], ev[:, u]).then_inc(ev_stored[u], 16)

            def store_conv(tb, j):
                par, n = j % 2, tb * (KX // 2) + j // 2
                sp.wait_ge(co_ready[par], n + 1)
                sp.dma_start(xcT[j * P:(j + 1) * P, bass.ds(tb * TB, TB)], co[:, par]).then_inc(co_stored[par], 16)

            def store(tb, s, conv):
                if s < 4:
                    for ft in (2 * s, 2 * s + 1):
                        u, w = ft % 4, tb * USES + ft // 4
                        sp.wait_ge(ev_ready[u], w + 1)
                        sp.dma_start(xbcT[ft * P:(ft + 1) * P, bass.ds(xbc_col(tb), TB)], ev[:, u]) \
                          .then_inc(ev_stored[u], 16)
                if s == 3:
                    sp.wait_ge(const_loaded, 16 * 4)
                    sp.wait_ge(dt_ev_ready, tb + 1)
                    sp.dma_start(dtT[:, bass.ds(tb * TB, TB)], dt_ev[P - 2 * HEADS:P]).then_inc(dt_stored, 16)
                if s % 2 and s > 4:
                    store_rows(tb, s, {5: z_s, 7: v_s, 9: q_s, 11: k_s}[s])
                if conv and 4 <= s < 8:
                    store_conv(tb - 1, 2 * (s - 4))
                    store_conv(tb - 1, 2 * (s - 4) + 1)

            def token_block(tb, more, conv):
                for s in range(SLOTS):
                    if s + 2 < SLOTS or more:
                        load_slot(tb, s + 2)
                    if s > 0:
                        store(tb, s - 1, conv)
                    elif conv:
                        store(tb - 1, SLOTS - 1, True)
                    if s == 2 and more:
                        load_x(tb + 1)
                    if conv and 4 <= s < 8:
                        load_conv(tb - 1, 2 * (s - 4))
                        load_conv(tb - 1, 2 * (s - 4) + 1)

            blocks(sp, token_block)
            store(NTB - 1, SLOTS - 1, True)
            for j in range(KX):
                load_conv(NTB - 1, j)
                if j >= 2:
                    store_conv(NTB - 1, j - 2)
            store_conv(NTB - 1, KX - 2)
            store_conv(NTB - 1, KX - 1)
            for u in range(TT):
                sp.wait_ge(ev_stored[u], 16 * NTB * USES)
            sp.wait_ge(dt_stored, 16 * NTB)
            for par in range(2):
                sp.wait_ge(co_stored[par], 16 * NTB * KX // 2)

        @block.scalar
        def _(act):
            def split_slot(tb, s):
                par, n = s % 2, tb * (SLOTS // 2) + s // 2
                act.wait_ge(slot_loaded[par], 16 * (n + 1))
                if s >= SLOTS:
                    wait_slot_used(act, tb + 1, s - SLOTS)
                else:
                    wait_slot_used(act, tb, s)
                act.copy(w_hi[:, par], raw[:, par]).then_inc(slot_hi_done[par], 1)

            def make_rstd(tb):
                act.wait_ge(x_loaded, 16 * (tb + 1))
                for u in range(TT):
                    act.wait_ge(x_sq_done, TT * tb + u)
                    act.activation(junk[:], x_t[:, u], ACT.Square, accum_out=x_ss[:, u:u + 1]).then_inc(x_sq_done, 1)
                act.wait_ge(x_sq_done, TT * (tb + 1))
                act.activation(x_ln[:], x_ss[:], ACT.Ln, scale=1.0 / D_MODEL, bias=eps[:]).then_inc(x_ln_done, 1)
                act.wait_ge(x_ln_done, tb + 1)
                act.wait_ge(xn_done, TT * tb)
                act.activation(x_rstd[:], x_ln[:], ACT.Exp, scale=-0.5).then_inc(x_rstd_done, 1)

            def h_high(tb, u):
                tok = slice(u * P, (u + 1) * P)
                act.wait_ge(h_f_done, TT * tb + u + 1)
                act.copy(h_hi[:, :, tok], h_f[:, :, tok]).then_inc(h_hi_done, 1)

            def tap0(tb, j):
                par, n = j % 2, tb * (KX // 2) + j // 2
                act.wait_ge(cx_loaded[par], 16 * (n + 1))
                act.wait_ge(co_ready[par], n)
                act.activation(cy[:, par], cx[:, par, 0:TB], ACT.Identity, scale=par_cols[:, j, 2:3],
                               bias=par_cols[:, j, 1:2]).then_inc(tap0_done[par], 1)

            def conv_silu(tb, j):
                par, n = j % 2, tb * (KX // 2) + j // 2
                act.wait_ge(taps_done[par], n + 1)
                act.wait_ge(co_stored[par], 16 * n)
                act.activation(co[:, par], cy[:, par], ACT.Silu).then_inc(co_ready[par], 1)

            def squares(tb, s, u):
                w = tb * USES + USE[s - 1]
                m = tb * 2 + (s - 9) // 2
                act.wait_ge(acc_ready[u], w + 1)
                act.wait_ge(ss_done[u], m)
                act.activation(sq[:, u], acc[:, u], ACT.Square).then_inc(sq_done[u], 1)

            def head_rstd(tb, s, u):
                m = tb * 2 + (s - 9) // 2
                act.wait_ge(ss_done[u], m + 1)
                act.activation(ss_ln[:, u], ss[:, u], ACT.Ln, scale=1.0 / HEAD, bias=eps[:]).then_inc(ln_done[u], 1)
                act.wait_ge(ln_done[u], m + 1)
                act.activation(rstd[:, u], ss_ln[:, u], ACT.Exp, scale=-0.5).then_inc(rstd_done[u], 1)

            def token_block(tb, more, conv):
                for s in range(SLOTS):
                    if s + 1 < SLOTS or more:
                        split_slot(tb, s + 1)
                    if s < 4:
                        for ft in (2 * s, 2 * s + 1):
                            u, w = ft % 4, tb * USES + ft // 4
                            act.wait_ge(acc_ready[u], w + 1)
                            act.wait_ge(ev_stored[u], 16 * w)
                            act.copy(ev[:, u], acc[:, u]).then_inc(ev_ready[u], 1)
                    if s == 3:
                        act.wait_ge(dt_ready, tb + 1)
                        act.wait_ge(dt_stored, 16 * tb)
                        act.copy(dt_ev[96:P], ps_dt[96:P]).then_inc(dt_ev_ready, 1)
                    if conv and 4 <= s < 8:
                        for j in (2 * (s - 4), 2 * (s - 4) + 1):
                            tap0(tb - 1, j)
                    if s == 5:
                        for u in range(TT):
                            w = tb * USES + USE[4]
                            act.wait_ge(acc_ready[u], w + 1)
                            act.wait_ge(ev_stored[u], 16 * w)
                            act.activation(ev[:, u], acc[:, u], ACT.Silu).then_inc(ev_ready[u], 1)
                    if conv and 4 <= s < 8:
                        for j in (2 * (s - 4), 2 * (s - 4) + 1):
                            conv_silu(tb - 1, j)
                    if s == 8 and more:
                        make_rstd(tb + 1)
                    if s == 9 or s == 11:
                        squares(tb, s, 0)
                        for u in range(TT):
                            if u + 1 < TT:
                                squares(tb, s, u + 1)
                            if s == 11 and more:
                                h_high(tb + 1, u)
                            head_rstd(tb, s, u)

            act.wait_ge(const_loaded, 16 * 4)
            act.copy(dt_hi[:], dt_raw[:]).then_inc(dt_hi_done, 1)
            act.wait_ge(consts_made, 2)
            make_rstd(0)
            split_slot(0, 0)
            for u in range(TT):
                h_high(0, u)
            blocks(act, token_block)
            for j in range(0, KX, 2):
                tap0(NTB - 1, j)
                tap0(NTB - 1, j + 1)
                conv_silu(NTB - 1, j)
                conv_silu(NTB - 1, j + 1)

        @block.vector
        def _(dve):
            def split_slot(tb, s):
                par, n = s % 2, tb * (SLOTS // 2) + s // 2
                dve.wait_ge(slot_hi_done[par], n + 1)
                dve.tensor_tensor(w_lo[:, par], raw[:, par], w_hi[:, par].bitcast(F32), ALU.subtract) \
                   .then_inc(slot_lo_done[par], 1)

            def scale_x(tb, u):
                if u == 0:
                    dve.wait_ge(x_rstd_done, tb + 1)
                dve.tensor_scalar(x_t[:, u], x_t[:, u], x_rstd[:, u:u + 1], None, ALU.mult).then_inc(xn_done, 1)

            def gain_h(tb, u):
                dve.wait_ge(h_turned, TT * tb + u + 1)
                dve.wait_ge(h_lo_done, TT * tb)
                dve.tensor_tensor(h_f[:, :, u * P:(u + 1) * P], ps_turn[:],
                                  par_cols[:, :, 0:1].broadcast_to([P, KD, P]), ALU.mult).then_inc(h_f_done, 1)

            def taps(tb, j):
                par, n = j % 2, tb * (KX // 2) + j // 2
                dve.wait_ge(tap0_done[par], n + 1)
                for t in range(1, D_CONV):
                    if t > 1:
                        dve.wait_ge(tap_step, (tb * KX + j) * (D_CONV - 2) + t - 1)
                    dve.scalar_tensor_tensor(cy[:, par], cx[:, par, t:t + TB], par_cols[:, j, 2 + t:3 + t], cy[:, par],
                                             ALU.mult, ALU.add).then_inc(taps_done[par] if t == D_CONV - 1 else tap_step, 1)

            def head_sums(tb, s, u):
                m = tb * 2 + (s - 9) // 2
                dve.wait_ge(sq_done[u], m + 1)
                dve.wait_ge(ln_done[u], m)
                dve.tensor_reduce(ss[:, u], sq[:, u].rearrange("p (h d) -> p h d", h=HEADS), AX_X, ALU.add) \
                   .then_inc(ss_done[u], 1)

            def head_scale(tb, s, u):
                w = tb * USES + USE[s - 1]
                m = tb * 2 + (s - 9) // 2
                dve.wait_ge(rstd_done[u], m + 1)
                dve.wait_ge(ev_stored[u], 16 * w)
                done = q_scaled[u] if s == 9 else ev_ready[u]
                dve.tensor_tensor(ev[:, u].rearrange("p (h d) -> p h d", h=HEADS),
                                  acc[:, u].rearrange("p (h d) -> p h d", h=HEADS),
                                  rstd[:, u].unsqueeze(2).broadcast_to([P, HEADS, HEAD]), ALU.mult) \
                   .then_inc(done, 1)

            def token_block(tb, more, conv):
                for s in range(SLOTS):
                    if s + 1 < SLOTS or more:
                        split_slot(tb, s + 1)
                    if conv and 4 <= s < 8:
                        for j in (2 * (s - 4), 2 * (s - 4) + 1):
                            taps(tb - 1, j)
                    if s == 7:
                        for u in range(TT):
                            w = tb * USES + USE[6]
                            dve.wait_ge(acc_ready[u], w + 1)
                            dve.wait_ge(ev_stored[u], 16 * w)
                            dve.tensor_copy(ev[:, u], acc[:, u]).then_inc(ev_ready[u], 1)
                    if s == 8 and more:
                        for u in range(TT):
                            scale_x(tb + 1, u)
                    if s in (9, 10, 11) and more:
                        gain_h(tb + 1, s - 9)
                    if s in (9, 11):
                        head_sums(tb, s, 0)
                        for u in range(TT):
                            if u + 1 < TT:
                                head_sums(tb, s, u + 1)
                            head_scale(tb, s, u)
                            if u == 1 and s == 11 and more:
                                gain_h(tb + 1, 3)

            dve.memset(eps[:], EPS).then_inc(consts_made, 1)
            dve.wait_ge(const_loaded, 16 * 4)
            dve.scalar_tensor_tensor(q_gain[:], qk_rows[:, 0], HEAD ** -0.5, qk_rows[:, 1], ALU.mult, ALU.mult) \
               .then_inc(consts_made, 1)
            for u in range(TT):
                scale_x(0, u)
            split_slot(0, 0)
            for u in range(TT):
                gain_h(0, u)
            dve.wait_ge(dt_hi_done, 1)
            dve.tensor_tensor(dt_lo[:], dt_raw[:], dt_hi[:].bitcast(F32), ALU.subtract).then_inc(dt_lo_done, 1)
            blocks(dve, token_block)
            for j in range(KX):
                taps(NTB - 1, j)

        @block.gpsimd
        def _(pool):
            def h_low(tb, u):
                tok = slice(u * P, (u + 1) * P)
                pool.wait_ge(h_hi_done, TT * tb + u + 1)
                pool.tensor_tensor(h_lo[:, :, tok], h_f[:, :, tok], h_hi[:, :, tok].bitcast(F32), ALU.subtract) \
                    .then_inc(h_lo_done, 1)

            def token_block(tb, more, conv):
                for u in range(TT):
                    pool.wait_ge(q_scaled[u], tb + 1)
                    view = ev[:, u].rearrange("p (h d) -> p h d", h=HEADS)
                    pool.tensor_tensor(view, view, q_gain[:].unsqueeze(1).broadcast_to([P, HEADS, HEAD]), ALU.mult) \
                        .then_inc(ev_ready[u], 1)
                if more:
                    for u in range(TT):
                        h_low(tb + 1, u)

            pool.memset(zero[:], 0.0).then_inc(zero_made, 1)
            pool.wait_ge(zero_made, 1)
            halo = xbcT.rearrange("(k p) t -> p k t", p=P)
            for c, n in ((0, HALO), (SEQ + HALO, 2 * HALO), (T + 3 * HALO, HALO)):
                pool.dma_start(halo[:, :, c:c + n], zero[:, :, 0:n]).then_inc(halo_stored, 16)
            pool.wait_ge(consts_made, 2)
            for u in range(TT):
                h_low(0, u)
            blocks(pool, token_block)

        @block.tensor
        def _(pe):
            def turn(tb, u):
                pe.wait_ge(xn_done, TT * tb + u + 1)
                pe.wait_ge(h_f_done, TT * tb + u)
                for k in range(KD):
                    last = pe.transpose(ps_turn[:, k], x_t[:, u, k * P:(k + 1) * P], ident[:])
                last.then_inc(h_turned, 1)

            def token_block(tb, more, conv):
                pe.wait_ge(h_lo_done, TT * (tb + 1))
                for s in range(SLOTS):
                    par = s % 2
                    pe.wait_ge(slot_lo_done[par], tb * (SLOTS // 2) + s // 2 + 1)
                    if s < 4:
                        hi = w_hi[:, par].rearrange("p (k c) -> p k c", k=KD)
                        lo = w_lo[:, par].rearrange("p (k c) -> p k c", k=KD)
                        for half in range(2):
                            ft = 2 * s + half
                            u, c = ft % 4, slice(half * P, (half + 1) * P)
                            pe.wait_ge(ev_ready[u], tb * USES + ft // 4)
                            for k in range(KD):
                                last = split_products(pe, acc[:, u], hi[:, k, c], lo[:, k, c], h_hi[:, k], h_lo[:, k],
                                                      k == 0, k == KD - 1)
                            last.then_inc(acc_ready[u], 1)
                    if s == 3:
                        pe.wait_ge(dt_lo_done, 1)
                        pe.wait_ge(dt_ev_ready, tb)
                        for k in range(KD):
                            last = split_products(pe, ps_dt[:], dt_hi[:, k], dt_lo[:, k], h_hi[:, k], h_lo[:, k],
                                                  k == 0, k == KD - 1)
                        last.then_inc(dt_ready, 1)
                    if s >= 4:
                        kh = s % 2
                        hi = w_hi[:, par].rearrange("p (k c) -> p k c", k=KH)
                        lo = w_lo[:, par].rearrange("p (k c) -> p k c", k=KH)
                        for u in range(TT):
                            tok = slice(u * P, (u + 1) * P)
                            if kh == 0:
                                pe.wait_ge(ev_ready[u], tb * USES + USE[s])
                            for k in range(KH):
                                last = split_products(pe, acc[:, u], h_hi[:, kh * KH + k, tok], h_lo[:, kh * KH + k, tok],
                                                      hi[:, k], lo[:, k], kh + k == 0, kh * KH + k == KD - 1)
                            if kh == 1:
                                last.then_inc(acc_ready[u], 1)
                            if s == 11 and u == 1 and more:
                                turn(tb + 1, 3)
                        if kh == 0:
                            last.then_inc(half_done, 1)
                    if s in (8, 9, 10) and more:
                        turn(tb + 1, s - 8)

            pe.wait_ge(const_loaded, 16 * 4)
            for u in range(TT):
                turn(0, u)
            blocks(pe, token_block)


def attention_phase(nc, q_s, k_s, v_s, bias_pad, copies, masks, ident_dram, mixT):
    NT = 20
    COLT = 4
    BANDS = NT // COLT
    NTOK = T // P
    FIRST = [0, 1, 3, 5, 8]
    COUNT = [3, 4, 4, 3, 2]
    BIAS_ROW = [4, 0, 0, 0, 4]
    COL = [0, 8, 24, 32]
    BIAS_COL = [16, 8, 8, 0]
    ROWS = T // GRID_W
    KG = ROWS // 4
    LAG_TURN, LAG_PV = 3, 4
    MASK0, MASKS = HEAD, 48
    BR, BC = 16, 48

    with ExitStack() as ctx:
        def sb(name, shape, dt=F32):
            return ctx.enter_context(nc.sbuf_tensor("a_" + name, shape, dt))

        sem = ctx.enter_context(phase_semaphores(nc, "a_"))

        def some(name, n):
            return [sem(f"{name}{i}") for i in range(n)]

        ident = sb("ident", [P, P])
        mask_raw = sb("mask_raw", [P, 2, T])
        qa = [sb(f"qa{i}", [P, T], F32R) for i in range(2)]
        qb = [sb(f"qb{i}", [P, T], F32R) for i in range(2)]
        ka = [sb(f"ka{i}", [P, T], F32R) for i in range(2)]
        kb = [sb(f"kb{i}", [P, T], F32R) for i in range(2)]
        v = sb("v", [P, 2, COLT * KG, HEAD])
        q_raw = sb("q_raw", [P, 2, NTOK, HEAD])
        k_raw = sb("k_raw", [P, 2, NTOK, HEAD])
        q_st = sb("q_st", [P, TT, 2, HEAD], F32R)
        k_st = sb("k_st", [P, TT, 3, HEAD], F32R)
        bias = sb("bias", [P, 2, BR, BC])
        prob = sb("prob", [P, 4, TB])
        probT = sb("probT", [P, 2, TT, P])
        top = sb("top", [P, 4])
        neg_top = sb("neg_top", [P, 4])
        total = sb("total", [P, 4])
        inv = sb("inv", [P, 4])
        outT = sb("outT", [P, T])

        ps_s = [ctx.enter_context(nc.psum_tensor(f"a_ps_s{i}", [P, TB], F32)) for i in range(2)]
        ps_p = [ctx.enter_context(nc.psum_tensor(f"a_ps_p{i}", [P, TT, P], F32)) for i in range(2)]
        ps_q = ctx.enter_context(nc.psum_tensor("a_ps_q", [P, TT, P], F32))
        ps_ka = ctx.enter_context(nc.psum_tensor("a_ps_ka", [P, TT, P], F32))
        ps_kb = ctx.enter_context(nc.psum_tensor("a_ps_kb", [P, TT, P], F32))
        ps_o = ctx.enter_context(nc.psum_tensor("a_ps_o", [P, COLT, P], F32))

        const_loaded = sem("const_loaded")
        copied = sem("copied")
        masks_set = sem("masks_set")
        qk_loaded = some("qk_loaded", 2)
        v_loaded = some("v_loaded", 2)
        bias_loaded = some("bias_loaded", 2)
        hi_made = sem("hi_made")
        st_made = sem("st_made")
        st_step = sem("st_step")
        q_turned = sem("q_turned")
        k_turned = sem("k_turned")
        qa_out = sem("qa_out")
        qb_out = sem("qb_out")
        ka_out = sem("ka_out")
        kb_out = sem("kb_out")
        scored = sem("scored")
        score_seen = sem("score_seen")
        topped = sem("topped")
        biased = sem("biased")
        exped = sem("exped")
        inverted = sem("inverted")
        scaled = sem("scaled")
        p_turned = sem("p_turned")
        p_out = sem("p_out")
        weighed = sem("weighed")
        o_out = sem("o_out")
        o_stored = some("o_stored", BANDS)

        def wait(eng, s, n):
            if not isinstance(n, int) or n > 0:
                eng.wait_ge(s, n)

        def pairs(eng, body):
            body(0, True, False)
            with eng.Fori(1, HEADS // 2 - 1) as i:
                body(i, False, False)
            body(HEADS // 2 - 1, False, True)

        def number(head):
            return 2 * head[0] + head[1]

        def following(head):
            return (head[0], 1) if head[1] == 0 else (head[0] + 1, 0)

        def behind(head, a, lag, first):
            if a >= lag:
                return head, a - lag
            if first and head[1] == 0:
                return None
            return ((head[0], 0) if head[1] == 1 else (head[0] - 1, 1)), a - lag + NT

        block = ctx.enter_context(nc.Block())

        @block.sync
        def _(sp):
            sp.dma_start(ident[:], ident_dram).then_inc(const_loaded, 16)
            sp.dma_start(mask_raw[MASK0:MASK0 + MASKS], masks).then_inc(const_loaded, 16)
            q_src = q_s.rearrange("(t p) d -> p t d", p=P)
            k_src = k_s.rearrange("(t p) d -> p t d", p=P)
            v_src = v_s.rearrange("(m r c) d -> r c m d", r=4, c=GRID_W)
            skewed = copies[BIAS_SKEW:BIAS_SKEW + 16 * (PITCH - 1)].rearrange("(j x) -> j x", j=16)

            def load_qk(head):
                d = bass.ds(number(head) * HEAD, HEAD)
                sp.dma_start(q_raw[:, head[1]], q_src[:, :, d]).then_inc(qk_loaded[head[1]], 16)
                sp.dma_start(k_raw[:, head[1]], k_src[:, :, d]).then_inc(qk_loaded[head[1]], 16)

            def load_bias(head):
                for i in range(8):
                    at = bass.ds(number(head) * (PR * PC) + (7 - i) * PC, BR * PC)
                    src = skewed[:, at].rearrange("j (r c) -> j r c", c=PC)[:, :, 0:BC]
                    sp.dma_start(bias[16 * i:16 * i + 16, head[1]], src).then_inc(bias_loaded[head[1]], 16)

            def load_v(head):
                d = bass.ds(number(head) * HEAD, HEAD)
                for c in range(COLT):
                    for r in range(4):
                        sp.dma_start(v[32 * r:32 * r + 32, head[1], c * KG:(c + 1) * KG],
                                     v_src[r, COL[c]:COL[c] + 32, :, d]).then_inc(v_loaded[head[1]], 16)

            for j in range(16):
                sp.dma_start(copies[j * PITCH:j * PITCH + HEADS * PR * PC], bias_pad).then_inc(copied, 16)
            load_qk((0, 0))
            load_qk((0, 1))
            load_v((0, 0))
            sp.wait_ge(copied, 16 * 16)
            load_bias((0, 0))
            load_bias((0, 1))
            load_v((0, 1))
            with sp.Fori(0, HEADS // 2 - 1) as i:
                for par in range(2):
                    head = (i, par)
                    sp.wait_ge(st_made, BANDS * (number(head) + 1))
                    load_qk((i + 1, par))
                    sp.wait_ge(topped, NT * (number(head) + 1))
                    load_bias((i + 1, par))
                    sp.wait_ge(weighed, NT * (number(head) + 1))
                    load_v((i + 1, par))

        @block.gpsimd
        def _(pool):
            def split_low(head, g):
                n, par = BANDS * number(head) + g, head[1]
                tiles = slice(g * TT, (g + 1) * TT)
                pool.wait_ge(hi_made, 2 * n + 2)
                pool.tensor_tensor(q_st[:, :, 1], q_raw[:, par, tiles], q_st[:, :, 0].bitcast(F32), ALU.subtract) \
                    .then_inc(st_step, 1)
                pool.wait_ge(st_step, n + 1)
                pool.tensor_tensor(k_st[:, :, 2], k_raw[:, par, tiles], k_st[:, :, 0].bitcast(F32), ALU.subtract) \
                    .then_inc(st_made, 1)

            def pair(i, first, last):
                for par in range(2):
                    head = (i, par)
                    ahead = not (last and par == 1)
                    for a in range(NT):
                        if ahead and a % COLT == 0:
                            split_low(following(head), a // COLT)

            for g in range(BANDS):
                split_low((0, 0), g)
            pairs(pool, pair)
            for b in range(BANDS):
                pool.wait_ge(o_stored[b], 16 * HEADS // 2)

        @block.vector
        def _(dve):
            def out_qk(head, g):
                n, cols = BANDS * number(head) + g, slice(g * TB, (g + 1) * TB)
                wait(dve, scored, NT * (number(head) - 1))
                dve.wait_ge(q_turned, n + 1)
                dve.tensor_copy(qa[head[1]][:, cols].rearrange("p (t i j) -> p t i j", t=COLT, i=8),
                                ps_q[:].rearrange("p t c -> p (t c)").rearrange("p (i t j) -> p t i j", i=8, t=COLT)) \
                   .then_inc(qa_out, 1)
                dve.wait_ge(k_turned, n + 1)
                dve.tensor_copy(kb[head[1]][0:HEAD, cols], ps_kb[0:HEAD].rearrange("p t c -> p (t c)")) \
                   .then_inc(kb_out, 1)

            def add_bias(head, a):
                G, b, c = NT * number(head) + a, a // COLT, a % COLT
                rows = COUNT[b] * 4
                n = COUNT[b] * P
                if a == 0:
                    dve.wait_ge(bias_loaded[head[1]], 16 * 8 * (head[0] + 1))
                dve.wait_ge(scored, G + 1)
                wait(dve, p_turned, G - 3)
                dve.sem_inc(score_seen, 1)
                dve.tensor_tensor_reduce(
                    prob[:, a % 4, 0:n].rearrange("p (r c) -> p r c", c=32),
                    ps_s[a % 2][:, 0:n].rearrange("p (r c) -> p r c", c=32),
                    bias[:, head[1], BIAS_ROW[b]:BIAS_ROW[b] + rows, BIAS_COL[c]:BIAS_COL[c] + 32],
                    1.0, LOWEST, ALU.add, ALU.max, top[:, a % 4:a % 4 + 1]).then_inc(topped, 1)

            def negate(head, a):
                G = NT * number(head) + a
                dve.wait_ge(topped, G + 1)
                dve.tensor_scalar(neg_top[:, a % 4:a % 4 + 1], top[:, a % 4:a % 4 + 1], -1.0, None, ALU.mult) \
                   .then_inc(biased, 1)

            def invert(head, a):
                G = NT * number(head) + a
                dve.wait_ge(exped, G + 1)
                dve.reciprocal(inv[:, a % 4:a % 4 + 1], total[:, a % 4:a % 4 + 1]).then_inc(inverted, 1)

            def scale(head, a):
                G, n = NT * number(head) + a, COUNT[a // COLT] * P
                dve.wait_ge(inverted, G + 1)
                dve.tensor_scalar(prob[:, a % 4, 0:n], prob[:, a % 4, 0:n], inv[:, a % 4:a % 4 + 1], None, ALU.mult) \
                   .then_inc(scaled, 1)

            def out_band(head, b):
                lo = HEAD * head[1]
                dve.wait_ge(weighed, NT * number(head) + COLT * (b + 1))
                if head[1] == 0:
                    wait(dve, o_stored[b], 16 * head[0])
                dst = outT[lo:lo + HEAD, b * TB:(b + 1) * TB].rearrange("p (i t j) -> p t i j", i=8, t=COLT)
                src = ps_o[lo:lo + HEAD].rearrange("p t (i j) -> p t i j", i=8)
                dve.tensor_copy(dst, src).then_inc(o_out, 1)

            def pair(i, first, last):
                for par in range(2):
                    head = (i, par)
                    ahead = not (last and par == 1)
                    for a in range(NT):
                        add_bias(head, a)
                        negate(head, a)
                        late = behind(head, a, 1, first)
                        if late:
                            invert(*late)
                            scale(*late)
                        if ahead and a % COLT == 2:
                            out_qk(following(head), a // COLT)
                        late = behind(head, a, LAG_PV, first)
                        if late and late[1] % COLT == COLT - 1:
                            out_band(late[0], late[1] // COLT)

            dve.wait_ge(const_loaded, 32)
            rows = slice(MASK0, MASK0 + MASKS)
            for i in range(2):
                dve.tensor_copy(qb[i][rows], mask_raw[rows, 0]).then_inc(masks_set, 1)
                dve.tensor_copy(kb[i][rows], mask_raw[rows, 1]).then_inc(masks_set, 1)
            for g in range(BANDS):
                out_qk((0, 0), g)
            pairs(dve, pair)
            end = (HEADS // 2 - 1, 1)
            invert(end, NT - 1)
            scale(end, NT - 1)
            out_band(end, BANDS - 1)

        @block.scalar
        def _(act):
            def split_high(head, g):
                n, par = BANDS * number(head) + g, head[1]
                tiles = slice(g * TT, (g + 1) * TT)
                if g == 0:
                    act.wait_ge(qk_loaded[par], 32 * (head[0] + 1))
                wait(act, k_turned, n)
                act.copy(q_st[:, :, 0], q_raw[:, par, tiles]).then_inc(hi_made, 1)
                act.copy(k_st[:, :, 0:2], k_raw[:, par, tiles].unsqueeze(2).broadcast_to([P, TT, 2, HEAD])) \
                   .then_inc(hi_made, 1)

            def out_q_high(head, g):
                n, cols = BANDS * number(head) + g, slice(g * TB, (g + 1) * TB)
                act.wait_ge(qa_out, n + 1)
                act.copy(qb[head[1]][0:HEAD, cols], qa[head[1]][0:HEAD, cols].bitcast(F32)).then_inc(qb_out, 1)

            def out_k(head, g):
                n, cols = BANDS * number(head) + g, slice(g * TB, (g + 1) * TB)
                wait(act, scored, NT * (number(head) - 1))
                act.wait_ge(k_turned, n + 1)
                act.copy(ka[head[1]][:, cols], ps_ka[:].rearrange("p t c -> p (t c)")).then_inc(ka_out, 1)

            def exp(head, a):
                G, n = NT * number(head) + a, COUNT[a // COLT] * P
                act.wait_ge(biased, G + 1)
                wait(act, inverted, G - 3)
                act.activation(prob[:, a % 4, 0:n], prob[:, a % 4, 0:n], ACT.Exp, bias=neg_top[:, a % 4:a % 4 + 1],
                               accum_out=total[:, a % 4:a % 4 + 1]).then_inc(exped, 1)

            def out_p(head, a):
                G, n = NT * number(head) + a, COUNT[a // COLT]
                act.wait_ge(p_turned, G + 1)
                wait(act, weighed, G - 1)
                act.copy(probT[:, a % 2, 0:n], ps_p[a % 2][:, 0:n]).then_inc(p_out, 1)

            def store(head, b):
                act.wait_ge(o_out, BANDS * number(head) + b + 1)
                act.dma_start(mixT[bass.ds(head[0] * P, P), b * TB:(b + 1) * TB], outT[:, b * TB:(b + 1) * TB]) \
                   .then_inc(o_stored[b], 16)

            def pair(i, first, last):
                for par in range(2):
                    head = (i, par)
                    ahead = not (last and par == 1)
                    for a in range(NT):
                        if ahead and a % COLT == 0:
                            split_high(following(head), a // COLT)
                        exp(head, a)
                        if ahead and a % COLT == 2:
                            out_k(following(head), a // COLT)
                        if ahead and a % COLT == 3:
                            out_q_high(following(head), a // COLT)
                        late = behind(head, a, LAG_TURN, first)
                        if late:
                            out_p(*late)
                        late = behind(head, a, LAG_PV + 2, first)
                        if late and late[0][1] == 1 and late[1] % COLT == COLT - 1:
                            store(late[0], late[1] // COLT)

            split_high((0, 0), 0)
            for g in range(BANDS):
                out_k((0, 0), g)
                if g + 1 < BANDS:
                    split_high((0, 0), g + 1)
                out_q_high((0, 0), g)
            pairs(act, pair)
            end = (HEADS // 2 - 1, 1)
            for a in range(NT - LAG_TURN, NT):
                out_p(end, a)
            store(end, BANDS - 2)
            store(end, BANDS - 1)

        @block.tensor
        def _(pe):
            def turn_qk(head, g):
                n = BANDS * number(head) + g
                pe.wait_ge(st_made, n + 1)
                wait(pe, qa_out, n)
                wait(pe, ka_out, n)
                wait(pe, kb_out, n)
                for t in range(TT):
                    last = pe.transpose(ps_q[:, t], q_st[:, t].rearrange("p s d -> p (s d)").bitcast(F32), ident[:])
                last.then_inc(q_turned, 1)
                for t in range(TT):
                    pe.transpose(ps_ka[:, t], k_st[:, t, 0:2].rearrange("p s d -> p (s d)").bitcast(F32), ident[:])
                    last = pe.transpose(ps_kb[0:HEAD, t], k_st[:, t, 2].bitcast(F32), ident[:])
                last.then_inc(k_turned, 1)

            def scores(head, a):
                G, b, c, par = NT * number(head) + a, a // COLT, a % COLT, head[1]
                if a == 0:
                    for s in (qa_out, qb_out, ka_out, kb_out):
                        pe.wait_ge(s, BANDS * (number(head) + 1))
                wait(pe, topped, G - 1)
                rows = slice(4 * FIRST[b], 4 * (FIRST[b] + COUNT[b]))
                cols = slice(COL[c], COL[c] + 32)

                def queries(x, k):
                    return x[par][0:k, a * P:(a + 1) * P]

                def keys(x, k):
                    return x[par][0:k].rearrange("p (r c) -> p r c", c=GRID_W)[:, rows, cols]

                out = ps_s[a % 2][:, 0:COUNT[b] * P].rearrange("p (r c) -> p r c", c=32)
                pe.matmul(out, queries(qa, P), keys(ka, P), start=True, stop=False)
                pe.matmul(out, queries(qb, MASK0 + MASKS), keys(kb, MASK0 + MASKS), start=False, stop=True) \
                  .then_inc(scored, 1)

            def turn_p(head, a):
                G = NT * number(head) + a
                pe.wait_ge(scaled, G + 1)
                wait(pe, p_out, G - 1)
                for j in range(COUNT[a // COLT]):
                    last = pe.transpose(ps_p[a % 2][:, j], prob[:, a % 4, j * P:(j + 1) * P], ident[:])
                last.then_inc(p_turned, 1)

            def weigh(head, a):
                G, b, c, par = NT * number(head) + a, a // COLT, a % COLT, head[1]
                if a == 0:
                    pe.wait_ge(v_loaded[par], 16 * 16 * (head[0] + 1))
                if c == 0:
                    wait(pe, o_out, BANDS * number(head) + b)
                pe.wait_ge(p_out, G + 1)
                for j in range(COUNT[b]):
                    last = pe.matmul(ps_o[HEAD * par:HEAD * (par + 1), c], v[:, par, c * KG + FIRST[b] + j],
                                     probT[:, a % 2, j], start=j == 0, stop=j == COUNT[b] - 1)
                last.then_inc(weighed, 1)

            def pair(i, first, last):
                for par in range(2):
                    head = (i, par)
                    ahead = not (last and par == 1)
                    for a in range(NT):
                        scores(head, a)
                        if ahead and a % COLT == 1:
                            turn_qk(following(head), a // COLT)
                        late = behind(head, a, LAG_PV, first)
                        if late:
                            weigh(*late)
                        late = behind(head, a, LAG_TURN, first)
                        if late:
                            turn_p(*late)

            pe.wait_ge(const_loaded, 32)
            pe.wait_ge(masks_set, 4)
            for g in range(BANDS):
                turn_qk((0, 0), g)
            pairs(pe, pair)
            end = (HEADS // 2 - 1, 1)
            weigh(end, NT - LAG_PV)
            for a in range(NT - LAG_TURN, NT):
                turn_p(end, a)
                weigh(end, a)


def ssd_phase(nc, xcT, dtT, z_s, head_rows, norm_cols, tri, tri_masks, ident_dram, ident_bf_dram, mixT):
    NCH = T // P
    PAIRS = NCH // 2
    LAST, FIRST = SEQ // P - 1, SEQ // P
    H2 = 2 * HEADS
    GH = HEADS // GROUPS
    GW = GH * HEAD
    A_, NB, E_, DT, CD, W_ = (H2 * i for i in range(6))
    KX, KB = D_SSM // P, GROUPS

    with ExitStack() as ctx:
        def sb(name, shape, dt=F32):
            return ctx.enter_context(nc.sbuf_tensor("s_" + name, shape, dt))

        sem = ctx.enter_context(phase_semaphores(nc, "s_"))

        def two(name):
            return [sem(name + "0"), sem(name + "1")]

        ident = sb("ident", [P, P])
        ident_bf = sb("ident_bf", [P, P], BF16)
        upper = sb("upper", [P, 3, P])
        masks = sb("masks", [P, 2, P], BF16)
        rows = sb("rows", [P, 3, H2])
        gain = sb("gain", [P, KX])
        eps = sb("eps", [P, 1])
        tab = sb("tab", [P, NCH, 6 * H2])
        x_tok = sb("x_tok", [P, NCH, D_SSM])
        s_f = sb("s_f", [P, NCH, D_SSM])
        h_b = sb("h_b", [P, NCH + 1, D_SSM])
        h_f = sb("h_f", [P, 2, D_SSM])

        def heads(x):
            return x.rearrange("p (h d) -> p h d", d=HEAD)

        def by_head(x, n=HEAD):
            return x.unsqueeze(2).broadcast_to([P, x.shape[1], n])

        const_loaded = sem("const_loaded")

        with ExitStack() as ctx1:
            def sb1(name, shape, dt=F32):
                return ctx1.enter_context(nc.sbuf_tensor("s1_" + name, shape, dt))

            def ps1(name, shape):
                return ctx1.enter_context(nc.psum_tensor("s1_" + name, shape, F32))

            dt_t = sb1("dt_t", [H2, T])
            neg_a = sb1("neg_a", [P, H2])
            tmp = [sb1(f"tmp{i}", [P, NCH, H2]) for i in range(6)]
            xc = sb1("xc", [P, 2, KX + KB, P])
            tab_c = sb1("tab_c", [P, 2, 2 * H2])
            b_tok = sb1("b_tok", [P, 2, KB * P])
            xw = sb1("xw", [P, 2, 2, D_SSM])
            h_cut = sb1("h_cut", [P, 2, D_SSM])
            ps_x = [ps1(f"ps_x{i}", [P, KX, P]) for i in range(2)]
            ps_b = [ps1(f"ps_b{i}", [P, 4, P]) for i in range(2)]
            ps_s = [[ps1(f"ps_s{i}{d}", [P, D_SSM]) for d in range(2)] for i in range(2)]

            dt_loaded = sem("dt_loaded")
            dt_turned = sem("dt_turned")
            chain = sem("chain")
            exps = sem("exps")
            table_a = sem("table_a")
            exponents = sem("exponents")
            tables_made = sem("tables_made")
            sums_ready = sem("sums_ready")
            xc_loaded = two("xc_loaded")
            x_turned = two("x_turned")
            x_out = two("x_out")
            b_out = two("b_out")
            tab_out = two("tab_out")
            xw_made = two("xw_made")
            s_ready = two("s_ready")
            s_out = two("s_out")
            cut_done = two("cut_done")
            h_done = two("h_done")

            def ahead(eng, early, late):
                early(0, 0, NCH - 1)
                with eng.Fori(0, PAIRS - 1) as i:
                    c = eng.snap(NCH - 1 - 2 * i)
                    early(i, 1, c - 1)
                    late(i, 0, c)
                    early(i + 1, 0, c - 2)
                    late(i, 1, c - 1)
                early(PAIRS - 1, 1, 0)
                late(PAIRS - 1, 0, 1)
                late(PAIRS - 1, 1, 0)

            def at(c):
                return bass.ds(c, 1)

            def flat(x):
                return x.rearrange("p o x -> p (o x)")

            def sums(b):
                return b[:].rearrange("p a c -> p (a c)")[:, 0:NCH * H2].rearrange("p (c h) -> p c h", h=H2)

            with nc.Block() as block:
                @block.sync
                def _(sp):
                    sp.dma_start(ident[:], ident_dram).then_inc(const_loaded, 16)
                    sp.dma_start(ident_bf[:], ident_bf_dram).then_inc(const_loaded, 16)
                    sp.dma_start(upper[:], tri).then_inc(const_loaded, 16)
                    sp.dma_start(masks[:], tri_masks).then_inc(const_loaded, 16)
                    sp.dma_start(rows[:], head_rows).then_inc(const_loaded, 16)
                    sp.dma_start(gain[:], norm_cols).then_inc(const_loaded, 16)
                    sp.dma_start(dt_t[:], dtT).then_inc(dt_loaded, 16)
                    src = xcT.rearrange("(k p) t -> p k t", p=P)
                    with sp.Fori(0, PAIRS) as i:
                        c = sp.snap(NCH - 1 - 2 * i)
                        for par in range(2):
                            sp.wait_ge(const_loaded, 16 * 6)
                            sp.wait_ge(x_turned[par], i)
                            sp.dma_start(xc[:, par], src[:, 0:KX + KB, bass.ds((c - par) * P, P)]) \
                              .then_inc(xc_loaded[par], 16)

                @block.vector
                def _(dve):
                    done = [0]

                    def link(ins):
                        done[0] += 1
                        ins.then_inc(chain, 1)
                        dve.wait_ge(chain, done[0])

                    u, na, s, z, p, v = (t[:] for t in tmp)

                    def cols(c, d=None):
                        a, b = (0, H2) if d is None else (d * HEADS, (d + 1) * HEADS)
                        return tab[:, :, c + a:c + b]

                    def half(x, d):
                        return x[:, :, d * HEADS:(d + 1) * HEADS]

                    def by_chunk(x):
                        return x.unsqueeze(1).broadcast_to([P, NCH, H2])

                    link(dve.memset(eps[:], EPS))
                    dve.wait_ge(const_loaded, 16 * 6)
                    dve.wait_ge(dt_turned, 1)
                    link(dve.tensor_tensor(u, sums(ps_x[0]), by_chunk(rows[:, 0]), ALU.add))
                    link(dve.scalar_tensor_tensor(na, u, -1.0, u, ALU.mult, ALU.min))
                    dve.wait_ge(exps, 2)
                    link(dve.tensor_scalar(s, na, 2.0, None, ALU.add))
                    link(dve.reciprocal(z, s))
                    link(dve.tensor_tensor(s, na, z, ALU.mult))
                    link(dve.tensor_tensor(z, s, s, ALU.mult))
                    link(dve.tensor_scalar(p, z, 1.0 / 17, None, ALU.mult))
                    for odd in (15, 13, 11, 9, 7, 5, 3):
                        link(dve.scalar_tensor_tensor(p, p, 1.0 / odd, z, ALU.add, ALU.mult))
                    link(dve.scalar_tensor_tensor(v, p, 1.0, s, ALU.add, ALU.mult))
                    link(dve.tensor_scalar(u, u, 0.0, None, ALU.max))
                    link(dve.scalar_tensor_tensor(cols(DT), v, 2.0, u, ALU.mult, ALU.add))
                    link(dve.tensor_scalar(neg_a[:], neg_a[:], -1.0, None, ALU.mult))
                    link(dve.tensor_tensor(cols(A_), cols(DT), by_chunk(neg_a[:]), ALU.mult))
                    dve.sem_inc(table_a, 1)
                    dve.wait_ge(sums_ready, 1)
                    pf, px, total = sums(ps_x[0]), sums(ps_x[1]), sums(ps_b[0])
                    link(dve.tensor_copy(v, total))
                    link(dve.tensor_scalar(cols(NB, 0), half(pf, 0), -1.0, None, ALU.mult))
                    link(dve.tensor_copy(cols(NB, 1), half(px, 1)))
                    link(dve.tensor_copy(half(u, 0), half(pf, 0)))
                    link(dve.tensor_tensor(half(u, 1), half(v, 1), half(px, 1), ALU.subtract))
                    link(dve.tensor_tensor(half(s, 0), half(v, 0), half(pf, 0), ALU.subtract))
                    link(dve.tensor_copy(half(s, 1), half(px, 1)))
                    dve.sem_inc(exponents, 1)
                    dve.wait_ge(exps, 5)
                    link(dve.tensor_tensor(cols(W_), s, cols(DT), ALU.mult))
                    for c in (CD, W_):
                        link(dve.memset(tab[:, LAST, c:c + HEADS], 0.0))
                        link(dve.memset(tab[:, FIRST, c + HEADS:c + H2], 0.0))
                    link(dve.memset(h_b[:, NCH], 0.0))
                    link(dve.memset(h_f[:, 0], 0.0))
                    dve.sem_inc(tables_made, 1)

                    def weigh_x(i, par, c):
                        dve.wait_ge(cut_done[par], i)
                        dve.tensor_copy(tab_c[:, par:par + 1], tab[:, at(c), CD:CD + 2 * H2]).then_inc(tab_out[par], 1)
                        dve.wait_ge(tab_out[par], i + 1)
                        dve.wait_ge(x_out[par], i + 1)
                        dve.wait_ge(s_ready[par], i)
                        for d in range(2):
                            dve.tensor_tensor(heads(xw[:, par, d]), heads(flat(x_tok[:, at(c)])),
                                              by_head(tab_c[:, par, H2 + d * HEADS:H2 + (d + 1) * HEADS]), ALU.mult) \
                               .then_inc(xw_made[par], 1)

                    def add_state(i, par, c):
                        dve.wait_ge(cut_done[par], i + 1)
                        dve.wait_ge(s_ready[par], i + 1)
                        dve.tensor_tensor(flat(h_b[:, at(c)]), h_cut[:, par], ps_s[par][1][:], ALU.add) \
                           .then_inc(h_done[par], 1)

                    ahead(dve, weigh_x, add_state)

                @block.scalar
                def _(act):
                    u, na, s, z, p, v = (t[:] for t in tmp)
                    act.wait_ge(const_loaded, 16 * 6)
                    act.activation(neg_a[:], rows[:, 1], ACT.Exp).then_inc(exps, 1)
                    act.wait_ge(chain, 3)
                    act.activation(na, na, ACT.Exp).then_inc(exps, 1)
                    act.wait_ge(exponents, 1)
                    act.activation(tab[:, :, E_:E_ + H2], u, ACT.Exp).then_inc(exps, 1)
                    act.activation(tab[:, :, CD:CD + H2], v, ACT.Exp).then_inc(exps, 1)
                    act.activation(s, s, ACT.Exp).then_inc(exps, 1)

                    def out_x(i, par, c):
                        act.wait_ge(x_turned[par], i + 1)
                        act.copy(flat(x_tok[:, at(c)]), ps_x[par][:].rearrange("p k c -> p (k c)")).then_inc(x_out[par], 1)
                        act.wait_ge(s_ready[par], i)
                        act.copy(b_tok[:, par], ps_b[par][:, 0:KB].rearrange("p k c -> p (k c)")).then_inc(b_out[par], 1)

                    def out_s(i, par, c):
                        act.wait_ge(s_ready[par], i + 1)
                        act.copy(flat(s_f[:, at(c)]), ps_s[par][0][:]).then_inc(s_out[par], 1)

                    ahead(act, out_x, out_s)

                @block.gpsimd
                def _(pool):
                    pool.wait_ge(tables_made, 1)
                    with pool.Fori(0, PAIRS) as i:
                        c = pool.snap(NCH - 1 - 2 * i)
                        for par in range(2):
                            pool.wait_ge(tab_out[par], i + 1)
                            pool.wait_ge(h_done[par], i)
                            pool.wait_ge(h_done[1 - par], i + par)
                            pool.tensor_tensor(heads(h_cut[:, par]), heads(flat(h_b[:, at(c - par + 1)])),
                                               by_head(tab_c[:, par, HEADS:H2]), ALU.mult).then_inc(cut_done[par], 1)

                @block.tensor
                def _(pe):
                    pe.wait_ge(const_loaded, 16 * 6)
                    pe.wait_ge(dt_loaded, 16)
                    for c in range(NCH):
                        last = pe.transpose(sums(ps_x[0])[:, c], dt_t[:, c * P:(c + 1) * P], ident[0:H2, 0:H2])
                    last.then_inc(dt_turned, 1)
                    pe.wait_ge(table_a, 1)
                    for b, which in ((ps_x[0], 0), (ps_x[1], 1), (ps_b[0], 2)):
                        last = pe.matmul(sums(b), upper[:, which], tab[:, :, A_:A_ + H2], start=True, stop=True)
                    last.then_inc(sums_ready, 1)
                    pe.wait_ge(tables_made, 1)

                    def turn(i, par, c):
                        pe.wait_ge(xc_loaded[par], 16 * (i + 1))
                        pe.wait_ge(x_out[par], i)
                        pe.wait_ge(b_out[par], i)
                        for k in range(KX):
                            pe.transpose(ps_x[par][:, k], xc[:, par, k], ident[:])
                        for k in range(KB):
                            last = pe.transpose(ps_b[par][:, k], xc[:, par, KX + k], ident[:])
                        last.then_inc(x_turned[par], 1)

                    def states(i, par, c):
                        pe.wait_ge(b_out[par], i + 1)
                        pe.wait_ge(xw_made[par], 2 * i + 2)
                        pe.wait_ge(s_out[par], i)
                        pe.wait_ge(h_done[par], i)
                        for d in range(2):
                            for g in range(GROUPS):
                                cols = slice(g * GW, (g + 1) * GW)
                                last = pe.matmul(ps_s[par][d][:, cols], b_tok[:, par, g * P:(g + 1) * P], xw[:, par, d, cols],
                                                 start=True, stop=True)
                        last.then_inc(s_ready[par], 1)

                    ahead(pe, turn, states)

        with ExitStack() as ctx2:
            def sb2(name, shape, dt=F32):
                return ctx2.enter_context(nc.sbuf_tensor("s2_" + name, shape, dt))

            def ps2(name, shape):
                return ctx2.enter_context(nc.psum_tensor("s2_" + name, shape, F32))

            NTAB = CD + HEADS
            bc = sb2("bc", [P, 2, 2 * KB, P])
            z_t = sb2("z_t", [P, 2, D_SSM])
            tab_c = sb2("tab_c", [P, 2, NTAB])
            cb = sb2("cb", [P, 2, GROUPS, P])
            decay = sb2("decay", [P, 2, 4, GH, P])
            xdt = sb2("xdt", [P, 2, 2, D_SSM])
            off_f = sb2("off_f", [P, 2, D_SSM])
            off_b = sb2("off_b", [P, 2, D_SSM])
            skip = sb2("skip", [P, 2, D_SSM])
            h_cut = sb2("h_cut", [P, 2, D_SSM])
            g_t = sb2("g_t", [P, 2, D_SSM])
            junk = sb2("junk", [P, 2, GROUPS, GW])
            ss = sb2("ss", [P, 2, GROUPS])
            ss_ln = sb2("ss_ln", [P, 2, GROUPS])
            rstd = sb2("rstd", [P, 2, GROUPS])
            gT = sb2("gT", [P, 2, KX, P])

            ps_cb = ps2("ps_cb", [P, 4, P])
            ps_r = [ps2(f"ps_r{i}", [P, GH, P]) for i in range(2)]
            ps_y = [ps2(f"ps_y{i}", [P, D_SSM]) for i in range(2)]
            ps_off = [ps2(f"ps_off{i}", [P, D_SSM]) for i in range(2)]
            ps_t = ps2("ps_t", [P, KX, P])

            def four(name):
                return [sem(f"{name}{i}") for i in range(4)]

            bc_loaded = two("bc_loaded")
            z_loaded = two("z_loaded")
            tab_done = sem("tab_done")
            cb_ready = sem("cb_ready")
            xdt_f_done = sem("xdt_f_done")
            xdt_b_done = sem("xdt_b_done")
            hf_done = sem("hf_done")
            off_read = sem("off_read")
            t_ready = sem("t_ready")
            t_out = sem("t_out")
            r_ready = four("r_ready")
            e_done = four("e_done")
            m_done = four("m_done")
            cb_out = two("cb_out")
            y_ready = two("y_ready")
            y_read = two("y_read")
            off_ready = two("off_ready")
            off_b_done = two("off_b_done")
            off_f_done = two("off_f_done")
            skip_x = two("skip_x")
            skip_done = two("skip_done")
            y_sum = two("y_sum")
            gated = two("gated")
            sq_done = two("sq_done")
            ln_done = two("ln_done")
            rstd_done = two("rstd_done")
            normed = two("normed")
            cutf_done = two("cutf_done")
            g_stored = two("g_stored")

            def chunk(i, par):
                return 2 * i + par

            def pairs(eng, body):
                body(0, True, False)
                with eng.Fori(1, PAIRS - 1) as i:
                    body(i, False, False)
                body(PAIRS - 1, False, True)

            def steps(eng, step):
                def body(i, first, last):
                    step((i, 0), (i, 1), None if first else (i - 1, 1))
                    step((i, 1), None if last else (i + 1, 0), (i, 0))
                pairs(eng, body)

            def flat2(x):
                return x.rearrange("p o x -> p (o x)")

            with nc.Block() as block:
                @block.sync
                def _(sp):
                    src = xcT.rearrange("(k p) t -> p k t", p=P)
                    dst = mixT.rearrange("(k p) t -> p k t", p=P)
                    K0 = D_ATT // P

                    def load(i, par):
                        tok = bass.ds(chunk(i, par) * P, P)
                        sp.wait_ge(off_ready[par], i)
                        sp.dma_start(bc[:, par], src[:, KX:, tok]).then_inc(bc_loaded[par], 16)
                        sp.wait_ge(gated[par], i)
                        sp.dma_start(z_t[:, par], z_s[tok, :]).then_inc(z_loaded[par], 16)

                    def store(i, par):
                        sp.wait_ge(t_out, chunk(i, par) + 1)
                        sp.dma_start(dst[:, K0:, bass.ds(chunk(i, par) * P, P)], gT[:, par]).then_inc(g_stored[par], 16)

                    def body(i, first, last):
                        for par in range(2):
                            if not last:
                                load(i + 1, par)
                            if not (first and par == 0):
                                store(*((i, 0) if par else (i - 1, 1)))

                    load(0, 0)
                    load(0, 1)
                    pairs(sp, body)
                    store(PAIRS - 1, 1)
                    for par in range(2):
                        sp.wait_ge(g_stored[par], 16 * PAIRS)

                @block.vector
                def _(dve):
                    def table(i, par):
                        c = chunk(i, par)
                        dve.wait_ge(y_ready[par], i)
                        dve.wait_ge(cutf_done[par], i)
                        dve.tensor_copy(tab_c[:, par:par + 1], tab[:, bass.ds(c, 1), 0:NTAB]).then_inc(tab_done, 1)
                        dve.wait_ge(tab_done, c + 1)
                        dve.tensor_tensor(heads(xdt[:, par, 0]), heads(flat2(x_tok[:, bass.ds(c, 1)])),
                                          by_head(tab_c[:, par, DT:DT + HEADS]), ALU.mult).then_inc(xdt_f_done, 1)

                    def mix(i, par, q):
                        dve.wait_ge(e_done[q], chunk(i, par) + 1)
                        dve.wait_ge(cb_out[par], i + 1)
                        dve.tensor_tensor(decay[:, par, q], decay[:, par, q],
                                          cb[:, par, q // 2].unsqueeze(1).broadcast_to([P, GH, P]), ALU.mult) \
                           .then_inc(m_done[q], 1)

                    def outputs(i, par):
                        c = chunk(i, par)
                        dve.wait_ge(off_ready[par], i + 1)
                        dve.wait_ge(skip_done[par], i)
                        dve.tensor_tensor(heads(off_f[:, par]), heads(ps_off[0][:]), by_head(tab_c[:, par, E_:E_ + HEADS]),
                                          ALU.mult).then_inc(off_f_done[par], 1)
                        dve.tensor_tensor(heads(off_b[:, par]), heads(ps_off[1][:]),
                                          by_head(tab_c[:, par, E_ + HEADS:E_ + H2]), ALU.mult).then_inc(off_read, 1)
                        dve.wait_ge(cutf_done[par], i + 1)
                        dve.tensor_tensor(h_f[:, 1 - par], h_cut[:, par], flat2(s_f[:, bass.ds(c, 1)]), ALU.add) \
                           .then_inc(hf_done, 1)
                        dve.wait_ge(off_f_done[par], i + 1)
                        dve.wait_ge(y_ready[par], i + 1)
                        dve.tensor_tensor(off_f[:, par], ps_y[par][:], off_f[:, par], ALU.add).then_inc(y_read[par], 1)
                        dve.wait_ge(y_read[par], i + 1)
                        dve.wait_ge(skip_done[par], i + 1)
                        dve.tensor_tensor(off_f[:, par], off_f[:, par], skip[:, par], ALU.add).then_inc(y_sum[par], 1)
                        dve.wait_ge(y_sum[par], i + 1)
                        dve.wait_ge(z_loaded[par], 16 * (i + 1))
                        if not isinstance(c, int) or c > 1:
                            dve.wait_ge(t_ready, c - 1)
                        dve.tensor_tensor(g_t[:, par], off_f[:, par], z_t[:, par], ALU.mult).then_inc(gated[par], 1)

                    def norm(i, par):
                        dve.wait_ge(rstd_done[par], i + 1)
                        for g in range(GROUPS):
                            c = slice(g * GW, (g + 1) * GW)
                            dve.tensor_scalar(g_t[:, par, c], g_t[:, par, c], rstd[:, par, g:g + 1], None, ALU.mult) \
                               .then_inc(normed[par], 1)

                    def out_turned(i, par):
                        dve.wait_ge(t_ready, chunk(i, par) + 1)
                        dve.wait_ge(g_stored[par], 16 * i)
                        dve.tensor_tensor(gT[:, par], ps_t[:], gain[:].unsqueeze(2).broadcast_to([P, KX, P]), ALU.mult) \
                           .then_inc(t_out, 1)

                    def step(now, after, before):
                        if after:
                            table(*after)
                        if before:
                            norm(*before)
                        if after:
                            mix(*after, 0)
                            mix(*after, 2)
                        outputs(*now)
                        if before:
                            out_turned(*before)

                    table(0, 0)
                    mix(0, 0, 0)
                    mix(0, 0, 2)
                    steps(dve, step)
                    norm(PAIRS - 1, 1)
                    out_turned(PAIRS - 1, 1)

                @block.gpsimd
                def _(pool):
                    def weigh_x(i, par):
                        c = chunk(i, par)
                        pool.wait_ge(tab_done, c + 1)
                        pool.wait_ge(y_ready[par], i)
                        pool.tensor_tensor(heads(xdt[:, par, 1]), heads(flat2(x_tok[:, bass.ds(c, 1)])),
                                           by_head(tab_c[:, par, DT + HEADS:DT + H2]), ALU.mult).then_inc(xdt_b_done, 1)

                    def mix(i, par, q):
                        pool.wait_ge(e_done[q], chunk(i, par) + 1)
                        pool.wait_ge(cb_out[par], i + 1)
                        pool.tensor_tensor(decay[:, par, q], decay[:, par, q],
                                           cb[:, par, q // 2].unsqueeze(1).broadcast_to([P, GH, P]), ALU.mult) \
                            .then_inc(m_done[q], 1)

                    def step(now, after, before):
                        i, par = now
                        c = chunk(i, par)
                        pool.wait_ge(hf_done, c)
                        pool.tensor_tensor(heads(h_cut[:, par]), heads(h_f[:, par]), by_head(tab_c[:, par, CD:CD + HEADS]),
                                           ALU.mult).then_inc(cutf_done[par], 1)
                        pool.wait_ge(const_loaded, 16 * 6)
                        pool.wait_ge(y_sum[par], i)
                        pool.tensor_tensor(heads(skip[:, par]), heads(flat2(x_tok[:, bass.ds(c, 1)])),
                                           by_head(rows[:, 2, 0:HEADS]), ALU.mult).then_inc(skip_x[par], 1)
                        if after:
                            weigh_x(*after)
                            mix(*after, 1)
                            mix(*after, 3)
                        pool.wait_ge(skip_x[par], i + 1)
                        pool.wait_ge(off_read, c + 1)
                        pool.tensor_tensor(skip[:, par], skip[:, par], off_b[:, par], ALU.add).then_inc(skip_done[par], 1)

                    weigh_x(0, 0)
                    mix(0, 0, 1)
                    mix(0, 0, 3)
                    steps(pool, step)

                @block.scalar
                def _(act):
                    def decays(i, par):
                        c = chunk(i, par)
                        act.wait_ge(cb_ready, c + 1)
                        act.wait_ge(y_ready[par], i)
                        act.copy(cb[:, par], ps_cb[:, 0:GROUPS]).then_inc(cb_out[par], 1)
                        for q in range(4):
                            d, g = q % 2, q // 2
                            act.wait_ge(r_ready[q], c + 1)
                            for h in range(GH):
                                at = NB + d * HEADS + g * GH + h
                                last = act.activation(decay[:, par, q, h], ps_r[q % 2][:, h], ACT.Exp,
                                                      bias=tab_c[:, par, at:at + 1], scale=-1.0 if d else 1.0)
                            last.then_inc(e_done[q], 1)

                    def group_rstd(i, par):
                        act.wait_ge(gated[par], i + 1)
                        for g in range(GROUPS):
                            act.activation(junk[:, par, g], g_t[:, par, g * GW:(g + 1) * GW], ACT.Square,
                                           accum_out=ss[:, par, g:g + 1]).then_inc(sq_done[par], 1)
                        act.wait_ge(sq_done[par], 2 * i + 2)
                        act.activation(ss_ln[:, par], ss[:, par], ACT.Ln, scale=1.0 / GW, bias=eps[:]).then_inc(ln_done[par], 1)
                        act.wait_ge(ln_done[par], i + 1)
                        act.activation(rstd[:, par], ss_ln[:, par], ACT.Exp, scale=-0.5).then_inc(rstd_done[par], 1)

                    def step(now, after, before):
                        if before:
                            group_rstd(*before)
                        if after:
                            decays(*after)

                    decays(0, 0)
                    steps(act, step)
                    group_rstd(PAIRS - 1, 1)

                @block.tensor
                def _(pe):
                    def products(i, par):
                        c = chunk(i, par)
                        pe.wait_ge(bc_loaded[par], 16 * (i + 1))
                        pe.wait_ge(cb_out[1 - par], i + par)
                        for g in range(GROUPS):
                            last = pe.matmul(ps_cb[:, g], bc[:, par, g], bc[:, par, KB + g], start=True, stop=True)
                        last.then_inc(cb_ready, 1)

                    def prefixes(i, par, q):
                        c, d, g = chunk(i, par), q % 2, q // 2
                        if q == 0:
                            pe.wait_ge(tab_done, c + 1)
                        pe.wait_ge(e_done[(q + 2) % 4], c + q // 2)
                        pe.matmul(ps_r[q % 2][:], ident_bf[:], masks[:, d].unsqueeze(1).broadcast_to([P, GH, P]),
                                  start=True, stop=False)
                        for h in range(GH):
                            at = A_ + d * HEADS + g * GH + h
                            last = pe.matmul(ps_r[q % 2][:, h], tab_c[:, par, at:at + 1].broadcast_to([P, P]), upper[:, d],
                                             start=False, stop=h == GH - 1)
                        last.then_inc(r_ready[q], 1)

                    def diagonal(i, par, g):
                        c = chunk(i, par)
                        if g == 0:
                            pe.wait_ge(xdt_f_done, c + 1)
                            pe.wait_ge(xdt_b_done, c + 1)
                            pe.wait_ge(y_read[par], i)
                        pe.wait_ge(m_done[2 * g], c + 1)
                        pe.wait_ge(m_done[2 * g + 1], c + 1)
                        for h in range(GH):
                            cols = slice((g * GH + h) * HEAD, (g * GH + h + 1) * HEAD)
                            pe.matmul(ps_y[par][:, cols], decay[:, par, 2 * g, h], xdt[:, par, 0, cols], start=True, stop=False)
                            last = pe.matmul(ps_y[par][:, cols], decay[:, par, 2 * g + 1, h], xdt[:, par, 1, cols],
                                             start=False, stop=True)
                        if g == GROUPS - 1:
                            last.then_inc(y_ready[par], 1)

                    def across(i, par):
                        c = chunk(i, par)
                        pe.wait_ge(hf_done, c)
                        pe.wait_ge(off_read, c)
                        for g in range(GROUPS):
                            cols = slice(g * GW, (g + 1) * GW)
                            pe.matmul(ps_off[0][:, cols], bc[:, par, KB + g], h_f[:, par, cols], start=True, stop=True)
                        for g in range(GROUPS):
                            cols = slice(g * GW, (g + 1) * GW)
                            last = pe.matmul(ps_off[1][:, cols], bc[:, par, KB + g],
                                             flat2(h_b[:, bass.ds(c + 1, 1), cols]), start=True, stop=True)
                        last.then_inc(off_ready[par], 1)

                    def turn(i, par):
                        c = chunk(i, par)
                        pe.wait_ge(normed[par], 2 * i + 2)
                        pe.wait_ge(t_out, c)
                        for k in range(KX):
                            last = pe.transpose(ps_t[:, k], g_t[:, par, k * P:(k + 1) * P], ident[:])
                        last.then_inc(t_ready, 1)

                    def step(now, after, before):
                        if after:
                            products(*after)
                            prefixes(*after, 0)
                            prefixes(*after, 1)
                        diagonal(*now, 0)
                        if after:
                            prefixes(*after, 2)
                        diagonal(*now, 1)
                        if after:
                            prefixes(*after, 3)
                        across(*now)
                        if before:
                            turn(*before)

                    products(0, 0)
                    for q in range(4):
                        prefixes(0, 0, q)
                    steps(pe, step)
                    turn(PAIRS - 1, 1)


def out_proj_phase(nc, mixT, w_out, x, norm_w, ident_dram, x1, h2T):
    PAIRS = T // P // 2
    BANKS = D_MODEL // TB

    with ExitStack() as ctx:
        def sb(name, shape, dt=F32):
            return ctx.enter_context(nc.sbuf_tensor("o_" + name, shape, dt))

        sem = ctx.enter_context(phase_semaphores(nc, "o_"))

        def two(name):
            return [sem(name + "0"), sem(name + "1")]

        ident = sb("ident", [P, P])
        gain = sb("gain", [P, KD])
        eps = sb("eps", [P, 1])
        w_raw = sb("w_raw", [P, KD, D_MODEL])
        w_hi = sb("w_hi", [P, KD, D_MODEL], F32R)
        w_lo = sb("w_lo", [P, KD, D_MODEL], F32R)
        mix = sb("mix", [P, 2, KD, P])
        mix_hi = sb("mix_hi", [P, 2, KD, P], F32R)
        mix_lo = sb("mix_lo", [P, 2, KD, P], F32R)
        x_t = sb("x_t", [P, 2, D_MODEL])
        x1_t = sb("x1_t", [P, 2, D_MODEL])
        junk = sb("junk", [P, 2, D_MODEL])
        xn = sb("xn", [P, 2, D_MODEL])
        h2 = sb("h2", [P, 2, KD, P])
        ss = sb("ss", [P, 2])
        ss_ln = sb("ss_ln", [P, 2])
        rstd = sb("rstd", [P, 2])

        acc = [ctx.enter_context(nc.psum_tensor(f"o_acc{i}", [P, BANKS, TB], F32)) for i in range(2)]
        ps_turn = [ctx.enter_context(nc.psum_tensor(f"o_ps_turn{i}", [P, KD, P], F32)) for i in range(2)]

        const_loaded = sem("const_loaded")
        eps_made = sem("eps_made")
        w_loaded = [sem(f"w_loaded{k}") for k in range(KD)]
        w_hi_done = sem("w_hi_done")
        w_lo_done = sem("w_lo_done")
        mix_loaded = two("mix_loaded")
        x_loaded = two("x_loaded")
        mix_hi_done = two("mix_hi_done")
        mix_lo_done = two("mix_lo_done")
        acc_ready = two("acc_ready")
        x1_made = two("x1_made")
        x1_stored = two("x1_stored")
        sq_done = two("sq_done")
        ln_done = two("ln_done")
        rstd_done = two("rstd_done")
        xn_done = two("xn_done")
        turned = two("turned")
        h2_made = two("h2_made")
        h2_stored = two("h2_stored")

        def steps(eng, step):
            def body(i, first, last):
                step((i, 0), (i, 1), None if first else (i - 1, 1))
                step((i, 1), None if last else (i + 1, 0), (i, 0))
            body(0, True, False)
            with eng.Fori(1, PAIRS - 1) as i:
                body(i, False, False)
            body(PAIRS - 1, False, True)

        def tokens(i, par):
            return bass.ds((2 * i + par) * P, P)

        block = ctx.enter_context(nc.Block())

        @block.sync
        def _(sp):
            w_src = w_out.rearrange("(k p) d -> p k d", p=P)
            mix_src = mixT.rearrange("(k p) t -> p k t", p=P)

            def load(i, par):
                sp.wait_ge(mix_lo_done[par], i)
                sp.dma_start(mix[:, par], mix_src[:, :, tokens(i, par)]).then_inc(mix_loaded[par], 16)
                sp.wait_ge(x1_made[par], BANKS * i)
                sp.dma_start(x_t[:, par], x[tokens(i, par), :]).then_inc(x_loaded[par], 16)

            sp.dma_start(w_raw[:, 0], w_src[:, 0]).then_inc(w_loaded[0], 16)
            load(0, 0)
            for k in range(1, KD):
                sp.dma_start(w_raw[:, k], w_src[:, k]).then_inc(w_loaded[k], 16)
            sp.dma_start(ident[:], ident_dram).then_inc(const_loaded, 16)
            sp.dma_start(gain[:], norm_w).then_inc(const_loaded, 16)
            load(0, 1)
            with sp.Fori(1, PAIRS) as i:
                load(i, 0)
                load(i, 1)

        @block.scalar
        def _(act):
            def split(i, par):
                act.wait_ge(mix_loaded[par], 16 * (i + 1))
                act.wait_ge(acc_ready[par], i)
                act.copy(mix_hi[:, par], mix[:, par]).then_inc(mix_hi_done[par], 1)

            def make_rstd(i, par):
                act.wait_ge(x1_made[par], BANKS * (i + 1))
                act.wait_ge(ln_done[par], i)
                act.activation(junk[:, par], x1_t[:, par], ACT.Square, accum_out=ss[:, par:par + 1]) \
                   .then_inc(sq_done[par], 1)
                act.wait_ge(sq_done[par], i + 1)
                act.activation(ss_ln[:, par:par + 1], ss[:, par:par + 1], ACT.Ln, scale=1.0 / D_MODEL, bias=eps[:]) \
                   .then_inc(ln_done[par], 1)
                act.wait_ge(ln_done[par], i + 1)
                act.wait_ge(xn_done[par], i)
                act.activation(rstd[:, par:par + 1], ss_ln[:, par:par + 1], ACT.Exp, scale=-0.5) \
                   .then_inc(rstd_done[par], 1)

            def step(now, after, before):
                if after:
                    split(*after)
                make_rstd(*now)

            act.wait_ge(eps_made, 1)
            split(0, 0)
            for k in range(KD):
                act.wait_ge(w_loaded[k], 16)
                act.copy(w_hi[:, k], w_raw[:, k]).then_inc(w_hi_done, 1)
            steps(act, step)

        @block.vector
        def _(dve):
            def split(i, par):
                dve.wait_ge(mix_hi_done[par], i + 1)
                dve.tensor_tensor(mix_lo[:, par], mix[:, par], mix_hi[:, par].bitcast(F32), ALU.subtract) \
                   .then_inc(mix_lo_done[par], 1)

            def add_x(i, par):
                dve.wait_ge(acc_ready[par], i + 1)
                dve.wait_ge(x_loaded[par], 16 * (i + 1))
                dve.wait_ge(x1_stored[par], 16 * i)
                for b in range(BANKS):
                    c = slice(b * TB, (b + 1) * TB)
                    dve.tensor_tensor(x1_t[:, par, c], acc[par][:, b], x_t[:, par, c], ALU.add).then_inc(x1_made[par], 1)

            def scale(i, par):
                dve.wait_ge(rstd_done[par], i + 1)
                dve.wait_ge(turned[par], i)
                dve.tensor_scalar(xn[:, par], x1_t[:, par], rstd[:, par:par + 1], None, ALU.mult) \
                   .then_inc(xn_done[par], 1)

            def out_turned(i, par):
                dve.wait_ge(turned[par], i + 1)
                dve.wait_ge(h2_stored[par], 16 * i)
                dve.tensor_tensor(h2[:, par], ps_turn[par][:], gain[:].unsqueeze(2).broadcast_to([P, KD, P]), ALU.mult) \
                   .then_inc(h2_made[par], 1)

            def step(now, after, before):
                if after:
                    split(*after)
                add_x(*now)
                if before:
                    out_turned(*before)
                scale(*now)

            dve.memset(eps[:], EPS).then_inc(eps_made, 1)
            split(0, 0)
            for k in range(KD):
                dve.wait_ge(w_hi_done, k + 1)
                dve.tensor_tensor(w_lo[:, k], w_raw[:, k], w_hi[:, k].bitcast(F32), ALU.subtract).then_inc(w_lo_done, 1)
            dve.wait_ge(const_loaded, 32)
            steps(dve, step)
            out_turned(PAIRS - 1, 1)

        @block.gpsimd
        def _(pool):
            h2_dst = h2T.rearrange("(k p) t -> p k t", p=P)

            def store_x1(i, par):
                pool.wait_ge(x1_made[par], BANKS * (i + 1))
                pool.dma_start(x1[tokens(i, par), :], x1_t[:, par]).then_inc(x1_stored[par], 16)

            def store_h2(i, par):
                pool.wait_ge(h2_made[par], i + 1)
                pool.dma_start(h2_dst[:, :, tokens(i, par)], h2[:, par]).then_inc(h2_stored[par], 16)

            def step(now, after, before):
                store_x1(*now)
                if before:
                    store_h2(*before)

            steps(pool, step)
            store_h2(PAIRS - 1, 1)
            for par in range(2):
                pool.wait_ge(x1_stored[par], 16 * PAIRS)
                pool.wait_ge(h2_stored[par], 16 * PAIRS)

        @block.tensor
        def _(pe):
            def products(i, par):
                pe.wait_ge(mix_lo_done[par], i + 1)
                pe.wait_ge(x1_made[par], BANKS * i)
                for k in range(KD):
                    if isinstance(i, int) and i == par == 0:
                        pe.wait_ge(w_lo_done, k + 1)
                    for b in range(BANKS):
                        c = slice(b * TB, (b + 1) * TB)
                        last = split_products(pe, acc[par][:, b], mix_hi[:, par, k], mix_lo[:, par, k],
                                              w_hi[:, k, c], w_lo[:, k, c], k == 0, k == KD - 1)
                last.then_inc(acc_ready[par], 1)

            def turn(i, par):
                pe.wait_ge(xn_done[par], i + 1)
                pe.wait_ge(h2_made[par], i)
                for k in range(KD):
                    last = pe.transpose(ps_turn[par][:, k], xn[:, par, k * P:(k + 1) * P], ident[:])
                last.then_inc(turned[par], 1)

            def step(now, after, before):
                products(*now)
                if before:
                    turn(*before)

            pe.wait_ge(const_loaded, 32)
            steps(pe, step)
            turn(PAIRS - 1, 1)


def ffn_phase(nc, h2T, x1, w_gate, w_up, w_down, ident_dram, y):
    HALF = KF // 2
    SLOT = 2 * KD
    PAIRS = KF // 2
    SLOTS2 = (KF + 2 * KD) // 2

    with ExitStack() as ctx:
        def sb(name, shape, dt=F32):
            return ctx.enter_context(nc.sbuf_tensor("f_" + name, shape, dt))

        sem = ctx.enter_context(phase_semaphores(nc, "f_"))

        def two(name):
            return [sem(name + "0"), sem(name + "1")]

        ident = sb("ident", [P, P])
        raw = sb("raw", [P, 2, SLOT, P])
        w_hi = sb("w_hi", [P, 2, SLOT, P], F32R)
        w_lo = sb("w_lo", [P, 2, SLOT, P], F32R)
        h_raw = sb("h_raw", [P, KD, TB])
        h_hi = sb("h_hi", [P, KD, TB], F32R)
        h_lo = sb("h_lo", [P, KD, TB], F32R)
        g_silu = sb("g_silu", [P, 2, TB])
        hid = sb("hid", [P, 2, TB])
        hid_hi = sb("hid_hi", [P, KF, TB], F32R)
        hid_lo = sb("hid_lo", [P, KF, TB], F32R)
        yT = sb("yT", [P, 2, TB])
        x1_t = sb("x1_t", [P, 2, TT, P])
        y_t = sb("y_t", [P, 2, TT, P])

        ps_gate = ctx.enter_context(nc.psum_tensor("f_ps_gate", [P, 2, TB], F32))
        ps_up = ctx.enter_context(nc.psum_tensor("f_ps_up", [P, 2, TB], F32))
        ps_down = ctx.enter_context(nc.psum_tensor("f_ps_down", [P, 2, TB], F32))
        ps_turn = ctx.enter_context(nc.psum_tensor("f_ps_turn", [P, TT, P], F32))

        id_loaded = sem("id_loaded")
        h_loaded = sem("h_loaded")
        h_hi_done = sem("h_hi_done")
        h_lo_done = sem("h_lo_done")
        slot_loaded = two("slot_loaded")
        slot_hi_done = two("slot_hi_done")
        slot_lo_done = two("slot_lo_done")
        slot_done = two("slot_done")
        gate_ready = two("gate_ready")
        silu_done = two("silu_done")
        prod_done = two("prod_done")
        hid_hi_done = two("hid_hi_done")
        hid_lo_done = two("hid_lo_done")
        yT_done = two("yT_done")
        turned = two("turned")
        x1_loaded = two("x1_loaded")
        y_added = two("y_added")
        y_stored = two("y_stored")

        def blocks(eng, body):
            with eng.Fori(0, NTB - 1) as tb:
                body(tb, True)
            body(NTB - 1, False)

        def down_slots(tb, d):
            return tb * SLOTS2 + PAIRS + d + 1

        block = ctx.enter_context(nc.Block())

        @block.sync
        def _(sp):
            sp.dma_start(ident[:], ident_dram).then_inc(id_loaded, 16)
            h_src = h2T.rearrange("(k p) t -> p k t", p=P)
            wg_src = w_gate.rearrange("(k p) f -> p k f", p=P)
            wu_src = w_up.rearrange("(k p) f -> p k f", p=P)
            wd_src = w_down.rearrange("(f p) d -> p f d", p=P)
            x1_src = x1.rearrange("(t p) d -> p t d", p=P)
            y_dst = y.rearrange("(t p) d -> p t d", p=P)

            def load_h(tb):
                sp.wait_ge(h_lo_done, KD * tb)
                sp.dma_start(h_raw[:], h_src[:, :, bass.ds(tb * TB, TB)]).then_inc(h_loaded, 16)

            def load_down(tb, d, par, q):
                for half in range(2):
                    sp.wait_ge(slot_lo_done[half], tb * SLOTS2 + PAIRS + d)
                    for a, b in ((0, HALF // 2), (HALF // 2, HALF)):
                        sp.dma_start(raw[:, half, a:b],
                                     wd_src[:, HALF * half + a:HALF * half + b, bass.ds(d * P, P)]) \
                          .then_inc(slot_loaded[half], 16)
                sp.wait_ge(y_added[par], q)
                sp.dma_start(x1_t[:, par], x1_src[:, bass.ds(tb * TT, TT), bass.ds(d * P, P)]) \
                  .then_inc(x1_loaded[par], 16)

            def store_y(tb, d, par, q):
                sp.wait_ge(y_added[par], q + 1)
                sp.dma_start(y_dst[:, bass.ds(tb * TT, TT), bass.ds(d * P, P)], y_t[:, par]) \
                  .then_inc(y_stored[par], 16)

            def token_block(tb, more):
                with sp.Fori(0, PAIRS) as i:
                    for par in range(2):
                        sp.wait_ge(slot_lo_done[par], tb * SLOTS2 + i)
                        cols = bass.ds((2 * i + par) * P, P)
                        sp.dma_start(raw[:, par, 0:KD], wg_src[:, :, cols]).then_inc(slot_loaded[par], 16)
                        sp.dma_start(raw[:, par, KD:SLOT], wu_src[:, :, cols]).then_inc(slot_loaded[par], 16)
                if more:
                    load_h(tb + 1)
                q = tb * (KD // 2)
                load_down(tb, 0, 0, q)
                load_down(tb, 1, 1, q)
                with sp.Fori(0, KD // 2 - 1) as i:
                    for par in range(2):
                        load_down(tb, 2 * i + 2 + par, par, q + i + 1)
                        store_y(tb, 2 * i + par, par, q + i)
                store_y(tb, KD - 2, 0, q + KD // 2 - 1)
                store_y(tb, KD - 1, 1, q + KD // 2 - 1)

            load_h(0)
            blocks(sp, token_block)
            for par in range(2):
                sp.wait_ge(y_stored[par], 16 * NTB * KD // 2)

        @block.scalar
        def _(act):
            def split_slot(n, par, size):
                act.wait_ge(slot_loaded[par], 32 * (n + 1))
                act.wait_ge(slot_done[par], n)
                act.copy(w_hi[:, par, 0:size], raw[:, par, 0:size]).then_inc(slot_hi_done[par], 1)

            def split_h(tb, k, behind):
                act.wait_ge(h_loaded, 16 * (tb + 1))
                act.wait_ge(slot_done[1], behind)
                act.copy(h_hi[:, k], h_raw[:, k]).then_inc(h_hi_done, 1)

            def silu(tb, i, par):
                g = tb * PAIRS + i
                act.wait_ge(gate_ready[par], g + 1)
                act.wait_ge(prod_done[par], g)
                act.activation(g_silu[:, par], ps_gate[:, par], ACT.Silu).then_inc(silu_done[par], 1)

            def out_tile(tb, d, par, q, more):
                if more:
                    split_h(tb + 1, d, tb * SLOTS2 + PAIRS)
                act.wait_ge(slot_done[1], down_slots(tb, d))
                act.wait_ge(turned[par], q)
                act.copy(yT[:, par], ps_down[:, par]).then_inc(yT_done[par], 1)

            def token_block(tb, more):
                n = tb * SLOTS2
                split_slot(n, 0, SLOT)
                with act.Fori(0, PAIRS - 1) as i:
                    split_slot(n + i, 1, SLOT)
                    silu(tb, i, 0)
                    split_slot(n + i + 1, 0, SLOT)
                    silu(tb, i, 1)
                split_slot(n + PAIRS - 1, 1, SLOT)
                silu(tb, PAIRS - 1, 0)
                n = tb * SLOTS2 + PAIRS
                split_slot(n, 0, HALF)
                silu(tb, PAIRS - 1, 1)
                split_slot(n, 1, HALF)
                q = tb * (KD // 2)
                with act.Fori(0, KD // 2 - 1) as i:
                    for par in range(2):
                        split_slot(n + 2 * i + par + 1, 0, HALF)
                        out_tile(tb, 2 * i + par, par, q + i, more)
                        split_slot(n + 2 * i + par + 1, 1, HALF)
                split_slot(n + KD - 1, 0, HALF)
                out_tile(tb, KD - 2, 0, q + KD // 2 - 1, more)
                split_slot(n + KD - 1, 1, HALF)
                out_tile(tb, KD - 1, 1, q + KD // 2 - 1, more)

            for k in range(KD):
                split_h(0, k, 0)
            blocks(act, token_block)

        @block.vector
        def _(dve):
            def split_slot(n, par, size):
                dve.wait_ge(slot_hi_done[par], n + 1)
                dve.tensor_tensor(w_lo[:, par, 0:size], raw[:, par, 0:size], w_hi[:, par, 0:size].bitcast(F32),
                                  ALU.subtract).then_inc(slot_lo_done[par], 1)

            def split_h(tb, k):
                dve.wait_ge(h_hi_done, KD * tb + k + 1)
                dve.tensor_tensor(h_lo[:, k], h_raw[:, k], h_hi[:, k].bitcast(F32), ALU.subtract) \
                   .then_inc(h_lo_done, 1)

            def product(tb, i, par):
                g = tb * PAIRS + i
                dve.wait_ge(silu_done[par], g + 1)
                dve.wait_ge(slot_done[par], tb * SLOTS2 + i + 1)
                dve.wait_ge(hid_lo_done[par], g)
                dve.tensor_tensor(hid[:, par], g_silu[:, par], ps_up[:, par], ALU.mult) \
                   .then_inc(prod_done[par], 1)

            def out_tile(tb, d, par, q, more):
                if more:
                    split_h(tb + 1, d)
                dve.wait_ge(turned[par], q + 1)
                dve.wait_ge(x1_loaded[par], 16 * (q + 1))
                dve.wait_ge(y_stored[par], 16 * q)
                dve.tensor_tensor(y_t[:, par], ps_turn[:], x1_t[:, par], ALU.add).then_inc(y_added[par], 1)

            def token_block(tb, more):
                n = tb * SLOTS2
                split_slot(n, 0, SLOT)
                with dve.Fori(0, PAIRS - 1) as i:
                    split_slot(n + i, 1, SLOT)
                    product(tb, i, 0)
                    split_slot(n + i + 1, 0, SLOT)
                    product(tb, i, 1)
                split_slot(n + PAIRS - 1, 1, SLOT)
                product(tb, PAIRS - 1, 0)
                n = tb * SLOTS2 + PAIRS
                split_slot(n, 0, HALF)
                product(tb, PAIRS - 1, 1)
                split_slot(n, 1, HALF)
                q = tb * (KD // 2)
                split_slot(n + 1, 0, HALF)
                with dve.Fori(0, KD // 2 - 1) as i:
                    split_slot(n + 2 * i + 1, 1, HALF)
                    split_slot(n + 2 * i + 2, 0, HALF)
                    out_tile(tb, 2 * i, 0, q + i, more)
                    split_slot(n + 2 * i + 2, 1, HALF)
                    split_slot(n + 2 * i + 3, 0, HALF)
                    out_tile(tb, 2 * i + 1, 1, q + i, more)
                split_slot(n + KD - 1, 1, HALF)
                out_tile(tb, KD - 2, 0, q + KD // 2 - 1, more)
                out_tile(tb, KD - 1, 1, q + KD // 2 - 1, more)

            for k in range(KD):
                split_h(0, k)
            blocks(dve, token_block)

        @block.gpsimd
        def _(pool):
            with pool.Fori(0, NTB) as tb:
                with pool.Fori(0, PAIRS) as i:
                    for par in range(2):
                        g = tb * PAIRS + i
                        f = bass.ds(2 * i + par, 1)
                        pool.wait_ge(slot_done[1], tb * SLOTS2)
                        pool.wait_ge(prod_done[par], g + 1)
                        pool.tensor_copy(hid_hi[:, f], hid[:, par:par + 1]).then_inc(hid_hi_done[par], 1)
                        pool.wait_ge(hid_hi_done[par], g + 1)
                        pool.tensor_tensor(hid_lo[:, f], hid[:, par:par + 1], hid_hi[:, f].bitcast(F32),
                                           ALU.subtract).then_inc(hid_lo_done[par], 1)

        @block.tensor
        def _(pe):
            def down_half(tb, d, par, q, half):
                pe.wait_ge(slot_lo_done[half], down_slots(tb, d))
                if half == 0:
                    pe.wait_ge(yT_done[par], q)
                for j in range(HALF):
                    f = HALF * half + j
                    last = split_products(pe, ps_down[:, par], w_hi[:, half, j], w_lo[:, half, j],
                                          hid_hi[:, f], hid_lo[:, f], f == 0, f == KF - 1)
                last.then_inc(slot_done[half], 1)

            def turn(par, q, behind):
                pe.wait_ge(yT_done[par], q + 1)
                pe.wait_ge(y_added[1 - par], behind)
                for t in range(TT):
                    last = pe.transpose(ps_turn[:, t], yT[:, par, t * P:(t + 1) * P], ident[:])
                last.then_inc(turned[par], 1)

            def token_block(tb, more):
                pe.wait_ge(id_loaded, 16)
                with pe.Fori(0, PAIRS) as i:
                    for par in range(2):
                        pe.wait_ge(h_lo_done, KD * (tb + 1))
                        pe.wait_ge(slot_lo_done[par], tb * SLOTS2 + i + 1)
                        pe.wait_ge(prod_done[par], tb * PAIRS + i)
                        for k in range(KD):
                            last = split_products(pe, ps_gate[:, par], w_hi[:, par, k], w_lo[:, par, k],
                                                  h_hi[:, k], h_lo[:, k], k == 0, k == KD - 1)
                        last.then_inc(gate_ready[par], 1)
                        for k in range(KD):
                            last = split_products(pe, ps_up[:, par], w_hi[:, par, KD + k], w_lo[:, par, KD + k],
                                                  h_hi[:, k], h_lo[:, k], k == 0, k == KD - 1)
                        last.then_inc(slot_done[par], 1)
                pe.wait_ge(hid_lo_done[0], PAIRS * (tb + 1))
                pe.wait_ge(hid_lo_done[1], PAIRS * (tb + 1))
                q = tb * (KD // 2)
                down_half(tb, 0, 0, q, 0)
                down_half(tb, 0, 0, q, 1)
                with pe.Fori(0, KD // 2 - 1) as i:
                    down_half(tb, 2 * i + 1, 1, q + i, 0)
                    turn(0, q + i, q + i)
                    down_half(tb, 2 * i + 1, 1, q + i, 1)
                    down_half(tb, 2 * i + 2, 0, q + i + 1, 0)
                    turn(1, q + i, q + i + 1)
                    down_half(tb, 2 * i + 2, 0, q + i + 1, 1)
                end = q + KD // 2 - 1
                down_half(tb, KD - 1, 1, end, 0)
                turn(0, end, end)
                down_half(tb, KD - 1, 1, end, 1)
                turn(1, end, end + 1)

            blocks(pe, token_block)


def build(nc, x, w_in, rpb, w_out, w_gate, w_up, w_down, cols, qk_rows, head_rows, ssm_gain, norm2, ident, ident_bf,
          tri, tri_masks, masks, y):
    def scratch(name, shape):
        return nc.dram_tensor(name, shape, F32, kind="Internal").ap()

    q_s, k_s, v_s, z_s = (scratch(n, (T, D_ATT)) for n in ("q_s", "k_s", "v_s", "z_s"))
    dtT = scratch("dtT", (2 * HEADS, T))
    xbcT = scratch("xbcT", (CONV_CH, T + 4 * (D_CONV // 2)))
    xcT = scratch("xcT", (CONV_CH, T))
    mixT = scratch("mixT", (D_ATT + D_SSM, T))
    copies = scratch("bias_copies", (16 * PITCH,))
    x1 = scratch("x1", (T, D_MODEL))
    h2T = scratch("h2T", (D_MODEL, T))
    in_proj_phase(nc, x, w_in, cols, qk_rows, ident, q_s, k_s, v_s, z_s, dtT, xbcT, xcT)
    attention_phase(nc, q_s, k_s, v_s, rpb, copies, masks, ident, mixT)
    ssd_phase(nc, xcT, dtT, z_s, head_rows, ssm_gain, tri, tri_masks, ident, ident_bf, mixT)
    out_proj_phase(nc, mixT, w_out, x, norm2, ident, x1, h2T)
    ffn_phase(nc, h2T, x1, w_gate, w_up, w_down, ident, y)


def by_partition(np, a, n):
    return np.moveaxis(a.reshape(a.shape[:-1] + (n, P)), (-1, -2), (0, 1))


def triangles(np):
    r = np.arange(P)
    ones = np.stack([r[:, None] <= r, r[:, None] < r, np.ones((P, P), bool)], axis=1).astype(np.float32)
    below = np.where(r[:, None] > r, -2.0 ** 100, 0.0)
    above = np.where(r[:, None] < r, 2.0 ** 100, 0.0)
    return ones, np.stack([below, above], axis=1).astype(mybir.dt.np(BF16))


def neighbourhoods(np):
    token = np.arange(T)
    row, col = token // GRID_W, token % GRID_W
    rows = SEQ // GRID_W
    first_row = np.where(row < rows, np.clip(row - WIN_ROWS // 2, 0, rows - WIN_ROWS), rows)
    first_col = np.clip(col - WIN_COLS // 2, 0, GRID_W - WIN_COLS)
    m = np.zeros((48, 2, T), np.float32)
    for r in range(32):
        m[r, 0] = np.where((r - first_col) % 32 < WIN_COLS, 0.0, -2.0 ** 100)
        m[r, 1] = col % 32 == r
    for r in range(16):
        m[32 + r, 0] = np.where((r - first_row) % 16 < WIN_ROWS, 0.0, -2.0 ** 100)
        m[32 + r, 1] = row % 16 == r
    m[:, 0] = m[:, 0].reshape(48, T // TB, 8, 4, 16).transpose(0, 1, 3, 2, 4).reshape(48, T)
    return m


def kernel(**inputs):
    import numpy as np
    import concourse.bacc as bacc
    from concourse.bass_utils import run_bass_kernel_spmd

    a = {name: np.asarray(value) for name, value in inputs.items()}
    weights = {name: value[0] for name, value in a.items() if not name.startswith("x_")}
    x = np.concatenate([a["x_prompt"][0], a["x_sample"][0]])

    cols = np.zeros((P, KD, 8), np.float32)
    cols[:, :, 0] = by_partition(np, weights["norm1_w"], KD)
    cols[:, :, 1] = by_partition(np, weights["conv_b"], KD)
    cols[:, :, 2:2 + D_CONV] = by_partition(np, weights["conv_w"], KD)
    qk = np.stack([weights["q_norm_w"], weights["k_norm_w"]])
    heads = np.stack([np.concatenate([weights["dt_bias_f"], weights["dt_bias_b"]]),
                      np.concatenate([weights["A_log_f"], weights["A_log_b"]]),
                      np.concatenate([weights["D_skip"], weights["D_skip"]])])
    ones, tri_masks = triangles(np)
    arrays = dict(
        x=x, w_in=weights["w_in"],
        rpb=np.pad(weights["rpb"], ((0, 0), (4, 4), (16, 16))).reshape(-1),
        w_out=weights["w_out"], w_gate=weights["w_gate"], w_up=weights["w_up"], w_down=weights["w_down"],
        cols=cols, qk_rows=np.broadcast_to(qk, (P,) + qk.shape), head_rows=np.broadcast_to(heads, (P,) + heads.shape),
        ssm_gain=by_partition(np, weights["ssm_norm_w"], D_SSM // P), norm2=by_partition(np, weights["norm2_w"], KD),
        ident=np.eye(P, dtype=np.float32), ident_bf=np.eye(P).astype(mybir.dt.np(BF16)),
        tri=ones, tri_masks=tri_masks, masks=neighbourhoods(np))
    arrays = {name + "_dram": np.ascontiguousarray(value) for name, value in arrays.items()}

    nc = bacc.Bacc("TRN2", target_bir_lowering=False, num_devices=1)
    args = [nc.dram_tensor(name, value.shape, mybir.dt.from_np(value.dtype), kind="ExternalInput").ap()
            for name, value in arrays.items()]
    y = nc.dram_tensor("y_dram", (T, D_MODEL), F32, kind="ExternalOutput").ap()
    build(nc, *args, y)
    result = run_bass_kernel_spmd(nc, [arrays], core_ids=[0]).results[0]["y_dram"]
    return result[None, :SEQ], result[None, SEQ:]
```

```python
from contextlib import ExitStack, contextmanager

import concourse.bass as bass
from concourse import mybir

ALU = mybir.AluOpType
ACT = mybir.ActivationFunctionType
AX_X = mybir.AxisListType.X
F32 = mybir.dt.float32
F32R = mybir.dt.float32r
BF16 = mybir.dt.bfloat16

P = 128
D_MODEL = 1024
D_FF = 2816
TB = 512
SEQ, DEC_SEQ = 2048, 512
T = SEQ + DEC_SEQ
NTB = T // TB
KD = D_MODEL // P
KF = D_FF // P
TT = TB // P
HEADS = 8
HEAD = 64
D_ATT = HEADS * HEAD
D_SSM = HEADS * HEAD
GROUPS = 2
D_STATE = 128
D_CONV = 5
CONV_CH = D_SSM + 2 * GROUPS * D_STATE
D_IN_PROJ = 3 * D_ATT + D_SSM + CONV_CH + 2 * HEADS
EPS = 1e-6
GRID_W = 64
WIN_ROWS, WIN_COLS = 8, 16
PR, PC = 4 + 2 * WIN_ROWS - 1 + 4, 16 + 2 * WIN_COLS - 1 + 16
PITCH = HEADS * PR * PC + PC
BIAS_SKEW = 15
LOG_EXP = "natural_log_exp_and_others"
LOWEST = -3.0e38


@contextmanager
def phase_semaphores(nc, prefix):
    held = []

    def sem(name):
        held.append(nc.alloc_semaphore(prefix + name))
        return held[-1]

    yield sem
    nc.clear_and_free_semaphores(held)
    nc.all_engine_barrier()


def split_products(pe, out, w_hi, w_lo, x_hi, x_lo, first, last):
    pe.matmul(out, w_hi, x_hi, start=first, stop=False)
    pe.matmul(out, w_hi, x_lo, start=False, stop=False)
    return pe.matmul(out, w_lo, x_hi, start=False, stop=last)


def in_proj_phase(nc, x, w_in, cols, qk_w, bias_pad, copies, ident_dram, q_s, k_s, v_s, z_s, dtT, xbcT, xcT):
    SLOTS = 12
    USES = 6
    USE = {4: 2, 6: 3, 8: 4, 10: 5}
    COL = {4: 3 * D_ATT, 6: 2 * D_ATT, 8: 0, 10: D_ATT}
    XBC0 = 3 * D_ATT + D_SSM
    LAST = D_IN_PROJ - P
    KH = KD // 2
    KX = CONV_CH // P
    HALO = D_CONV // 2
    CB = 4
    LAST_CONVS = (3, 3, 2, 2, 3, 1, 2, 0)

    with ExitStack() as ctx:
        def sb(name, shape, dt=F32):
            return ctx.enter_context(nc.sbuf_tensor("i_" + name, shape, dt))

        sem = ctx.enter_context(phase_semaphores(nc, "i_"))

        def some(name, n):
            return [sem(f"{name}{i}") for i in range(n)]

        ident = sb("ident", [P, P])
        par_cols = sb("cols", [P, KD, 8])
        qk_rows = sb("qk_rows", [P, 2, HEAD])
        q_gain = sb("q_gain", [P, HEAD])
        eps = sb("eps", [P, 1])
        raw = sb("raw", [P, 2, 2 * KD * P])
        w_hi = sb("w_hi", [P, 2, 2 * KD * P], F32R)
        w_lo = sb("w_lo", [P, 2, 2 * KD * P], F32R)
        dt_raw = sb("dt_raw", [P, KD, P])
        dt_hi = sb("dt_hi", [P, KD, P], F32R)
        dt_lo = sb("dt_lo", [P, KD, P], F32R)
        x_t = sb("x_t", [P, TT, D_MODEL])
        junk = sb("junk", [P, D_MODEL])
        x_ss = sb("x_ss", [P, TT])
        x_ln = sb("x_ln", [P, TT])
        x_rstd = sb("x_rstd", [P, TT])
        h_f = sb("h_f", [P, KD, TB])
        h_hi = sb("h_hi", [P, KD, TB], F32R)
        h_lo = sb("h_lo", [P, KD, TB], F32R)
        ev = sb("ev", [P, TT, TB])
        dt_ev = sb("dt_ev", [P, TB])
        sq = sb("sq", [P, TT, TB])
        ss = sb("ss", [P, TT, HEADS])
        ss_ln = sb("ss_ln", [P, TT, HEADS])
        rstd = sb("rstd", [P, TT, HEADS])
        cx = sb("cx", [P, CB, TB + 2 * HALO])
        cy = sb("cy", [P, CB, TB])
        co = sb("co", [P, CB, TB])

        acc = ctx.enter_context(nc.psum_tensor("i_acc", [P, TT, TB], F32))
        ps_turn = ctx.enter_context(nc.psum_tensor("i_ps_turn", [P, KD, P], F32))
        ps_dt = ctx.enter_context(nc.psum_tensor("i_ps_dt", [P, TB], F32))

        zero = sb("zero", [P, CONV_CH // P, 2 * HALO])

        const_loaded = sem("const_loaded")
        dt_loaded = sem("dt_loaded")
        zero_made = sem("zero_made")
        bias_copied = sem("bias_copied")
        halo_stored = sem("halo_stored")
        xbc_seen = sem("xbc_seen")
        consts_made = sem("consts_made")
        dt_hi_done = sem("dt_hi_done")
        dt_lo_done = sem("dt_lo_done")
        slot_loaded = some("slot_loaded", 2)
        slot_hi_done = some("slot_hi_done", 2)
        slot_lo_done = some("slot_lo_done", 2)
        half_done = sem("half_done")
        acc_ready = some("acc_ready", TT)
        ev_ready = some("ev_ready", TT)
        ev_stored = some("ev_stored", TT)
        dt_ready = sem("dt_ready")
        dt_ev_ready = sem("dt_ev_ready")
        dt_stored = sem("dt_stored")
        sq_done = some("sq_done", TT)
        ss_done = some("ss_done", TT)
        ln_done = some("ln_done", TT)
        rstd_done = some("rstd_done", TT)
        q_scaled = some("q_scaled", TT)
        x_loaded = some("x_loaded", TT)
        first_ln_done = sem("first_ln_done")
        first_rstd_done = sem("first_rstd_done")
        x_sq_done = sem("x_sq_done")
        x_ln_done = sem("x_ln_done")
        x_rstd_done = sem("x_rstd_done")
        xn_done = sem("xn_done")
        h_turned = sem("h_turned")
        h_f_done = sem("h_f_done")
        h_hi_done = sem("h_hi_done")
        h_lo_done = sem("h_lo_done")
        cx_loaded = some("cx_loaded", CB)
        tap0_done = some("tap0_done", CB)
        taps_done = some("taps_done", CB)
        tap_step = some("tap_step", CB)
        co_ready = some("co_ready", CB)
        co_stored = some("co_stored", CB)

        def wait_slot_used(eng, tb, s):
            if s % 2 == 0 and s not in (2, 4):
                eng.wait_ge(half_done, tb * 4 + (s - 4) // 2 if s >= 6 else tb * 4)
            elif s in (2, 4):
                eng.wait_ge(acc_ready[1], tb * USES + s // 2)
            else:
                eng.wait_ge(acc_ready[3], tb * USES + s // 2)

        def blocks(eng, body):
            body(0, True, False)
            with eng.Fori(1, NTB - 1) as tb:
                body(tb, True, True)
            body(NTB - 1, False, True)

        def turn_bank(tb, u):
            if isinstance(tb, int) and tb == 0 and u % 2:
                return acc[:, 0:2].rearrange("p b (k c) -> p (b k) c", c=P)
            return ps_turn[:]

        def convs(tb, s, conv):
            if isinstance(tb, int) and tb == NTB - 1:
                both = [(tb - 1, j) for j in range(KX)] + [(tb, j) for j in range(KX)]
                behind = [sum(LAST_CONVS[:max(0, n - 4)]) for n in (s, s + 1)]
                return both[behind[0]:behind[1]]
            return [(tb - 1, 2 * (s - 4) + i) for i in range(2)] if conv and 4 <= s < 8 else []

        def xbc_col(tb):
            return tb * TB + HALO + (2 * HALO if isinstance(tb, int) and tb == NTB - 1 else 0)

        block = ctx.enter_context(nc.Block())

        @block.sync
        def _(sp):
            w_src = w_in.rearrange("(k p) c -> p k c", p=P)
            x_src = x.rearrange("(t p) d -> p t d", p=P)

            def load_x(tb, u):
                if u == 0:
                    sp.wait_ge(h_turned, TT * tb)
                sp.dma_start(x_t[:, u:u + 1], x_src[:, bass.ds(tb * TT + u, 1), :]).then_inc(x_loaded[u], 16)

            def load_slot(tb, s):
                par, n = s % 2, tb * (SLOTS // 2) + s // 2
                sp.wait_ge(slot_lo_done[par], n)
                s = s % SLOTS
                if s < 4:
                    dst = raw[:, par].rearrange("p (k c) -> p k c", k=KD)
                    src = w_src[:, :, XBC0 + 2 * P * s:XBC0 + 2 * P * (s + 1)]
                else:
                    c0, k0 = COL[s - s % 2], KH * (s % 2)
                    dst = raw[:, par].rearrange("p (k c) -> p k c", k=KH)
                    src = w_src[:, k0:k0 + KH, c0:c0 + TB]
                sp.dma_start(dst, src).then_inc(slot_loaded[par], 16)

            def load_conv(tb, j):
                b, n = j % CB, tb * (KX // CB) + j // CB
                sp.wait_ge(taps_done[b], n)
                if j == 0:
                    sp.sem_inc(xbc_seen, 1)
                    if not isinstance(tb, int) or tb < NTB - 1:
                        for u in range(TT):
                            sp.wait_ge(ev_stored[u], 16 * ((tb + 1) * USES + 2))
                    sp.wait_ge(halo_stored, 16 * 3)
                    sp.sem_inc(xbc_seen, 1)
                sp.dma_start(cx[:, b], xbcT[j * P:(j + 1) * P, bass.ds(xbc_col(tb) - HALO, TB + 2 * HALO)]) \
                  .then_inc(cx_loaded[b], 16)

            load_x(0, 0)
            sp.dma_start(ident[:], ident_dram).then_inc(const_loaded, 16)
            sp.dma_start(par_cols[:], cols).then_inc(const_loaded, 16)
            for u in range(1, TT):
                load_x(0, u)
            load_slot(0, 0)
            load_slot(0, 1)
            sp.dma_start(qk_rows[:], qk_w).then_inc(dt_loaded, 16)
            sp.dma_start(dt_raw[:], w_src[:, :, LAST:LAST + P]).then_inc(dt_loaded, 16)

            def store_rows(tb, s, dst):
                for u in range(TT):
                    sp.wait_ge(ev_ready[u], tb * USES + USE[s - 1] + 1)
                    sp.dma_start(dst[bass.ds(tb * TB + u * P, P), :], ev[:, u]).then_inc(ev_stored[u], 16)

            def store_conv(tb, j):
                b, n = j % CB, tb * (KX // CB) + j // CB
                sp.wait_ge(co_ready[b], n + 1)
                sp.dma_start(xcT[j * P:(j + 1) * P, bass.ds(tb * TB, TB)], co[:, b]).then_inc(co_stored[b], 16)

            def store(tb, s, conv):
                if s < 4:
                    for ft in (2 * s, 2 * s + 1):
                        u, w = ft % 4, tb * USES + ft // 4
                        sp.wait_ge(ev_ready[u], w + 1)
                        sp.dma_start(xbcT[ft * P:(ft + 1) * P, bass.ds(xbc_col(tb), TB)], ev[:, u]) \
                          .then_inc(ev_stored[u], 16)
                if s == 3:
                    sp.wait_ge(dt_loaded, 32)
                    sp.wait_ge(dt_ev_ready, tb + 1)
                    sp.dma_start(dtT[:, bass.ds(tb * TB, TB)], dt_ev[P - 2 * HEADS:P]).then_inc(dt_stored, 16)
                if s % 2 and s > 4:
                    store_rows(tb, s, {5: z_s, 7: v_s, 9: q_s, 11: k_s}[s])

            def token_block(tb, more, conv):
                for s in range(SLOTS):
                    if s + 2 < SLOTS or more:
                        load_slot(tb, s + 2)
                    if s > 0:
                        store(tb, s - 1, conv)
                    elif conv:
                        store(tb - 1, SLOTS - 1, True)
                    if s == 2 and more:
                        for u in range(TT):
                            load_x(tb + 1, u)
                    for tile in (convs(tb, s, conv) if s == 4 else []) + (convs(tb, s + 1, conv) if s >= 4 else []):
                        load_conv(*tile)
                    if s > 0:
                        for tile in convs(tb, s - 1, conv):
                            store_conv(*tile)

            blocks(sp, token_block)
            store(NTB - 1, SLOTS - 1, True)
            for u in range(TT):
                sp.wait_ge(ev_stored[u], 16 * NTB * USES)
            sp.wait_ge(dt_stored, 16 * NTB)
            for b in range(CB):
                sp.wait_ge(co_stored[b], 16 * NTB * KX // CB)

        @block.scalar
        def _(act):
            def split_slot(tb, s):
                par, n = s % 2, tb * (SLOTS // 2) + s // 2
                act.wait_ge(slot_loaded[par], 16 * (n + 1))
                if s >= SLOTS:
                    wait_slot_used(act, tb + 1, s - SLOTS)
                else:
                    wait_slot_used(act, tb, s)
                act.copy(w_hi[:, par], raw[:, par]).then_inc(slot_hi_done[par], 1)

            def x_squares(tb, u):
                act.wait_ge(x_loaded[u], 16 * (tb + 1))
                act.wait_ge(x_sq_done, TT * tb + u)
                act.activation(junk[:], x_t[:, u], ACT.Square, accum_out=x_ss[:, u:u + 1]).then_inc(x_sq_done, 1)

            def make_rstd(tb):
                act.preload_act_table_set(LOG_EXP)
                act.wait_ge(x_sq_done, TT * (tb + 1))
                act.activation(x_ln[:], x_ss[:], ACT.Ln, scale=1.0 / D_MODEL, bias=eps[:]).then_inc(x_ln_done, 1)
                act.wait_ge(x_ln_done, tb)
                act.wait_ge(xn_done, TT * tb)
                act.activation(x_rstd[:], x_ln[:], ACT.Exp, scale=-0.5).then_inc(x_rstd_done, 1)

            def first_rstd(u):
                col = slice(u, u + 1)
                act.wait_ge(x_loaded[u], 16)
                act.wait_ge(x_sq_done, u)
                act.activation(junk[:], x_t[:, u], ACT.Square, accum_out=x_ss[:, col]).then_inc(x_sq_done, 1)
                act.wait_ge(x_sq_done, u + 1)
                act.activation(x_ln[:, col], x_ss[:, col], ACT.Ln, scale=1.0 / D_MODEL, bias=eps[:]) \
                   .then_inc(first_ln_done, 1)
                act.wait_ge(first_ln_done, u + 1)
                act.activation(x_rstd[:, col], x_ln[:, col], ACT.Exp, scale=-0.5).then_inc(first_rstd_done, 1)

            def h_high(tb, u):
                tok = slice(u * P, (u + 1) * P)
                act.wait_ge(h_f_done, TT * tb + u + 1)
                act.copy(h_hi[:, :, tok], h_f[:, :, tok]).then_inc(h_hi_done, 1)

            def tap0(tb, j):
                b, n = j % CB, tb * (KX // CB) + j // CB
                act.wait_ge(cx_loaded[b], 16 * (n + 1))
                act.wait_ge(co_ready[b], n)
                act.activation(cy[:, b], cx[:, b, 0:TB], ACT.Identity, scale=par_cols[:, j, 2:3],
                               bias=par_cols[:, j, 1:2]).then_inc(tap0_done[b], 1)

            def conv_silu(tb, j):
                b, n = j % CB, tb * (KX // CB) + j // CB
                act.wait_ge(taps_done[b], n + 1)
                act.wait_ge(co_stored[b], 16 * n)
                act.activation(co[:, b], cy[:, b], ACT.Silu).then_inc(co_ready[b], 1)

            def squares(tb, s, u):
                w = tb * USES + USE[s - 1]
                m = tb * 2 + (s - 9) // 2
                act.wait_ge(acc_ready[u], w + 1)
                act.wait_ge(ss_done[u], m)
                act.activation(sq[:, u], acc[:, u], ACT.Square).then_inc(sq_done[u], 1)

            def head_rstd(tb, s, u):
                m = tb * 2 + (s - 9) // 2
                act.wait_ge(ss_done[u], m + 1)
                act.activation(ss_ln[:, u], ss[:, u], ACT.Ln, scale=1.0 / HEAD, bias=eps[:]).then_inc(ln_done[u], 1)
                act.wait_ge(ln_done[u], m + 1)
                act.activation(rstd[:, u], ss_ln[:, u], ACT.Exp, scale=-0.5).then_inc(rstd_done[u], 1)

            def token_block(tb, more, conv):
                for s in range(SLOTS):
                    if s + 1 < SLOTS or more:
                        split_slot(tb, s + 1)
                    if s < 4:
                        for ft in (2 * s, 2 * s + 1):
                            u, w = ft % 4, tb * USES + ft // 4
                            act.wait_ge(acc_ready[u], w + 1)
                            act.wait_ge(ev_stored[u], 16 * w)
                            act.copy(ev[:, u], acc[:, u]).then_inc(ev_ready[u], 1)
                    if s == 3:
                        act.wait_ge(dt_ready, tb + 1)
                        act.wait_ge(dt_stored, 16 * tb)
                        act.copy(dt_ev[96:P], ps_dt[96:P]).then_inc(dt_ev_ready, 1)
                    if s > 0:
                        for tile in convs(tb, s - 1, conv):
                            conv_silu(*tile)
                    for tile in convs(tb, s, conv):
                        tap0(*tile)
                    if s == 5:
                        for u in range(TT):
                            w = tb * USES + USE[4]
                            act.wait_ge(acc_ready[u], w + 1)
                            act.wait_ge(ev_stored[u], 16 * w)
                            act.activation(ev[:, u], acc[:, u], ACT.Silu).then_inc(ev_ready[u], 1)
                    if 4 <= s < 8 and more:
                        x_squares(tb + 1, s - 4)
                    if s == 8 and more:
                        make_rstd(tb + 1)
                    if s == 9 or s == 11:
                        if not more:
                            act.preload_act_table_set(LOG_EXP)
                        squares(tb, s, 0)
                        for u in range(TT):
                            if s == 11 and more:
                                act.wait_ge(acc_ready[u], (tb + 1) * USES)
                                h_high(tb + 1, u)
                            if u + 1 < TT and not (s == 11 and u + 2 == TT):
                                squares(tb, s, u + 1)
                            if s == 11 and u + 1 == TT:
                                squares(tb, s, u)
                                head_rstd(tb, s, u - 1)
                            if not (s == 11 and u + 2 == TT):
                                head_rstd(tb, s, u)

            act.preload_act_table_set(LOG_EXP)
            act.wait_ge(consts_made, 1)
            for u in range(TT - 1):
                first_rstd(u)
            h_high(0, 0)
            first_rstd(TT - 1)
            h_high(0, 1)
            split_slot(0, 0)
            h_high(0, 2)
            h_high(0, 3)
            act.wait_ge(dt_loaded, 32)
            act.copy(dt_hi[:], dt_raw[:]).then_inc(dt_hi_done, 1)
            blocks(act, token_block)

        @block.vector
        def _(dve):
            def split_slot(tb, s):
                par, n = s % 2, tb * (SLOTS // 2) + s // 2
                dve.wait_ge(slot_hi_done[par], n + 1)
                dve.tensor_tensor(w_lo[:, par], raw[:, par], w_hi[:, par].bitcast(F32), ALU.subtract) \
                   .then_inc(slot_lo_done[par], 1)

            def scale_x(tb, u):
                if isinstance(tb, int) and tb == 0:
                    dve.wait_ge(first_rstd_done, u + 1)
                elif u == 0:
                    dve.wait_ge(x_rstd_done, tb)
                dve.tensor_scalar(x_t[:, u], x_t[:, u], x_rstd[:, u:u + 1], None, ALU.mult).then_inc(xn_done, 1)

            def gain_h(tb, u):
                dve.wait_ge(h_turned, TT * tb + u + 1)
                dve.wait_ge(h_lo_done, TT * tb)
                dve.tensor_tensor(h_f[:, :, u * P:(u + 1) * P], turn_bank(tb, u),
                                  par_cols[:, :, 0:1].broadcast_to([P, KD, P]), ALU.mult).then_inc(h_f_done, 1)

            def h_low(tb, u):
                tok = slice(u * P, (u + 1) * P)
                dve.wait_ge(h_hi_done, TT * tb + u + 1)
                dve.tensor_tensor(h_lo[:, :, tok], h_f[:, :, tok], h_hi[:, :, tok].bitcast(F32), ALU.subtract) \
                   .then_inc(h_lo_done, 1)

            def taps(tiles):
                for t in range(1, D_CONV):
                    for tb, j in tiles:
                        b, n = j % CB, tb * (KX // CB) + j // CB
                        if t == 1:
                            dve.wait_ge(tap0_done[b], n + 1)
                        else:
                            dve.wait_ge(tap_step[b], n * (D_CONV - 2) + t - 1)
                        dve.scalar_tensor_tensor(cy[:, b], cx[:, b, t:t + TB], par_cols[:, j, 2 + t:3 + t], cy[:, b],
                                                 ALU.mult, ALU.add) \
                           .then_inc(taps_done[b] if t == D_CONV - 1 else tap_step[b], 1)

            def head_sums(tb, s, u):
                m = tb * 2 + (s - 9) // 2
                dve.wait_ge(sq_done[u], m + 1)
                dve.wait_ge(ln_done[u], m)
                dve.tensor_reduce(ss[:, u], sq[:, u].rearrange("p (h d) -> p h d", h=HEADS), AX_X, ALU.add) \
                   .then_inc(ss_done[u], 1)

            def head_scale(tb, s, u):
                w = tb * USES + USE[s - 1]
                m = tb * 2 + (s - 9) // 2
                dve.wait_ge(rstd_done[u], m + 1)
                dve.wait_ge(ev_stored[u], 16 * w)
                done = q_scaled[u] if s == 9 else ev_ready[u]
                dve.tensor_tensor(ev[:, u].rearrange("p (h d) -> p h d", h=HEADS),
                                  acc[:, u].rearrange("p (h d) -> p h d", h=HEADS),
                                  rstd[:, u].unsqueeze(2).broadcast_to([P, HEADS, HEAD]), ALU.mult) \
                   .then_inc(done, 1)

            def token_block(tb, more, conv):
                for s in range(SLOTS):
                    if s + 1 < SLOTS or more:
                        split_slot(tb, s + 1)
                    taps(convs(tb, s, conv))
                    if s == 7:
                        for u in range(TT):
                            w = tb * USES + USE[6]
                            dve.wait_ge(acc_ready[u], w + 1)
                            dve.wait_ge(ev_stored[u], 16 * w)
                            dve.tensor_copy(ev[:, u], acc[:, u]).then_inc(ev_ready[u], 1)
                    if s == 8 and more:
                        for u in range(TT):
                            scale_x(tb + 1, u)
                    if s in (9, 10, 11) and more:
                        gain_h(tb + 1, s - 9)
                    if s in (9, 11):
                        head_sums(tb, s, 0)
                        for u in range(TT):
                            if u + 1 == TT and s == 11 and more:
                                h_low(tb + 1, u)
                            if u + 1 < TT and not (s == 11 and u + 2 == TT):
                                head_sums(tb, s, u + 1)
                            if u == 0 and s == 11 and more:
                                gain_h(tb + 1, 3)
                            if s == 11 and u + 1 == TT:
                                head_sums(tb, s, u)
                                head_scale(tb, s, u - 1)
                            if not (s == 11 and u + 2 == TT):
                                head_scale(tb, s, u)

            dve.memset(eps[:], EPS).then_inc(consts_made, 1)
            scale_x(0, 0)
            scale_x(0, 1)
            dve.wait_ge(const_loaded, 32)
            gain_h(0, 0)
            scale_x(0, 2)
            gain_h(0, 1)
            scale_x(0, 3)
            h_low(0, 1)
            gain_h(0, 2)
            gain_h(0, 3)
            split_slot(0, 0)
            h_low(0, 3)
            dve.wait_ge(dt_loaded, 32)
            dve.scalar_tensor_tensor(q_gain[:], qk_rows[:, 0], HEAD ** -0.5, qk_rows[:, 1], ALU.mult, ALU.mult) \
               .then_inc(consts_made, 1)
            dve.wait_ge(dt_hi_done, 1)
            dve.tensor_tensor(dt_lo[:], dt_raw[:], dt_hi[:].bitcast(F32), ALU.subtract).then_inc(dt_lo_done, 1)
            blocks(dve, token_block)

        @block.gpsimd
        def _(pool):
            def h_low(tb, u):
                tok = slice(u * P, (u + 1) * P)
                pool.wait_ge(h_hi_done, TT * tb + u + 1)
                pool.tensor_tensor(h_lo[:, :, tok], h_f[:, :, tok], h_hi[:, :, tok].bitcast(F32), ALU.subtract) \
                    .then_inc(h_lo_done, 1)

            def token_block(tb, more, conv):
                for u in range(TT):
                    pool.wait_ge(q_scaled[u], tb + 1)
                    view = ev[:, u].rearrange("p (h d) -> p h d", h=HEADS)
                    pool.tensor_tensor(view, view, q_gain[:].unsqueeze(1).broadcast_to([P, HEADS, HEAD]), ALU.mult) \
                        .then_inc(ev_ready[u], 1)
                if more:
                    for u in range(TT - 1):
                        h_low(tb + 1, u)

            pool.memset(zero[:], 0.0).then_inc(zero_made, 1)
            pool.wait_ge(zero_made, 1)
            halo = xbcT.rearrange("(k p) t -> p k t", p=P)
            for c, n in ((0, HALO), (SEQ + HALO, 2 * HALO), (T + 3 * HALO, HALO)):
                pool.dma_start(halo[:, :, c:c + n], zero[:, :, 0:n]).then_inc(halo_stored, 16)
            h_low(0, 0)
            h_low(0, 2)
            for j in range(16):
                pool.dma_start(copies[j * PITCH:j * PITCH + HEADS * PR * PC], bias_pad).then_inc(bias_copied, 16)
            pool.wait_ge(consts_made, 2)
            blocks(pool, token_block)
            pool.wait_ge(bias_copied, 16 * 16)

        @block.tensor
        def _(pe):
            def turn(tb, u):
                pe.wait_ge(xn_done, TT * tb + u + 1)
                if not isinstance(tb, int) or tb > 0:
                    pe.wait_ge(h_f_done, TT * tb + u)
                elif u > 1:
                    pe.wait_ge(h_f_done, u - 1)
                for k in range(KD):
                    last = pe.transpose(turn_bank(tb, u)[:, k], x_t[:, u, k * P:(k + 1) * P], ident[:])
                last.then_inc(h_turned, 1)

            def token_block(tb, more, conv):
                pe.wait_ge(h_lo_done, TT * (tb + 1))
                for s in range(SLOTS):
                    par = s % 2
                    pe.wait_ge(slot_lo_done[par], tb * (SLOTS // 2) + s // 2 + 1)
                    if s < 4:
                        hi = w_hi[:, par].rearrange("p (k c) -> p k c", k=KD)
                        lo = w_lo[:, par].rearrange("p (k c) -> p k c", k=KD)
                        for half in range(2):
                            ft = 2 * s + half
                            u, c = ft % 4, slice(half * P, (half + 1) * P)
                            pe.wait_ge(ev_ready[u], tb * USES + ft // 4)
                            for k in range(KD):
                                last = split_products(pe, acc[:, u], hi[:, k, c], lo[:, k, c], h_hi[:, k], h_lo[:, k],
                                                      k == 0, k == KD - 1)
                            last.then_inc(acc_ready[u], 1)
                    if s == 3:
                        pe.wait_ge(dt_lo_done, 1)
                        pe.wait_ge(dt_ev_ready, tb)
                        for k in range(KD):
                            last = split_products(pe, ps_dt[:], dt_hi[:, k], dt_lo[:, k], h_hi[:, k], h_lo[:, k],
                                                  k == 0, k == KD - 1)
                        last.then_inc(dt_ready, 1)
                    if s >= 4:
                        kh = s % 2
                        hi = w_hi[:, par].rearrange("p (k c) -> p k c", k=KH)
                        lo = w_lo[:, par].rearrange("p (k c) -> p k c", k=KH)
                        for u in range(TT):
                            tok = slice(u * P, (u + 1) * P)
                            if kh == 0:
                                pe.wait_ge(ev_ready[u], tb * USES + USE[s])
                            for k in range(KH):
                                last = split_products(pe, acc[:, u], h_hi[:, kh * KH + k, tok], h_lo[:, kh * KH + k, tok],
                                                      hi[:, k], lo[:, k], kh + k == 0, kh * KH + k == KD - 1)
                            if kh == 1:
                                last.then_inc(acc_ready[u], 1)
                            if s == 11 and u == 1 and more:
                                turn(tb + 1, 3)
                        if kh == 0:
                            last.then_inc(half_done, 1)
                    if s in (8, 9, 10) and more:
                        turn(tb + 1, s - 8)

            pe.wait_ge(const_loaded, 32)
            for u in range(TT):
                turn(0, u)
            blocks(pe, token_block)


def attention_phase(nc, q_s, k_s, v_s, copies, masks, ident_dram, mixT):
    NT = 20
    COLT = 4
    BANDS = NT // COLT
    NTOK = T // P
    FIRST = [0, 1, 3, 5, 8]
    COUNT = [3, 4, 4, 3, 2]
    BIAS_ROW = [4, 0, 0, 0, 4]
    COL = [0, 8, 24, 32]
    BIAS_COL = [16, 8, 8, 0]
    ROWS = T // GRID_W
    KG = ROWS // 4
    LAG_TURN, LAG_PV = 2, 3
    GROUP_AT = {0: 0, 4: 1, 8: 2, 11: 3, 14: 4}
    FIRST_GROUP_AT = {3 * g + 3: g for g in range(BANDS)}
    MASK0, MASKS = HEAD, 48
    BR, BC = 16, 48

    with ExitStack() as ctx:
        def sb(name, shape, dt=F32):
            return ctx.enter_context(nc.sbuf_tensor("a_" + name, shape, dt))

        sem = ctx.enter_context(phase_semaphores(nc, "a_"))

        def some(name, n):
            return [sem(f"{name}{i}") for i in range(n)]

        ident = sb("ident", [P, P])
        qa = [sb(f"qa{i}", [P, T], F32R) for i in range(2)]
        qb = [sb(f"qb{i}", [P, T], F32R) for i in range(2)]
        ka = [sb(f"ka{i}", [P, T], F32R) for i in range(2)]
        kb = [sb(f"kb{i}", [P, T], F32R) for i in range(2)]
        v = sb("v", [P, 2, COLT * KG, HEAD])
        q_raw = sb("q_raw", [P, 2, NTOK, HEAD])
        k_raw = sb("k_raw", [P, 2, NTOK, HEAD])
        q_st = sb("q_st", [P, 2, TT, 2, HEAD], F32R)
        k_st = sb("k_st", [P, 2, TT, 3, HEAD], F32R)
        bias = sb("bias", [P, 2, BR, BC])
        prob = sb("prob", [P, 4, TB])
        probT = sb("probT", [P, 2, TT, P])
        top = sb("top", [P, 4])
        neg_top = sb("neg_top", [P, 4])
        total = sb("total", [P, 4])
        inv = sb("inv", [P, 4])
        outT = sb("outT", [P, T])

        ps_s = [ctx.enter_context(nc.psum_tensor(f"a_ps_s{i}", [P, TB], F32)) for i in range(2)]
        ps_p = [ctx.enter_context(nc.psum_tensor(f"a_ps_p{i}", [P, TT, P], F32)) for i in range(2)]
        ps_q = ctx.enter_context(nc.psum_tensor("a_ps_q", [P, TT, P], F32))
        ps_ka = ctx.enter_context(nc.psum_tensor("a_ps_ka", [P, TT, P], F32))
        ps_kb = ctx.enter_context(nc.psum_tensor("a_ps_kb", [P, TT, P], F32))
        ps_o = ctx.enter_context(nc.psum_tensor("a_ps_o", [P, COLT, P], F32))

        const_loaded = sem("const_loaded")
        masks_set = some("masks_set", 2)
        qk_loaded = some("qk_loaded", 2)
        first_loaded = some("first_loaded", BANDS)
        v_loaded = some("v_loaded", 2)
        bias_loaded = some("bias_loaded", 2)
        hi_made = sem("hi_made")
        st_made = sem("st_made")
        st_step = sem("st_step")
        q_turned = sem("q_turned")
        k_turned = sem("k_turned")
        qa_out = sem("qa_out")
        qb_out = sem("qb_out")
        ka_out = sem("ka_out")
        kb_out = sem("kb_out")
        scored = sem("scored")
        score_seen = sem("score_seen")
        topped = sem("topped")
        biased = sem("biased")
        exped = sem("exped")
        inverted = sem("inverted")
        scaled = some("scaled", 2)
        p_turned = sem("p_turned")
        p_out = sem("p_out")
        weighed = sem("weighed")
        o_out = sem("o_out")
        o_stored = some("o_stored", BANDS)

        def wait(eng, s, n):
            if not isinstance(n, int) or n > 0:
                eng.wait_ge(s, n)

        def pairs(eng, body):
            body(0, True, False)
            with eng.Fori(1, HEADS // 2 - 1) as i:
                body(i, False, False)
            body(HEADS // 2 - 1, False, True)

        def st(head, g):
            return (head[1] + g) % 2

        def number(head):
            return 2 * head[0] + head[1]

        def following(head):
            return (head[0], 1) if head[1] == 0 else (head[0] + 1, 0)

        def behind(head, a, lag, first):
            if a >= lag:
                return head, a - lag
            if first and head[1] == 0:
                return None
            return ((head[0], 0) if head[1] == 1 else (head[0] - 1, 1)), a - lag + NT

        block = ctx.enter_context(nc.Block())

        @block.sync
        def _(sp):
            q_src = q_s.rearrange("(t p) d -> p t d", p=P)
            k_src = k_s.rearrange("(t p) d -> p t d", p=P)
            v_src = v_s.rearrange("(m r c) d -> r c m d", r=4, c=GRID_W)
            skewed = copies[BIAS_SKEW:BIAS_SKEW + 16 * (PITCH - 1)].rearrange("(j x) -> j x", j=16)

            def load_qk(head):
                d = bass.ds(number(head) * HEAD, HEAD)
                sp.dma_start(q_raw[:, head[1]], q_src[:, :, d]).then_inc(qk_loaded[head[1]], 16)
                sp.dma_start(k_raw[:, head[1]], k_src[:, :, d]).then_inc(qk_loaded[head[1]], 16)

            def load_bias(head):
                for i in range(8):
                    at = bass.ds(number(head) * (PR * PC) + (7 - i) * PC, BR * PC)
                    src = skewed[:, at].rearrange("j (r c) -> j r c", c=PC)[:, :, 0:BC]
                    sp.dma_start(bias[16 * i:16 * i + 16, head[1]], src).then_inc(bias_loaded[head[1]], 16)

            def load_v(head):
                d = bass.ds(number(head) * HEAD, HEAD)
                for c in range(COLT):
                    for r in range(4):
                        sp.dma_start(v[32 * r:32 * r + 32, head[1], c * KG:(c + 1) * KG],
                                     v_src[r, COL[c]:COL[c] + 32, :, d]).then_inc(v_loaded[head[1]], 16)

            for g in range(BANDS):
                t = slice(g * TT, (g + 1) * TT)
                sp.dma_start(q_raw[:, 0, t], q_src[:, t, 0:HEAD]).then_inc(first_loaded[g], 16)
                sp.dma_start(k_raw[:, 0, t], k_src[:, t, 0:HEAD]).then_inc(first_loaded[g], 16)
                if g == 0:
                    sp.dma_start(ident[:], ident_dram).then_inc(const_loaded, 16)
            load_bias((0, 0))
            load_v((0, 0))
            load_qk((0, 1))
            load_bias((0, 1))
            load_v((0, 1))
            with sp.Fori(0, HEADS // 2 - 1) as i:
                for par in range(2):
                    head = (i, par)
                    sp.wait_ge(st_made, BANDS * (number(head) + 1))
                    load_qk((i + 1, par))
                    sp.wait_ge(topped, NT * (number(head) + 1))
                    load_bias((i + 1, par))
                    sp.wait_ge(weighed, NT * (number(head) + 1))
                    load_v((i + 1, par))

        @block.gpsimd
        def _(pool):
            def split_low(head, g):
                n, par = BANDS * number(head) + g, head[1]
                tiles = slice(g * TT, (g + 1) * TT)
                b = st(head, g)
                pool.wait_ge(hi_made, 2 * n + 2)
                pool.tensor_tensor(q_st[:, b, :, 1], q_raw[:, par, tiles], q_st[:, b, :, 0].bitcast(F32), ALU.subtract) \
                    .then_inc(st_step, 1)
                pool.wait_ge(st_step, n + 1)
                pool.tensor_tensor(k_st[:, b, :, 2], k_raw[:, par, tiles], k_st[:, b, :, 0].bitcast(F32), ALU.subtract) \
                    .then_inc(st_made, 1)

            def scale(head, a):
                G, n = NT * number(head) + a, COUNT[a // COLT] * P
                pool.wait_ge(inverted, G + 1)
                pool.tensor_tensor(prob[:, a % 4, 0:n], prob[:, a % 4, 0:n],
                                   inv[:, a % 4:a % 4 + 1].broadcast_to([P, n]), ALU.mult).then_inc(scaled[1], 1)

            def pair(i, first, last):
                for par in range(2):
                    head = (i, par)
                    ahead = not (last and par == 1)
                    at = FIRST_GROUP_AT if first and par == 0 else GROUP_AT
                    for a in range(NT):
                        late = behind(head, a, 1, first)
                        if late and late[1] % 2 == 1:
                            scale(*late)
                        if ahead and a in at:
                            split_low(following(head), at[a])

            for g in range(BANDS):
                split_low((0, 0), g)
                if g in (1, 3):
                    i = g // 2
                    for side, which in ((qb[i], 0), (kb[i], 1)):
                        pool.dma_start(side[MASK0:MASK0 + MASKS], masks[:, which].bitcast(F32R)) \
                            .then_inc(masks_set[i], 16)
            pairs(pool, pair)
            scale((HEADS // 2 - 1, 1), NT - 1)
            for b in range(BANDS):
                pool.wait_ge(o_stored[b], 16 * HEADS // 2)

        @block.vector
        def _(dve):
            def out_q(head, g):
                n, cols = BANDS * number(head) + g, slice(g * TB, (g + 1) * TB)
                wait(dve, scored, NT * (number(head) - 1))
                dve.wait_ge(q_turned, n + 1)
                dve.tensor_copy(qa[head[1]][:, cols].rearrange("p (t i j) -> p t i j", t=COLT, i=8),
                                ps_q[:].rearrange("p t c -> p (t c)").rearrange("p (i t j) -> p t i j", i=8, t=COLT)) \
                   .then_inc(qa_out, 1)

            def out_k_low(head, g):
                n, cols = BANDS * number(head) + g, slice(g * TB, (g + 1) * TB)
                wait(dve, scored, NT * (number(head) - 1))
                dve.wait_ge(k_turned, n + 1)
                dve.tensor_copy(kb[head[1]][0:HEAD, cols], ps_kb[0:HEAD].rearrange("p t c -> p (t c)")) \
                   .then_inc(kb_out, 1)

            def add_bias(head, a):
                G, b, c = NT * number(head) + a, a // COLT, a % COLT
                rows = COUNT[b] * 4
                n = COUNT[b] * P
                if a == 0:
                    dve.wait_ge(bias_loaded[head[1]], 16 * 8 * (head[0] + 1))
                dve.wait_ge(scored, G + 1)
                wait(dve, p_turned, G - 3)
                dve.sem_inc(score_seen, 1)
                dve.tensor_tensor_reduce(
                    prob[:, a % 4, 0:n].rearrange("p (r c) -> p r c", c=32),
                    ps_s[a % 2][:, 0:n].rearrange("p (r c) -> p r c", c=32),
                    bias[:, head[1], BIAS_ROW[b]:BIAS_ROW[b] + rows, BIAS_COL[c]:BIAS_COL[c] + 32],
                    1.0, LOWEST, ALU.add, ALU.max, top[:, a % 4:a % 4 + 1]).then_inc(topped, 1)

            def negate(head, a):
                G = NT * number(head) + a
                dve.wait_ge(topped, G + 1)
                dve.tensor_scalar(neg_top[:, a % 4:a % 4 + 1], top[:, a % 4:a % 4 + 1], -1.0, None, ALU.mult) \
                   .then_inc(biased, 1)

            def invert(head, a):
                G = NT * number(head) + a
                dve.wait_ge(exped, G + 1)
                dve.reciprocal(inv[:, a % 4:a % 4 + 1], total[:, a % 4:a % 4 + 1]).then_inc(inverted, 1)

            def scale(head, a):
                G, n = NT * number(head) + a, COUNT[a // COLT] * P
                dve.wait_ge(inverted, G + 1)
                dve.tensor_scalar(prob[:, a % 4, 0:n], prob[:, a % 4, 0:n], inv[:, a % 4:a % 4 + 1], None, ALU.mult) \
                   .then_inc(scaled[0], 1)

            def out_band(head, b):
                lo = HEAD * head[1]
                dve.wait_ge(weighed, NT * number(head) + COLT * (b + 1))
                if head[1] == 0:
                    wait(dve, o_stored[b], 16 * head[0])
                dst = outT[lo:lo + HEAD, b * TB:(b + 1) * TB].rearrange("p (i t j) -> p t i j", i=8, t=COLT)
                src = ps_o[lo:lo + HEAD].rearrange("p t (i j) -> p t i j", i=8)
                dve.tensor_copy(dst, src).then_inc(o_out, 1)

            def pair(i, first, last):
                for par in range(2):
                    head = (i, par)
                    ahead = not (last and par == 1)
                    at = FIRST_GROUP_AT if first and par == 0 else GROUP_AT
                    for a in range(NT):
                        add_bias(head, a)
                        late = behind(head, a, 1, first)
                        if late:
                            invert(*late)
                        negate(head, a)
                        if late and late[1] % 2 == 0:
                            scale(*late)
                        if ahead and a - 3 in at:
                            out_q(following(head), at[a - 3])
                        if ahead and a - 4 in at:
                            out_k_low(following(head), at[a - 4])
                        late = behind(head, a, LAG_PV, first)
                        if late and late[1] % COLT == COLT - 1:
                            out_band(late[0], late[1] // COLT)

            for g in range(BANDS):
                out_q((0, 0), g)
                out_k_low((0, 0), g)
            pairs(dve, pair)
            end = (HEADS // 2 - 1, 1)
            invert(end, NT - 1)
            out_band(end, BANDS - 1)

        @block.scalar
        def _(act):
            def split_high(head, g):
                n, par = BANDS * number(head) + g, head[1]
                tiles = slice(g * TT, (g + 1) * TT)
                if isinstance(head[0], int) and head == (0, 0):
                    act.wait_ge(first_loaded[g], 32)
                elif g == 0:
                    act.wait_ge(qk_loaded[par], 32 * (head[0] + par))
                b = st(head, g)
                wait(act, k_turned, n - 1)
                act.copy(q_st[:, b, :, 0], q_raw[:, par, tiles]).then_inc(hi_made, 1)
                act.copy(k_st[:, b, :, 0:2], k_raw[:, par, tiles].unsqueeze(2).broadcast_to([P, TT, 2, HEAD])) \
                   .then_inc(hi_made, 1)

            def out_q_high(head, g):
                n, cols = BANDS * number(head) + g, slice(g * TB, (g + 1) * TB)
                act.wait_ge(qa_out, n + 1)
                act.copy(qb[head[1]][0:HEAD, cols], qa[head[1]][0:HEAD, cols].bitcast(F32)).then_inc(qb_out, 1)

            def out_k(head, g):
                n, cols = BANDS * number(head) + g, slice(g * TB, (g + 1) * TB)
                wait(act, scored, NT * (number(head) - 1))
                act.wait_ge(k_turned, n + 1)
                act.copy(ka[head[1]][:, cols], ps_ka[:].rearrange("p t c -> p (t c)")).then_inc(ka_out, 1)

            def exp(head, a):
                G, n = NT * number(head) + a, COUNT[a // COLT] * P
                act.wait_ge(biased, G + 1)
                wait(act, inverted, G - 3)
                act.activation(prob[:, a % 4, 0:n], prob[:, a % 4, 0:n], ACT.Exp, bias=neg_top[:, a % 4:a % 4 + 1],
                               accum_out=total[:, a % 4:a % 4 + 1]).then_inc(exped, 1)

            def out_p(head, a):
                G, n = NT * number(head) + a, COUNT[a // COLT]
                act.wait_ge(p_turned, G + 1)
                wait(act, weighed, G - 1)
                act.copy(probT[:, a % 2, 0:n], ps_p[a % 2][:, 0:n]).then_inc(p_out, 1)

            def store(head, b):
                act.wait_ge(o_out, BANDS * number(head) + b + 1)
                act.dma_start(mixT[bass.ds(head[0] * P, P), b * TB:(b + 1) * TB], outT[:, b * TB:(b + 1) * TB]) \
                   .then_inc(o_stored[b], 16)

            def pair(i, first, last):
                for par in range(2):
                    head = (i, par)
                    ahead = not (last and par == 1)
                    at = FIRST_GROUP_AT if first and par == 0 else GROUP_AT
                    for a in range(NT):
                        if ahead and a in at:
                            split_high(following(head), at[a])
                        late = behind(head, a, LAG_TURN, first)
                        if late:
                            out_p(*late)
                        exp(head, a)
                        if ahead and a - 4 in at:
                            out_q_high(following(head), at[a - 4])
                            out_k(following(head), at[a - 4])
                        late = behind(head, a, LAG_PV + 2, first)
                        if late and late[0][1] == 1 and late[1] % COLT == COLT - 1:
                            store(late[0], late[1] // COLT)

            split_high((0, 0), 0)
            split_high((0, 0), 1)
            for g in range(BANDS):
                out_k((0, 0), g)
                if g + 2 < BANDS:
                    split_high((0, 0), g + 2)
                out_q_high((0, 0), g)
            pairs(act, pair)
            end = (HEADS // 2 - 1, 1)
            for a in range(NT - LAG_TURN, NT):
                out_p(end, a)
            store(end, BANDS - 2)
            store(end, BANDS - 1)

        @block.tensor
        def _(pe):
            def turn_q(head, g):
                n = BANDS * number(head) + g
                pe.wait_ge(st_made, n + 1)
                wait(pe, qa_out, n)
                for t in range(TT):
                    last = pe.transpose(ps_q[:, t], q_st[:, st(head, g), t].rearrange("p s d -> p (s d)").bitcast(F32), ident[:])
                last.then_inc(q_turned, 1)

            def turn_k(head, g):
                n = BANDS * number(head) + g
                wait(pe, ka_out, n)
                wait(pe, kb_out, n)
                for t in range(TT):
                    pe.transpose(ps_ka[:, t], k_st[:, st(head, g), t, 0:2].rearrange("p s d -> p (s d)").bitcast(F32), ident[:])
                    last = pe.transpose(ps_kb[0:HEAD, t], k_st[:, st(head, g), t, 2].bitcast(F32), ident[:])
                last.then_inc(k_turned, 1)

            def scores(head, a):
                G, b, c, par = NT * number(head) + a, a // COLT, a % COLT, head[1]
                if a == 0:
                    pe.wait_ge(masks_set[par], 32)
                    for s in (qa_out, qb_out, ka_out, kb_out):
                        pe.wait_ge(s, BANDS * (number(head) + 1))
                wait(pe, topped, G - 1)
                rows = slice(4 * FIRST[b], 4 * (FIRST[b] + COUNT[b]))
                cols = slice(COL[c], COL[c] + 32)

                def queries(x, k):
                    return x[par][0:k, a * P:(a + 1) * P]

                def keys(x, k):
                    return x[par][0:k].rearrange("p (r c) -> p r c", c=GRID_W)[:, rows, cols]

                out = ps_s[a % 2][:, 0:COUNT[b] * P].rearrange("p (r c) -> p r c", c=32)
                pe.matmul(out, queries(qa, P), keys(ka, P), start=True, stop=False)
                pe.matmul(out, queries(qb, MASK0 + MASKS), keys(kb, MASK0 + MASKS), start=False, stop=True) \
                  .then_inc(scored, 1)

            def turn_p(head, a):
                G = NT * number(head) + a
                pe.wait_ge(scaled[a % 2], (NT // 2) * number(head) + a // 2 + 1)
                wait(pe, p_out, G - 1)
                for j in range(COUNT[a // COLT]):
                    last = pe.transpose(ps_p[a % 2][:, j], prob[:, a % 4, j * P:(j + 1) * P], ident[:])
                last.then_inc(p_turned, 1)

            def weigh(head, a):
                G, b, c, par = NT * number(head) + a, a // COLT, a % COLT, head[1]
                if a == 0:
                    pe.wait_ge(v_loaded[par], 16 * 16 * (head[0] + 1))
                if c == 0:
                    wait(pe, o_out, BANDS * number(head) + b)
                pe.wait_ge(p_out, G + 1)
                for j in range(COUNT[b]):
                    last = pe.matmul(ps_o[HEAD * par:HEAD * (par + 1), c], v[:, par, c * KG + FIRST[b] + j],
                                     probT[:, a % 2, j], start=j == 0, stop=j == COUNT[b] - 1)
                last.then_inc(weighed, 1)

            def pair(i, first, last):
                for par in range(2):
                    head = (i, par)
                    ahead = not (last and par == 1)
                    at = FIRST_GROUP_AT if first and par == 0 else GROUP_AT
                    for a in range(NT):
                        scores(head, a)
                        late = behind(head, a, LAG_PV, first)
                        if late:
                            weigh(*late)
                        late = behind(head, a, LAG_TURN, first)
                        if late:
                            turn_p(*late)
                        if ahead and a - 2 in at:
                            turn_q(following(head), at[a - 2])
                        if ahead and a - 3 in at:
                            turn_k(following(head), at[a - 3])

            pe.wait_ge(const_loaded, 16)
            for g in range(BANDS):
                turn_q((0, 0), g)
                turn_k((0, 0), g)
            pairs(pe, pair)
            end = (HEADS // 2 - 1, 1)
            weigh(end, NT - LAG_PV)
            for a in range(NT - LAG_TURN, NT):
                turn_p(end, a)
                weigh(end, a)


def ssd_phase(nc, xcT, dtT, z_s, head_rows, norm_cols, tri, tri_masks, ident_dram, ident_bf_dram, mixT):
    NCH = T // P
    PAIRS = NCH // 2
    LAST, FIRST = SEQ // P - 1, SEQ // P
    H2 = 2 * HEADS
    GH = HEADS // GROUPS
    GW = GH * HEAD
    A_, NB, E_, DT, CD, W_ = (H2 * i for i in range(6))
    KX, KB = D_SSM // P, GROUPS

    with ExitStack() as ctx:
        def sb(name, shape, dt=F32):
            return ctx.enter_context(nc.sbuf_tensor("s_" + name, shape, dt))

        sem = ctx.enter_context(phase_semaphores(nc, "s_"))

        def two(name):
            return [sem(name + "0"), sem(name + "1")]

        ident = sb("ident", [P, P])
        ident_bf = sb("ident_bf", [P, P], BF16)
        upper = sb("upper", [P, 3, P])
        masks = sb("masks", [P, 2, P], BF16)
        rows = sb("rows", [P, 3, H2])
        gain = sb("gain", [P, KX])
        eps = sb("eps", [P, 1])
        tab = sb("tab", [P, NCH, 6 * H2])
        x_tok = sb("x_tok", [P, NCH, D_SSM])
        s_f = sb("s_f", [P, NCH, D_SSM])
        h_b = sb("h_b", [P, NCH + 1, D_SSM])
        h_f = sb("h_f", [P, 2, D_SSM])

        def heads(x):
            return x.rearrange("p (h d) -> p h d", d=HEAD)

        def by_head(x, n=HEAD):
            return x.unsqueeze(2).broadcast_to([P, x.shape[1], n])

        const_loaded = sem("const_loaded")

        with ExitStack() as ctx1:
            def sb1(name, shape, dt=F32):
                return ctx1.enter_context(nc.sbuf_tensor("s1_" + name, shape, dt))

            def ps1(name, shape):
                return ctx1.enter_context(nc.psum_tensor("s1_" + name, shape, F32))

            dt_t = sb1("dt_t", [H2, T])
            neg_a = sb1("neg_a", [P, H2])
            tmp = [sb1(f"tmp{i}", [P, NCH, H2]) for i in range(6)]
            xc = sb1("xc", [P, 2, KX + KB, P])
            tab_c = sb1("tab_c", [P, 2, 2 * H2])
            b_tok = sb1("b_tok", [P, 2, KB * P])
            xw = sb1("xw", [P, 2, 2, D_SSM])
            h_cut = sb1("h_cut", [P, 2, D_SSM])
            ps_x = [ps1(f"ps_x{i}", [P, KX, P]) for i in range(2)]
            ps_b = [ps1(f"ps_b{i}", [P, 4, P]) for i in range(2)]
            ps_s = [[ps1(f"ps_s{i}{d}", [P, D_SSM]) for d in range(2)] for i in range(2)]

            dt_loaded = sem("dt_loaded")
            dt_turned = sem("dt_turned")
            chain = sem("chain")
            exps = sem("exps")
            table_a = sem("table_a")
            exponents = sem("exponents")
            tables_made = sem("tables_made")
            sums_ready = sem("sums_ready")
            xc_loaded = two("xc_loaded")
            x_turned = two("x_turned")
            x_out = two("x_out")
            b_out = two("b_out")
            tab_out = two("tab_out")
            xw_made = two("xw_made")
            s_ready = two("s_ready")
            s_out = two("s_out")
            cut_done = two("cut_done")
            h_done = two("h_done")

            def ahead(eng, early, late):
                early(0, 0, NCH - 1)
                with eng.Fori(0, PAIRS - 1) as i:
                    c = eng.snap(NCH - 1 - 2 * i)
                    early(i, 1, c - 1)
                    late(i, 0, c)
                    early(i + 1, 0, c - 2)
                    late(i, 1, c - 1)
                early(PAIRS - 1, 1, 0)
                late(PAIRS - 1, 0, 1)
                late(PAIRS - 1, 1, 0)

            def at(c):
                return bass.ds(c, 1)

            def flat(x):
                return x.rearrange("p o x -> p (o x)")

            def sums(b):
                return b[:].rearrange("p a c -> p (a c)")[:, 0:NCH * H2].rearrange("p (c h) -> p c h", h=H2)

            with nc.Block() as block:
                @block.sync
                def _(sp):
                    sp.dma_start(ident[:], ident_dram).then_inc(const_loaded, 16)
                    sp.dma_start(ident_bf[:], ident_bf_dram).then_inc(const_loaded, 16)
                    sp.dma_start(upper[:], tri).then_inc(const_loaded, 16)
                    sp.dma_start(masks[:], tri_masks).then_inc(const_loaded, 16)
                    sp.dma_start(rows[:], head_rows).then_inc(const_loaded, 16)
                    sp.dma_start(gain[:], norm_cols).then_inc(const_loaded, 16)
                    sp.dma_start(dt_t[:], dtT).then_inc(dt_loaded, 16)
                    src = xcT.rearrange("(k p) t -> p k t", p=P)
                    with sp.Fori(0, PAIRS) as i:
                        c = sp.snap(NCH - 1 - 2 * i)
                        for par in range(2):
                            sp.wait_ge(const_loaded, 16 * 6)
                            sp.wait_ge(x_turned[par], i)
                            sp.dma_start(xc[:, par], src[:, 0:KX + KB, bass.ds((c - par) * P, P)]) \
                              .then_inc(xc_loaded[par], 16)

                @block.vector
                def _(dve):
                    done = [0]

                    def link(ins):
                        done[0] += 1
                        ins.then_inc(chain, 1)
                        dve.wait_ge(chain, done[0])

                    u, na, s, z, p, v = (t[:] for t in tmp)

                    def cols(c, d=None):
                        a, b = (0, H2) if d is None else (d * HEADS, (d + 1) * HEADS)
                        return tab[:, :, c + a:c + b]

                    def half(x, d):
                        return x[:, :, d * HEADS:(d + 1) * HEADS]

                    def by_chunk(x):
                        return x.unsqueeze(1).broadcast_to([P, NCH, H2])

                    link(dve.memset(eps[:], EPS))
                    dve.wait_ge(const_loaded, 16 * 6)
                    dve.wait_ge(dt_turned, 1)
                    link(dve.tensor_tensor(u, sums(ps_x[0]), by_chunk(rows[:, 0]), ALU.add))
                    link(dve.scalar_tensor_tensor(na, u, -1.0, u, ALU.mult, ALU.min))
                    dve.wait_ge(exps, 2)
                    link(dve.tensor_scalar(s, na, 2.0, None, ALU.add))
                    link(dve.reciprocal(z, s))
                    link(dve.tensor_tensor(s, na, z, ALU.mult))
                    link(dve.tensor_tensor(z, s, s, ALU.mult))
                    link(dve.tensor_scalar(p, z, 1.0 / 17, None, ALU.mult))
                    for odd in (15, 13, 11, 9, 7, 5, 3):
                        link(dve.scalar_tensor_tensor(p, p, 1.0 / odd, z, ALU.add, ALU.mult))
                    link(dve.scalar_tensor_tensor(v, p, 1.0, s, ALU.add, ALU.mult))
                    link(dve.tensor_scalar(u, u, 0.0, None, ALU.max))
                    link(dve.scalar_tensor_tensor(cols(DT), v, 2.0, u, ALU.mult, ALU.add))
                    link(dve.tensor_scalar(neg_a[:], neg_a[:], -1.0, None, ALU.mult))
                    link(dve.tensor_tensor(cols(A_), cols(DT), by_chunk(neg_a[:]), ALU.mult))
                    dve.sem_inc(table_a, 1)
                    dve.wait_ge(sums_ready, 1)
                    pf, px, total = sums(ps_x[0]), sums(ps_x[1]), sums(ps_b[0])
                    link(dve.tensor_copy(v, total))
                    link(dve.tensor_scalar(cols(NB, 0), half(pf, 0), -1.0, None, ALU.mult))
                    link(dve.tensor_copy(cols(NB, 1), half(px, 1)))
                    link(dve.tensor_copy(half(u, 0), half(pf, 0)))
                    link(dve.tensor_tensor(half(u, 1), half(v, 1), half(px, 1), ALU.subtract))
                    link(dve.tensor_tensor(half(s, 0), half(v, 0), half(pf, 0), ALU.subtract))
                    link(dve.tensor_copy(half(s, 1), half(px, 1)))
                    dve.sem_inc(exponents, 1)
                    dve.wait_ge(exps, 5)
                    link(dve.tensor_tensor(cols(W_), s, cols(DT), ALU.mult))
                    for c in (CD, W_):
                        link(dve.memset(tab[:, LAST, c:c + HEADS], 0.0))
                        link(dve.memset(tab[:, FIRST, c + HEADS:c + H2], 0.0))
                    link(dve.memset(h_b[:, NCH], 0.0))
                    link(dve.memset(h_f[:, 0], 0.0))
                    dve.sem_inc(tables_made, 1)

                    def weigh_x(i, par, c):
                        dve.wait_ge(cut_done[par], i)
                        dve.tensor_copy(tab_c[:, par:par + 1], tab[:, at(c), CD:CD + 2 * H2]).then_inc(tab_out[par], 1)
                        dve.wait_ge(tab_out[par], i + 1)
                        dve.wait_ge(x_out[par], i + 1)
                        dve.wait_ge(s_ready[par], i)
                        for d in range(2):
                            dve.tensor_tensor(heads(xw[:, par, d]), heads(flat(x_tok[:, at(c)])),
                                              by_head(tab_c[:, par, H2 + d * HEADS:H2 + (d + 1) * HEADS]), ALU.mult) \
                               .then_inc(xw_made[par], 1)

                    def add_state(i, par, c):
                        dve.wait_ge(cut_done[par], i + 1)
                        dve.wait_ge(s_ready[par], i + 1)
                        dve.tensor_tensor(flat(h_b[:, at(c)]), h_cut[:, par], ps_s[par][1][:], ALU.add) \
                           .then_inc(h_done[par], 1)

                    ahead(dve, weigh_x, add_state)

                @block.scalar
                def _(act):
                    u, na, s, z, p, v = (t[:] for t in tmp)
                    act.preload_act_table_set(LOG_EXP)
                    act.wait_ge(const_loaded, 16 * 6)
                    act.activation(neg_a[:], rows[:, 1], ACT.Exp).then_inc(exps, 1)
                    act.wait_ge(chain, 3)
                    act.activation(na, na, ACT.Exp).then_inc(exps, 1)
                    act.wait_ge(exponents, 1)
                    act.activation(tab[:, :, E_:E_ + H2], u, ACT.Exp).then_inc(exps, 1)
                    act.activation(tab[:, :, CD:CD + H2], v, ACT.Exp).then_inc(exps, 1)
                    act.activation(s, s, ACT.Exp).then_inc(exps, 1)

                    def out_x(i, par, c):
                        act.wait_ge(x_turned[par], i + 1)
                        act.copy(flat(x_tok[:, at(c)]), ps_x[par][:].rearrange("p k c -> p (k c)")).then_inc(x_out[par], 1)
                        act.wait_ge(s_ready[par], i)
                        act.copy(b_tok[:, par], ps_b[par][:, 0:KB].rearrange("p k c -> p (k c)")).then_inc(b_out[par], 1)

                    def out_s(i, par, c):
                        act.wait_ge(s_ready[par], i + 1)
                        act.copy(flat(s_f[:, at(c)]), ps_s[par][0][:]).then_inc(s_out[par], 1)

                    ahead(act, out_x, out_s)

                @block.gpsimd
                def _(pool):
                    pool.wait_ge(tables_made, 1)
                    with pool.Fori(0, PAIRS) as i:
                        c = pool.snap(NCH - 1 - 2 * i)
                        for par in range(2):
                            pool.wait_ge(tab_out[par], i + 1)
                            pool.wait_ge(h_done[par], i)
                            pool.wait_ge(h_done[1 - par], i + par)
                            pool.tensor_tensor(heads(h_cut[:, par]), heads(flat(h_b[:, at(c - par + 1)])),
                                               by_head(tab_c[:, par, HEADS:H2]), ALU.mult).then_inc(cut_done[par], 1)

                @block.tensor
                def _(pe):
                    pe.wait_ge(const_loaded, 16 * 6)
                    pe.wait_ge(dt_loaded, 16)
                    for c in range(NCH):
                        last = pe.transpose(sums(ps_x[0])[:, c], dt_t[:, c * P:(c + 1) * P], ident[0:H2, 0:H2])
                    last.then_inc(dt_turned, 1)
                    pe.wait_ge(table_a, 1)
                    for b, which in ((ps_x[0], 0), (ps_x[1], 1), (ps_b[0], 2)):
                        last = pe.matmul(sums(b), upper[:, which], tab[:, :, A_:A_ + H2], start=True, stop=True)
                    last.then_inc(sums_ready, 1)
                    pe.wait_ge(tables_made, 1)

                    def turn(i, par, c):
                        pe.wait_ge(xc_loaded[par], 16 * (i + 1))
                        pe.wait_ge(x_out[par], i)
                        pe.wait_ge(b_out[par], i)
                        for k in range(KX):
                            pe.transpose(ps_x[par][:, k], xc[:, par, k], ident[:])
                        for k in range(KB):
                            last = pe.transpose(ps_b[par][:, k], xc[:, par, KX + k], ident[:])
                        last.then_inc(x_turned[par], 1)

                    def states(i, par, c):
                        pe.wait_ge(b_out[par], i + 1)
                        pe.wait_ge(xw_made[par], 2 * i + 2)
                        pe.wait_ge(s_out[par], i)
                        pe.wait_ge(h_done[par], i)
                        for d in range(2):
                            for g in range(GROUPS):
                                cols = slice(g * GW, (g + 1) * GW)
                                last = pe.matmul(ps_s[par][d][:, cols], b_tok[:, par, g * P:(g + 1) * P], xw[:, par, d, cols],
                                                 start=True, stop=True)
                        last.then_inc(s_ready[par], 1)

                    ahead(pe, turn, states)

        with ExitStack() as ctx2:
            def sb2(name, shape, dt=F32):
                return ctx2.enter_context(nc.sbuf_tensor("s2_" + name, shape, dt))

            def ps2(name, shape):
                return ctx2.enter_context(nc.psum_tensor("s2_" + name, shape, F32))

            NTAB = CD + HEADS
            bc = sb2("bc", [P, 2, 2 * KB, P])
            z_t = sb2("z_t", [P, 2, D_SSM])
            tab_c = sb2("tab_c", [P, 2, NTAB])
            cb = sb2("cb", [P, 2, GROUPS, P])
            decay = sb2("decay", [P, 2, 4, GH, P])
            xdt = sb2("xdt", [P, 2, 2, D_SSM])
            off_f = sb2("off_f", [P, 2, D_SSM])
            off_b = sb2("off_b", [P, 2, D_SSM])
            skip = sb2("skip", [P, 2, D_SSM])
            h_cut = sb2("h_cut", [P, 2, D_SSM])
            g_t = sb2("g_t", [P, 2, D_SSM])
            junk = sb2("junk", [P, 2, GROUPS, GW])
            ss = sb2("ss", [P, 2, GROUPS])
            ss_ln = sb2("ss_ln", [P, 2, GROUPS])
            rstd = sb2("rstd", [P, 2, GROUPS])
            gT = sb2("gT", [P, 2, KX, P])

            ps_cb = ps2("ps_cb", [P, 4, P])
            ps_r = [ps2(f"ps_r{i}", [P, GH, P]) for i in range(2)]
            ps_y = [ps2(f"ps_y{i}", [P, D_SSM]) for i in range(2)]
            ps_off = [ps2(f"ps_off{i}", [P, D_SSM]) for i in range(2)]
            ps_t = ps2("ps_t", [P, KX, P])

            def four(name):
                return [sem(f"{name}{i}") for i in range(4)]

            bc_loaded = two("bc_loaded")
            z_loaded = two("z_loaded")
            tab_done = sem("tab_done")
            cb_ready = sem("cb_ready")
            xdt_f_done = sem("xdt_f_done")
            xdt_b_done = sem("xdt_b_done")
            hf_done = sem("hf_done")
            off_read = sem("off_read")
            t_ready = sem("t_ready")
            t_out = sem("t_out")
            r_ready = four("r_ready")
            e_done = four("e_done")
            m_done = four("m_done")
            cb_out = two("cb_out")
            y_ready = two("y_ready")
            y_read = two("y_read")
            off_ready = two("off_ready")
            off_b_done = two("off_b_done")
            off_f_done = two("off_f_done")
            skip_x = two("skip_x")
            skip_done = two("skip_done")
            y_sum = two("y_sum")
            gated = two("gated")
            sq_done = two("sq_done")
            ln_done = two("ln_done")
            rstd_done = two("rstd_done")
            normed = two("normed")
            cutf_done = two("cutf_done")
            g_stored = two("g_stored")

            def chunk(i, par):
                return 2 * i + par

            def pairs(eng, body):
                body(0, True, False)
                with eng.Fori(1, PAIRS - 1) as i:
                    body(i, False, False)
                body(PAIRS - 1, False, True)

            def steps(eng, step):
                def body(i, first, last):
                    step((i, 0), (i, 1), None if last else (i + 1, 0), None if first else (i - 1, 1))
                    step((i, 1), None if last else (i + 1, 0), None if last else (i + 1, 1), (i, 0))
                pairs(eng, body)

            def flat2(x):
                return x.rearrange("p o x -> p (o x)")

            with nc.Block() as block:
                @block.sync
                def _(sp):
                    src = xcT.rearrange("(k p) t -> p k t", p=P)
                    dst = mixT.rearrange("(k p) t -> p k t", p=P)
                    K0 = D_ATT // P

                    def load_bc(i, par):
                        tok = bass.ds(chunk(i, par) * P, P)
                        sp.wait_ge(off_ready[par], i)
                        sp.dma_start(bc[:, par], src[:, KX:, tok]).then_inc(bc_loaded[par], 16)

                    def load_z(i, par):
                        tok = bass.ds(chunk(i, par) * P, P)
                        sp.wait_ge(gated[par], i)
                        sp.dma_start(z_t[:, par], z_s[tok, :]).then_inc(z_loaded[par], 16)

                    def store(i, par):
                        sp.wait_ge(t_out, chunk(i, par) + 1)
                        sp.dma_start(dst[:, K0:, bass.ds(chunk(i, par) * P, P)], gT[:, par]).then_inc(g_stored[par], 16)

                    def body(i, first, last):
                        for par in range(2):
                            if not last:
                                load_bc(i + 1, par)
                            if not (first and par == 0):
                                store(*((i, 0) if par else (i - 1, 1)))
                            if not last:
                                load_z(i + 1, par)

                    for par in range(2):
                        load_bc(0, par)
                        load_z(0, par)
                    pairs(sp, body)
                    store(PAIRS - 1, 1)
                    for par in range(2):
                        sp.wait_ge(g_stored[par], 16 * PAIRS)

                @block.vector
                def _(dve):
                    def table(i, par):
                        c = chunk(i, par)
                        dve.wait_ge(y_ready[par], i)
                        dve.wait_ge(cutf_done[par], i)
                        dve.tensor_copy(tab_c[:, par:par + 1], tab[:, bass.ds(c, 1), 0:NTAB]).then_inc(tab_done, 1)
                        dve.wait_ge(tab_done, c + 1)
                        dve.tensor_tensor(heads(xdt[:, par, 0]), heads(flat2(x_tok[:, bass.ds(c, 1)])),
                                          by_head(tab_c[:, par, DT:DT + HEADS]), ALU.mult).then_inc(xdt_f_done, 1)

                    def mix(i, par, q):
                        dve.wait_ge(e_done[q], chunk(i, par) + 1)
                        dve.wait_ge(cb_out[par], i + 1)
                        dve.tensor_tensor(decay[:, par, q], decay[:, par, q],
                                          cb[:, par, q // 2].unsqueeze(1).broadcast_to([P, GH, P]), ALU.mult) \
                           .then_inc(m_done[q], 1)

                    def across(i, par):
                        c = chunk(i, par)
                        dve.wait_ge(off_ready[par], i + 1)
                        dve.wait_ge(skip_done[par], i)
                        dve.tensor_tensor(heads(off_f[:, par]), heads(ps_off[0][:]), by_head(tab_c[:, par, E_:E_ + HEADS]),
                                          ALU.mult).then_inc(off_f_done[par], 1)
                        dve.tensor_tensor(heads(off_b[:, par]), heads(ps_off[1][:]),
                                          by_head(tab_c[:, par, E_ + HEADS:E_ + H2]), ALU.mult).then_inc(off_read, 1)
                        dve.wait_ge(cutf_done[par], i + 1)
                        dve.tensor_tensor(h_f[:, 1 - par], h_cut[:, par], flat2(s_f[:, bass.ds(c, 1)]), ALU.add) \
                           .then_inc(hf_done, 1)

                    def outputs(i, par):
                        c = chunk(i, par)
                        dve.wait_ge(off_f_done[par], i + 1)
                        dve.wait_ge(y_ready[par], i + 1)
                        dve.tensor_tensor(off_f[:, par], ps_y[par][:], off_f[:, par], ALU.add).then_inc(y_read[par], 1)
                        dve.wait_ge(y_read[par], i + 1)
                        dve.wait_ge(skip_done[par], i + 1)
                        dve.tensor_tensor(off_f[:, par], off_f[:, par], skip[:, par], ALU.add).then_inc(y_sum[par], 1)
                        dve.wait_ge(y_sum[par], i + 1)
                        dve.wait_ge(z_loaded[par], 16 * (i + 1))
                        if not isinstance(c, int) or c > 1:
                            dve.wait_ge(t_ready, c - 1)
                        dve.tensor_tensor(g_t[:, par], off_f[:, par], z_t[:, par], ALU.mult).then_inc(gated[par], 1)

                    def norm(i, par):
                        dve.wait_ge(rstd_done[par], i + 1)
                        for g in range(GROUPS):
                            c = slice(g * GW, (g + 1) * GW)
                            dve.tensor_scalar(g_t[:, par, c], g_t[:, par, c], rstd[:, par, g:g + 1], None, ALU.mult) \
                               .then_inc(normed[par], 1)

                    def out_turned(i, par):
                        dve.wait_ge(t_ready, chunk(i, par) + 1)
                        dve.wait_ge(g_stored[par], 16 * i)
                        dve.tensor_tensor(gT[:, par], ps_t[:], gain[:].unsqueeze(2).broadcast_to([P, KX, P]), ALU.mult) \
                           .then_inc(t_out, 1)

                    def step(now, after, later, before):
                        across(*now)
                        if after:
                            mix(*after, 0)
                        if before:
                            norm(*before)
                        if after:
                            mix(*after, 2)
                        outputs(*now)
                        if later:
                            table(*later)
                        if before:
                            out_turned(*before)

                    table(0, 0)
                    table(0, 1)
                    mix(0, 0, 0)
                    mix(0, 0, 2)
                    steps(dve, step)
                    norm(PAIRS - 1, 1)
                    out_turned(PAIRS - 1, 1)

                @block.gpsimd
                def _(pool):
                    def weigh_x(i, par):
                        c = chunk(i, par)
                        pool.wait_ge(tab_done, c + 1)
                        pool.wait_ge(y_ready[par], i)
                        pool.tensor_tensor(heads(xdt[:, par, 1]), heads(flat2(x_tok[:, bass.ds(c, 1)])),
                                           by_head(tab_c[:, par, DT + HEADS:DT + H2]), ALU.mult).then_inc(xdt_b_done, 1)

                    def mix(i, par, q):
                        pool.wait_ge(e_done[q], chunk(i, par) + 1)
                        pool.wait_ge(cb_out[par], i + 1)
                        pool.tensor_tensor(decay[:, par, q], decay[:, par, q],
                                           cb[:, par, q // 2].unsqueeze(1).broadcast_to([P, GH, P]), ALU.mult) \
                            .then_inc(m_done[q], 1)

                    def step(now, after, later, before):
                        i, par = now
                        c = chunk(i, par)
                        pool.wait_ge(hf_done, c)
                        pool.tensor_tensor(heads(h_cut[:, par]), heads(h_f[:, par]), by_head(tab_c[:, par, CD:CD + HEADS]),
                                           ALU.mult).then_inc(cutf_done[par], 1)
                        pool.wait_ge(const_loaded, 16 * 6)
                        pool.wait_ge(y_sum[par], i)
                        pool.tensor_tensor(heads(skip[:, par]), heads(flat2(x_tok[:, bass.ds(c, 1)])),
                                           by_head(rows[:, 2, 0:HEADS]), ALU.mult).then_inc(skip_x[par], 1)
                        if after:
                            weigh_x(*after)
                        pool.wait_ge(skip_x[par], i + 1)
                        pool.wait_ge(off_read, c + 1)
                        pool.tensor_tensor(skip[:, par], skip[:, par], off_b[:, par], ALU.add).then_inc(skip_done[par], 1)
                        if after:
                            mix(*after, 1)
                            mix(*after, 3)

                    weigh_x(0, 0)
                    mix(0, 0, 1)
                    mix(0, 0, 3)
                    steps(pool, step)

                @block.scalar
                def _(act):
                    def decays(i, par, quarters):
                        c = chunk(i, par)
                        act.wait_ge(y_ready[par], i)
                        for q in quarters:
                            if q == 0:
                                act.wait_ge(cb_ready, c + 1)
                                act.copy(cb[:, par], ps_cb[:, 0:GROUPS]).then_inc(cb_out[par], 1)
                            d, g = q % 2, q // 2
                            act.wait_ge(r_ready[q], c + 1)
                            for h in range(GH):
                                at = NB + d * HEADS + g * GH + h
                                last = act.activation(decay[:, par, q, h], ps_r[q % 2][:, h], ACT.Exp,
                                                      bias=tab_c[:, par, at:at + 1], scale=-1.0 if d else 1.0)
                            last.then_inc(e_done[q], 1)

                    def group_rstd(i, par):
                        act.wait_ge(gated[par], i + 1)
                        for g in range(GROUPS):
                            act.activation(junk[:, par, g], g_t[:, par, g * GW:(g + 1) * GW], ACT.Square,
                                           accum_out=ss[:, par, g:g + 1]).then_inc(sq_done[par], 1)
                        act.wait_ge(sq_done[par], 2 * i + 2)
                        act.activation(ss_ln[:, par], ss[:, par], ACT.Ln, scale=1.0 / GW, bias=eps[:]).then_inc(ln_done[par], 1)
                        act.wait_ge(ln_done[par], i + 1)
                        act.activation(rstd[:, par], ss_ln[:, par], ACT.Exp, scale=-0.5).then_inc(rstd_done[par], 1)

                    def step(now, after, later, before):
                        if after:
                            decays(*after, (0, 1))
                        if before:
                            group_rstd(*before)
                        if after:
                            decays(*after, (2, 3))

                    act.preload_act_table_set(LOG_EXP)
                    decays(0, 0, range(4))
                    steps(act, step)
                    group_rstd(PAIRS - 1, 1)

                @block.tensor
                def _(pe):
                    def products(i, par):
                        c = chunk(i, par)
                        pe.wait_ge(bc_loaded[par], 16 * (i + 1))
                        pe.wait_ge(cb_out[1 - par], i + par)
                        for g in range(GROUPS):
                            last = pe.matmul(ps_cb[:, g], bc[:, par, g], bc[:, par, KB + g], start=True, stop=True)
                        last.then_inc(cb_ready, 1)

                    def prefixes(i, par, q):
                        c, d, g = chunk(i, par), q % 2, q // 2
                        if q == 0:
                            pe.wait_ge(tab_done, c + 1)
                        pe.wait_ge(e_done[(q + 2) % 4], c + q // 2)
                        pe.matmul(ps_r[q % 2][:], ident_bf[:], masks[:, d].unsqueeze(1).broadcast_to([P, GH, P]),
                                  start=True, stop=False)
                        for h in range(GH):
                            at = A_ + d * HEADS + g * GH + h
                            last = pe.matmul(ps_r[q % 2][:, h], tab_c[:, par, at:at + 1].broadcast_to([P, P]), upper[:, d],
                                             start=False, stop=h == GH - 1)
                        last.then_inc(r_ready[q], 1)

                    def diagonal(i, par, g):
                        c = chunk(i, par)
                        if g == 0:
                            pe.wait_ge(xdt_f_done, c + 1)
                            pe.wait_ge(xdt_b_done, c + 1)
                            pe.wait_ge(y_read[par], i)
                        pe.wait_ge(m_done[2 * g], c + 1)
                        pe.wait_ge(m_done[2 * g + 1], c + 1)
                        for h in range(GH):
                            cols = slice((g * GH + h) * HEAD, (g * GH + h + 1) * HEAD)
                            pe.matmul(ps_y[par][:, cols], decay[:, par, 2 * g, h], xdt[:, par, 0, cols], start=True, stop=False)
                            last = pe.matmul(ps_y[par][:, cols], decay[:, par, 2 * g + 1, h], xdt[:, par, 1, cols],
                                             start=False, stop=True)
                        if g == GROUPS - 1:
                            last.then_inc(y_ready[par], 1)

                    def across(i, par):
                        c = chunk(i, par)
                        pe.wait_ge(hf_done, c)
                        pe.wait_ge(off_read, c)
                        for g in range(GROUPS):
                            cols = slice(g * GW, (g + 1) * GW)
                            pe.matmul(ps_off[0][:, cols], bc[:, par, KB + g], h_f[:, par, cols], start=True, stop=True)
                        for g in range(GROUPS):
                            cols = slice(g * GW, (g + 1) * GW)
                            last = pe.matmul(ps_off[1][:, cols], bc[:, par, KB + g],
                                             flat2(h_b[:, bass.ds(c + 1, 1), cols]), start=True, stop=True)
                        last.then_inc(off_ready[par], 1)

                    def turn(i, par):
                        c = chunk(i, par)
                        pe.wait_ge(normed[par], 2 * i + 2)
                        pe.wait_ge(t_out, c)
                        for k in range(KX):
                            last = pe.transpose(ps_t[:, k], g_t[:, par, k * P:(k + 1) * P], ident[:])
                        last.then_inc(t_ready, 1)

                    def step(now, after, later, before):
                        across(*now)
                        if after:
                            prefixes(*after, 0)
                            products(*after)
                            prefixes(*after, 1)
                        diagonal(*now, 0)
                        if after:
                            prefixes(*after, 2)
                        diagonal(*now, 1)
                        if after:
                            prefixes(*after, 3)
                        if before:
                            turn(*before)

                    products(0, 0)
                    for q in range(4):
                        prefixes(0, 0, q)
                    steps(pe, step)
                    turn(PAIRS - 1, 1)


def out_proj_phase(nc, mixT, w_out, x, norm_w, ident_dram, x1, h2T):
    PAIRS = T // P // 2
    BANKS = D_MODEL // TB

    with ExitStack() as ctx:
        def sb(name, shape, dt=F32):
            return ctx.enter_context(nc.sbuf_tensor("o_" + name, shape, dt))

        sem = ctx.enter_context(phase_semaphores(nc, "o_"))

        def two(name):
            return [sem(name + "0"), sem(name + "1")]

        ident = sb("ident", [P, P])
        gain = sb("gain", [P, KD])
        eps = sb("eps", [P, 1])
        w_raw = sb("w_raw", [P, KD, D_MODEL])
        w_hi = sb("w_hi", [P, KD, D_MODEL], F32R)
        w_lo = sb("w_lo", [P, KD, D_MODEL], F32R)
        mix = sb("mix", [P, 2, KD, P])
        mix_hi = sb("mix_hi", [P, 2, KD, P], F32R)
        mix_lo = sb("mix_lo", [P, 2, KD, P], F32R)
        x_t = sb("x_t", [P, 2, D_MODEL])
        x1_t = sb("x1_t", [P, 2, D_MODEL])
        junk = sb("junk", [P, 2, D_MODEL])
        xn = sb("xn", [P, 2, D_MODEL])
        h2 = sb("h2", [P, 2, KD, P])
        ss = sb("ss", [P, 2])
        ss_ln = sb("ss_ln", [P, 2])
        rstd = sb("rstd", [P, 2])

        acc = [ctx.enter_context(nc.psum_tensor(f"o_acc{i}", [P, BANKS, TB], F32)) for i in range(2)]
        ps_turn = [ctx.enter_context(nc.psum_tensor(f"o_ps_turn{i}", [P, KD, P], F32)) for i in range(2)]

        const_loaded = sem("const_loaded")
        eps_made = sem("eps_made")
        w_loaded = [sem(f"w_loaded{k}") for k in range(KD)]
        w_hi_done = sem("w_hi_done")
        w_lo_done = sem("w_lo_done")
        mix_loaded = two("mix_loaded")
        x_loaded = two("x_loaded")
        mix_hi_done = two("mix_hi_done")
        mix_lo_done = two("mix_lo_done")
        acc_ready = two("acc_ready")
        x1_made = two("x1_made")
        x1_stored = two("x1_stored")
        sq_done = two("sq_done")
        ln_done = two("ln_done")
        rstd_done = two("rstd_done")
        xn_done = two("xn_done")
        turned = two("turned")
        h2_made = two("h2_made")
        h2_stored = two("h2_stored")

        def steps(eng, step):
            def body(i, first, last):
                step((i, 0), (i, 1), None if first else (i - 1, 1))
                step((i, 1), None if last else (i + 1, 0), (i, 0))
            body(0, True, False)
            with eng.Fori(1, PAIRS - 1) as i:
                body(i, False, False)
            body(PAIRS - 1, False, True)

        def tokens(i, par):
            return bass.ds((2 * i + par) * P, P)

        block = ctx.enter_context(nc.Block())

        @block.sync
        def _(sp):
            w_src = w_out.rearrange("(k p) d -> p k d", p=P)
            mix_src = mixT.rearrange("(k p) t -> p k t", p=P)

            def load(i, par):
                sp.wait_ge(mix_lo_done[par], i)
                sp.dma_start(mix[:, par], mix_src[:, :, tokens(i, par)]).then_inc(mix_loaded[par], 16)
                sp.wait_ge(x1_made[par], BANKS * i)
                sp.dma_start(x_t[:, par], x[tokens(i, par), :]).then_inc(x_loaded[par], 16)

            load(0, 0)
            for k in range(KD):
                sp.dma_start(w_raw[:, k], w_src[:, k]).then_inc(w_loaded[k], 16)
                if k == 1:
                    sp.dma_start(ident[:], ident_dram).then_inc(const_loaded, 16)
                    sp.dma_start(gain[:], norm_w).then_inc(const_loaded, 16)
            load(0, 1)
            with sp.Fori(1, PAIRS) as i:
                load(i, 0)
                load(i, 1)

        @block.scalar
        def _(act):
            def split(i, par):
                act.wait_ge(mix_loaded[par], 16 * (i + 1))
                act.wait_ge(acc_ready[par], i)
                act.copy(mix_hi[:, par], mix[:, par]).then_inc(mix_hi_done[par], 1)

            def make_rstd(i, par):
                act.wait_ge(x1_made[par], BANKS * (i + 1))
                act.wait_ge(ln_done[par], i)
                act.activation(junk[:, par], x1_t[:, par], ACT.Square, accum_out=ss[:, par:par + 1]) \
                   .then_inc(sq_done[par], 1)
                act.wait_ge(sq_done[par], i + 1)
                act.activation(ss_ln[:, par:par + 1], ss[:, par:par + 1], ACT.Ln, scale=1.0 / D_MODEL, bias=eps[:]) \
                   .then_inc(ln_done[par], 1)
                act.wait_ge(ln_done[par], i + 1)
                act.wait_ge(xn_done[par], i)
                act.activation(rstd[:, par:par + 1], ss_ln[:, par:par + 1], ACT.Exp, scale=-0.5) \
                   .then_inc(rstd_done[par], 1)

            def step(now, after, before):
                if after:
                    split(*after)
                make_rstd(*now)

            act.preload_act_table_set(LOG_EXP)
            act.wait_ge(eps_made, 1)
            split(0, 0)
            for k in range(KD):
                act.wait_ge(w_loaded[k], 16)
                act.copy(w_hi[:, k], w_raw[:, k]).then_inc(w_hi_done, 1)
            steps(act, step)

        @block.vector
        def _(dve):
            def split(i, par):
                dve.wait_ge(mix_hi_done[par], i + 1)
                dve.tensor_tensor(mix_lo[:, par], mix[:, par], mix_hi[:, par].bitcast(F32), ALU.subtract) \
                   .then_inc(mix_lo_done[par], 1)

            def add_x(i, par):
                dve.wait_ge(acc_ready[par], i + 1)
                dve.wait_ge(x_loaded[par], 16 * (i + 1))
                dve.wait_ge(x1_stored[par], 16 * i)
                for b in range(BANKS):
                    c = slice(b * TB, (b + 1) * TB)
                    dve.tensor_tensor(x1_t[:, par, c], acc[par][:, b], x_t[:, par, c], ALU.add).then_inc(x1_made[par], 1)

            def scale(i, par):
                dve.wait_ge(rstd_done[par], i + 1)
                dve.wait_ge(turned[par], i)
                dve.tensor_scalar(xn[:, par], x1_t[:, par], rstd[:, par:par + 1], None, ALU.mult) \
                   .then_inc(xn_done[par], 1)

            def out_turned(i, par):
                dve.wait_ge(turned[par], i + 1)
                dve.wait_ge(h2_stored[par], 16 * i)
                dve.tensor_tensor(h2[:, par], ps_turn[par][:], gain[:].unsqueeze(2).broadcast_to([P, KD, P]), ALU.mult) \
                   .then_inc(h2_made[par], 1)

            def step(now, after, before):
                if after:
                    split(*after)
                add_x(*now)
                if before:
                    out_turned(*before)
                scale(*now)

            dve.memset(eps[:], EPS).then_inc(eps_made, 1)
            split(0, 0)
            for k in range(KD):
                dve.wait_ge(w_hi_done, k + 1)
                dve.tensor_tensor(w_lo[:, k], w_raw[:, k], w_hi[:, k].bitcast(F32), ALU.subtract).then_inc(w_lo_done, 1)
            dve.wait_ge(const_loaded, 32)
            steps(dve, step)
            out_turned(PAIRS - 1, 1)

        @block.gpsimd
        def _(pool):
            h2_dst = h2T.rearrange("(k p) t -> p k t", p=P)

            def store_x1(i, par):
                pool.wait_ge(x1_made[par], BANKS * (i + 1))
                pool.dma_start(x1[tokens(i, par), :], x1_t[:, par]).then_inc(x1_stored[par], 16)

            def store_h2(i, par):
                pool.wait_ge(h2_made[par], i + 1)
                pool.dma_start(h2_dst[:, :, tokens(i, par)], h2[:, par]).then_inc(h2_stored[par], 16)

            def step(now, after, before):
                store_x1(*now)
                if before:
                    store_h2(*before)

            steps(pool, step)
            store_h2(PAIRS - 1, 1)
            for par in range(2):
                pool.wait_ge(x1_stored[par], 16 * PAIRS)
                pool.wait_ge(h2_stored[par], 16 * PAIRS)

        @block.tensor
        def _(pe):
            def products(i, par):
                pe.wait_ge(mix_lo_done[par], i + 1)
                pe.wait_ge(x1_made[par], BANKS * i)
                for k in range(KD):
                    if isinstance(i, int) and i == par == 0:
                        pe.wait_ge(w_lo_done, k + 1)
                    for b in range(BANKS):
                        c = slice(b * TB, (b + 1) * TB)
                        last = split_products(pe, acc[par][:, b], mix_hi[:, par, k], mix_lo[:, par, k],
                                              w_hi[:, k, c], w_lo[:, k, c], k == 0, k == KD - 1)
                last.then_inc(acc_ready[par], 1)

            def turn(i, par):
                pe.wait_ge(xn_done[par], i + 1)
                pe.wait_ge(h2_made[par], i)
                for k in range(KD):
                    last = pe.transpose(ps_turn[par][:, k], xn[:, par, k * P:(k + 1) * P], ident[:])
                last.then_inc(turned[par], 1)

            def step(now, after, before):
                products(*now)
                if before:
                    turn(*before)

            pe.wait_ge(const_loaded, 32)
            steps(pe, step)
            turn(PAIRS - 1, 1)


def ffn_phase(nc, h2T, x1, w_gate, w_up, w_down, ident_dram, y):
    HALF = KF // 2
    SLOT = 2 * KD
    PAIRS = KF // 2
    SLOTS2 = (KF + 2 * KD) // 2
    H_PARTS = 4

    with ExitStack() as ctx:
        def sb(name, shape, dt=F32):
            return ctx.enter_context(nc.sbuf_tensor("f_" + name, shape, dt))

        sem = ctx.enter_context(phase_semaphores(nc, "f_"))

        def two(name):
            return [sem(name + "0"), sem(name + "1")]

        ident = sb("ident", [P, P])
        raw = sb("raw", [P, 2, SLOT, P])
        w_hi = sb("w_hi", [P, 2, SLOT, P], F32R)
        w_lo = sb("w_lo", [P, 2, SLOT, P], F32R)
        h_raw = sb("h_raw", [P, KD, TB])
        h_hi = sb("h_hi", [P, KD, TB], F32R)
        h_lo = sb("h_lo", [P, KD, TB], F32R)
        g_silu = sb("g_silu", [P, 2, TB])
        hid = sb("hid", [P, 2, TB])
        hid_hi = sb("hid_hi", [P, KF, TB], F32R)
        hid_lo = sb("hid_lo", [P, KF, TB], F32R)
        yT = sb("yT", [P, 2, TB])
        x1_t = sb("x1_t", [P, 2, TT, P])
        y_t = sb("y_t", [P, 2, TT, P])

        ps_gate = ctx.enter_context(nc.psum_tensor("f_ps_gate", [P, 2, TB], F32))
        ps_up = ctx.enter_context(nc.psum_tensor("f_ps_up", [P, 2, TB], F32))
        ps_down = ctx.enter_context(nc.psum_tensor("f_ps_down", [P, 2, TB], F32))
        ps_turn = ctx.enter_context(nc.psum_tensor("f_ps_turn", [P, TT, P], F32))

        id_loaded = sem("id_loaded")
        h_loaded = [sem(f"h_loaded{i}") for i in range(H_PARTS)]
        h_hi_done = sem("h_hi_done")
        h_lo_done = sem("h_lo_done")
        slot_loaded = two("slot_loaded")
        slot_hi_done = two("slot_hi_done")
        slot_lo_done = two("slot_lo_done")
        slot_done = two("slot_done")
        gate_ready = two("gate_ready")
        silu_done = two("silu_done")
        prod_done = two("prod_done")
        hid_hi_done = two("hid_hi_done")
        hid_lo_done = two("hid_lo_done")
        yT_done = two("yT_done")
        turned = two("turned")
        x1_loaded = two("x1_loaded")
        y_added = two("y_added")
        y_stored = two("y_stored")

        def blocks(eng, body):
            with eng.Fori(0, NTB - 1) as tb:
                body(tb, True)
            body(NTB - 1, False)

        def down_slots(tb, d):
            return tb * SLOTS2 + PAIRS + d + 1

        block = ctx.enter_context(nc.Block())

        @block.sync
        def _(sp):
            h_src = h2T.rearrange("(k p) t -> p k t", p=P)
            wg_src = w_gate.rearrange("(k p) f -> p k f", p=P)
            wu_src = w_up.rearrange("(k p) f -> p k f", p=P)
            wd_src = w_down.rearrange("(f p) d -> p f d", p=P)
            x1_src = x1.rearrange("(t p) d -> p t d", p=P)
            y_dst = y.rearrange("(t p) d -> p t d", p=P)

            def load_h(tb):
                sp.wait_ge(h_lo_done, KD * tb)
                for i in range(H_PARTS):
                    k = slice(i * KD // H_PARTS, (i + 1) * KD // H_PARTS)
                    sp.dma_start(h_raw[:, k], h_src[:, k, bass.ds(tb * TB, TB)]).then_inc(h_loaded[i], 16)

            def load_pair(tb, i):
                for par in range(2):
                    sp.wait_ge(slot_lo_done[par], tb * SLOTS2 + i)
                    cols = bass.ds((2 * i + par) * P, P)
                    sp.dma_start(raw[:, par, 0:KD], wg_src[:, :, cols]).then_inc(slot_loaded[par], 16)
                    sp.dma_start(raw[:, par, KD:SLOT], wu_src[:, :, cols]).then_inc(slot_loaded[par], 16)

            def load_down(tb, d, par, q):
                for half in range(2):
                    sp.wait_ge(slot_lo_done[half], tb * SLOTS2 + PAIRS + d)
                    for a, b in ((0, HALF // 2), (HALF // 2, HALF)):
                        sp.dma_start(raw[:, half, a:b],
                                     wd_src[:, HALF * half + a:HALF * half + b, bass.ds(d * P, P)]) \
                          .then_inc(slot_loaded[half], 16)
                sp.wait_ge(y_added[par], q)
                sp.dma_start(x1_t[:, par], x1_src[:, bass.ds(tb * TT, TT), bass.ds(d * P, P)]) \
                  .then_inc(x1_loaded[par], 16)

            def store_y(tb, d, par, q):
                sp.wait_ge(y_added[par], q + 1)
                sp.dma_start(y_dst[:, bass.ds(tb * TT, TT), bass.ds(d * P, P)], y_t[:, par]) \
                  .then_inc(y_stored[par], 16)

            def token_block(tb, more):
                with sp.Fori(1, PAIRS) as i:
                    load_pair(tb, i)
                if more:
                    load_h(tb + 1)
                q = tb * (KD // 2)
                load_down(tb, 0, 0, q)
                load_down(tb, 1, 1, q)
                with sp.Fori(0, KD // 2 - 1) as i:
                    for par in range(2):
                        load_down(tb, 2 * i + 2 + par, par, q + i + 1)
                        store_y(tb, 2 * i + par, par, q + i)
                if more:
                    load_pair(tb + 1, 0)
                store_y(tb, KD - 2, 0, q + KD // 2 - 1)
                store_y(tb, KD - 1, 1, q + KD // 2 - 1)

            load_h(0)
            load_pair(0, 0)
            sp.dma_start(ident[:], ident_dram).then_inc(id_loaded, 16)
            blocks(sp, token_block)
            for par in range(2):
                sp.wait_ge(y_stored[par], 16 * NTB * KD // 2)

        @block.scalar
        def _(act):
            def split_slot(n, par, size):
                act.wait_ge(slot_loaded[par], 32 * (n + 1))
                act.wait_ge(slot_done[par], n)
                act.copy(w_hi[:, par, 0:size], raw[:, par, 0:size]).then_inc(slot_hi_done[par], 1)

            def split_h(tb, k, behind):
                for i in range(H_PARTS):
                    if not isinstance(k, int) or k * H_PARTS // KD == i:
                        act.wait_ge(h_loaded[i], 16 * (tb + 1))
                act.wait_ge(slot_done[1], behind)
                act.copy(h_hi[:, k], h_raw[:, k]).then_inc(h_hi_done, 1)

            def silu(tb, i, par):
                g = tb * PAIRS + i
                act.wait_ge(gate_ready[par], g + 1)
                act.wait_ge(prod_done[par], g)
                act.activation(g_silu[:, par], ps_gate[:, par], ACT.Silu).then_inc(silu_done[par], 1)

            def out_tile(tb, d, par, q, more):
                if more:
                    split_h(tb + 1, d, tb * SLOTS2 + PAIRS)
                act.wait_ge(slot_done[1], down_slots(tb, d))
                act.wait_ge(turned[par], q)
                act.copy(yT[:, par], ps_down[:, par]).then_inc(yT_done[par], 1)

            def token_block(tb, more):
                n = tb * SLOTS2
                with act.Fori(0, PAIRS - 1) as i:
                    split_slot(n + i, 1, SLOT)
                    silu(tb, i, 0)
                    split_slot(n + i + 1, 0, SLOT)
                    silu(tb, i, 1)
                split_slot(n + PAIRS - 1, 1, SLOT)
                silu(tb, PAIRS - 1, 0)
                n = tb * SLOTS2 + PAIRS
                split_slot(n, 0, HALF)
                silu(tb, PAIRS - 1, 1)
                split_slot(n, 1, HALF)
                q = tb * (KD // 2)
                with act.Fori(0, KD // 2 - 1) as i:
                    for par in range(2):
                        split_slot(n + 2 * i + par + 1, 0, HALF)
                        out_tile(tb, 2 * i + par, par, q + i, more)
                        split_slot(n + 2 * i + par + 1, 1, HALF)
                split_slot(n + KD - 1, 0, HALF)
                out_tile(tb, KD - 2, 0, q + KD // 2 - 1, more)
                split_slot(n + KD - 1, 1, HALF)
                if more:
                    split_slot(n + KD, 0, SLOT)
                out_tile(tb, KD - 1, 1, q + KD // 2 - 1, more)

            act.preload_act_table(ACT.Silu)
            for k in range(KD):
                split_h(0, k, 0)
            split_slot(0, 0, SLOT)
            blocks(act, token_block)

        @block.vector
        def _(dve):
            def split_slot(n, par, size):
                dve.wait_ge(slot_hi_done[par], n + 1)
                dve.tensor_tensor(w_lo[:, par, 0:size], raw[:, par, 0:size], w_hi[:, par, 0:size].bitcast(F32),
                                  ALU.subtract).then_inc(slot_lo_done[par], 1)

            def split_h(tb, k):
                dve.wait_ge(h_hi_done, KD * tb + k + 1)
                dve.tensor_tensor(h_lo[:, k], h_raw[:, k], h_hi[:, k].bitcast(F32), ALU.subtract) \
                   .then_inc(h_lo_done, 1)

            def product(tb, i, par):
                g = tb * PAIRS + i
                dve.wait_ge(silu_done[par], g + 1)
                dve.wait_ge(slot_done[par], tb * SLOTS2 + i + 1)
                dve.wait_ge(hid_lo_done[par], g)
                dve.tensor_tensor(hid[:, par], g_silu[:, par], ps_up[:, par], ALU.mult) \
                   .then_inc(prod_done[par], 1)

            def out_tile(tb, d, par, q, more):
                if more:
                    split_h(tb + 1, d)
                dve.wait_ge(turned[par], q + 1)
                dve.wait_ge(x1_loaded[par], 16 * (q + 1))
                dve.wait_ge(y_stored[par], 16 * q)
                dve.tensor_tensor(y_t[:, par], ps_turn[:], x1_t[:, par], ALU.add).then_inc(y_added[par], 1)

            def token_block(tb, more):
                n = tb * SLOTS2
                with dve.Fori(0, PAIRS - 1) as i:
                    split_slot(n + i, 1, SLOT)
                    product(tb, i, 0)
                    split_slot(n + i + 1, 0, SLOT)
                    product(tb, i, 1)
                split_slot(n + PAIRS - 1, 1, SLOT)
                product(tb, PAIRS - 1, 0)
                n = tb * SLOTS2 + PAIRS
                split_slot(n, 0, HALF)
                product(tb, PAIRS - 1, 1)
                split_slot(n, 1, HALF)
                q = tb * (KD // 2)
                split_slot(n + 1, 0, HALF)
                with dve.Fori(0, KD // 2 - 1) as i:
                    split_slot(n + 2 * i + 1, 1, HALF)
                    split_slot(n + 2 * i + 2, 0, HALF)
                    out_tile(tb, 2 * i, 0, q + i, more)
                    split_slot(n + 2 * i + 2, 1, HALF)
                    split_slot(n + 2 * i + 3, 0, HALF)
                    out_tile(tb, 2 * i + 1, 1, q + i, more)
                split_slot(n + KD - 1, 1, HALF)
                out_tile(tb, KD - 2, 0, q + KD // 2 - 1, more)
                if more:
                    split_slot(n + KD, 0, SLOT)
                out_tile(tb, KD - 1, 1, q + KD // 2 - 1, more)

            for k in range(KD):
                split_h(0, k)
            split_slot(0, 0, SLOT)
            blocks(dve, token_block)

        @block.gpsimd
        def _(pool):
            with pool.Fori(0, NTB) as tb:
                with pool.Fori(0, PAIRS) as i:
                    for par in range(2):
                        g = tb * PAIRS + i
                        f = bass.ds(2 * i + par, 1)
                        pool.wait_ge(slot_done[1], tb * SLOTS2)
                        pool.wait_ge(prod_done[par], g + 1)
                        pool.tensor_copy(hid_hi[:, f], hid[:, par:par + 1]).then_inc(hid_hi_done[par], 1)
                        pool.wait_ge(hid_hi_done[par], g + 1)
                        pool.tensor_tensor(hid_lo[:, f], hid[:, par:par + 1], hid_hi[:, f].bitcast(F32),
                                           ALU.subtract).then_inc(hid_lo_done[par], 1)

        @block.tensor
        def _(pe):
            def down_half(tb, d, par, q, half):
                pe.wait_ge(slot_lo_done[half], down_slots(tb, d))
                if half == 0:
                    pe.wait_ge(yT_done[par], q)
                for j in range(HALF):
                    f = HALF * half + j
                    last = split_products(pe, ps_down[:, par], w_hi[:, half, j], w_lo[:, half, j],
                                          hid_hi[:, f], hid_lo[:, f], f == 0, f == KF - 1)
                last.then_inc(slot_done[half], 1)

            def turn(par, q, behind):
                pe.wait_ge(yT_done[par], q + 1)
                pe.wait_ge(y_added[1 - par], behind)
                for t in range(TT):
                    last = pe.transpose(ps_turn[:, t], yT[:, par, t * P:(t + 1) * P], ident[:])
                last.then_inc(turned[par], 1)

            def token_block(tb, more):
                pe.wait_ge(id_loaded, 16)
                with pe.Fori(0, PAIRS) as i:
                    for par in range(2):
                        pe.wait_ge(h_lo_done, KD * (tb + 1))
                        pe.wait_ge(slot_lo_done[par], tb * SLOTS2 + i + 1)
                        pe.wait_ge(prod_done[par], tb * PAIRS + i)
                        for k in range(KD):
                            last = split_products(pe, ps_gate[:, par], w_hi[:, par, k], w_lo[:, par, k],
                                                  h_hi[:, k], h_lo[:, k], k == 0, k == KD - 1)
                        last.then_inc(gate_ready[par], 1)
                        for k in range(KD):
                            last = split_products(pe, ps_up[:, par], w_hi[:, par, KD + k], w_lo[:, par, KD + k],
                                                  h_hi[:, k], h_lo[:, k], k == 0, k == KD - 1)
                        last.then_inc(slot_done[par], 1)
                q = tb * (KD // 2)
                for half in range(2):
                    for par in range(2):
                        pe.wait_ge(hid_lo_done[par], PAIRS * tb + (PAIRS if half else (HALF + 1) // 2))
                    down_half(tb, 0, 0, q, half)
                with pe.Fori(0, KD // 2 - 1) as i:
                    down_half(tb, 2 * i + 1, 1, q + i, 0)
                    turn(0, q + i, q + i)
                    down_half(tb, 2 * i + 1, 1, q + i, 1)
                    down_half(tb, 2 * i + 2, 0, q + i + 1, 0)
                    turn(1, q + i, q + i + 1)
                    down_half(tb, 2 * i + 2, 0, q + i + 1, 1)
                end = q + KD // 2 - 1
                down_half(tb, KD - 1, 1, end, 0)
                turn(0, end, end)
                down_half(tb, KD - 1, 1, end, 1)
                turn(1, end, end + 1)

            blocks(pe, token_block)


def build(nc, x, w_in, rpb, w_out, w_gate, w_up, w_down, cols, qk_rows, head_rows, ssm_gain, norm2, ident, ident_bf,
          tri, tri_masks, masks, y):
    def scratch(name, shape):
        return nc.dram_tensor(name, shape, F32, kind="Internal").ap()

    q_s, k_s, v_s, z_s = (scratch(n, (T, D_ATT)) for n in ("q_s", "k_s", "v_s", "z_s"))
    dtT = scratch("dtT", (2 * HEADS, T))
    xbcT = scratch("xbcT", (CONV_CH, T + 4 * (D_CONV // 2)))
    xcT = scratch("xcT", (CONV_CH, T))
    mixT = scratch("mixT", (D_ATT + D_SSM, T))
    copies = scratch("bias_copies", (16 * PITCH,))
    x1 = scratch("x1", (T, D_MODEL))
    h2T = scratch("h2T", (D_MODEL, T))
    in_proj_phase(nc, x, w_in, cols, qk_rows, rpb, copies, ident, q_s, k_s, v_s, z_s, dtT, xbcT, xcT)
    attention_phase(nc, q_s, k_s, v_s, copies, masks, ident, mixT)
    ssd_phase(nc, xcT, dtT, z_s, head_rows, ssm_gain, tri, tri_masks, ident, ident_bf, mixT)
    out_proj_phase(nc, mixT, w_out, x, norm2, ident, x1, h2T)
    ffn_phase(nc, h2T, x1, w_gate, w_up, w_down, ident, y)


def by_partition(np, a, n):
    return np.moveaxis(a.reshape(a.shape[:-1] + (n, P)), (-1, -2), (0, 1))


def triangles(np):
    r = np.arange(P)
    ones = np.stack([r[:, None] <= r, r[:, None] < r, np.ones((P, P), bool)], axis=1).astype(np.float32)
    below = np.where(r[:, None] > r, -2.0 ** 100, 0.0)
    above = np.where(r[:, None] < r, 2.0 ** 100, 0.0)
    return ones, np.stack([below, above], axis=1).astype(mybir.dt.np(BF16))


def neighbourhoods(np):
    token = np.arange(T)
    row, col = token // GRID_W, token % GRID_W
    rows = SEQ // GRID_W
    first_row = np.where(row < rows, np.clip(row - WIN_ROWS // 2, 0, rows - WIN_ROWS), rows)
    first_col = np.clip(col - WIN_COLS // 2, 0, GRID_W - WIN_COLS)
    m = np.zeros((48, 2, T), np.float32)
    for r in range(32):
        m[r, 0] = np.where((r - first_col) % 32 < WIN_COLS, 0.0, -2.0 ** 100)
        m[r, 1] = col % 32 == r
    for r in range(16):
        m[32 + r, 0] = np.where((r - first_row) % 16 < WIN_ROWS, 0.0, -2.0 ** 100)
        m[32 + r, 1] = row % 16 == r
    m[:, 0] = m[:, 0].reshape(48, T // TB, 8, 4, 16).transpose(0, 1, 3, 2, 4).reshape(48, T)
    return m


def kernel(**inputs):
    import numpy as np
    import concourse.bacc as bacc
    from concourse.bass_utils import run_bass_kernel_spmd

    a = {name: np.asarray(value) for name, value in inputs.items()}
    weights = {name: value[0] for name, value in a.items() if not name.startswith("x_")}
    x = np.concatenate([a["x_prompt"][0], a["x_sample"][0]])

    cols = np.zeros((P, KD, 8), np.float32)
    cols[:, :, 0] = by_partition(np, weights["norm1_w"], KD)
    cols[:, :, 1] = by_partition(np, weights["conv_b"], KD)
    cols[:, :, 2:2 + D_CONV] = by_partition(np, weights["conv_w"], KD)
    qk = np.stack([weights["q_norm_w"], weights["k_norm_w"]])
    heads = np.stack([np.concatenate([weights["dt_bias_f"], weights["dt_bias_b"]]),
                      np.concatenate([weights["A_log_f"], weights["A_log_b"]]),
                      np.concatenate([weights["D_skip"], weights["D_skip"]])])
    ones, tri_masks = triangles(np)
    arrays = dict(
        x=x, w_in=weights["w_in"],
        rpb=np.pad(weights["rpb"], ((0, 0), (4, 4), (16, 16))).reshape(-1),
        w_out=weights["w_out"], w_gate=weights["w_gate"], w_up=weights["w_up"], w_down=weights["w_down"],
        cols=cols, qk_rows=np.broadcast_to(qk, (P,) + qk.shape), head_rows=np.broadcast_to(heads, (P,) + heads.shape),
        ssm_gain=by_partition(np, weights["ssm_norm_w"], D_SSM // P), norm2=by_partition(np, weights["norm2_w"], KD),
        ident=np.eye(P, dtype=np.float32), ident_bf=np.eye(P).astype(mybir.dt.np(BF16)),
        tri=ones, tri_masks=tri_masks, masks=neighbourhoods(np))
    arrays = {name + "_dram": np.ascontiguousarray(value) for name, value in arrays.items()}

    nc = bacc.Bacc("TRN2", target_bir_lowering=False, num_devices=1)
    args = [nc.dram_tensor(name, value.shape, mybir.dt.from_np(value.dtype), kind="ExternalInput").ap()
            for name, value in arrays.items()]
    y = nc.dram_tensor("y_dram", (T, D_MODEL), F32, kind="ExternalOutput").ap()
    build(nc, *args, y)
    result = run_bass_kernel_spmd(nc, [arrays], core_ids=[0]).results[0]["y_dram"]
    return result[None, :SEQ], result[None, SEQ:]
```
